# Optimizing a Trainium2 kernel written in Bass

```python
import jax, jax.numpy as jnp
from jax import lax
import numpy as np

D_MODEL = 2048
BATCH = 1
SEQ = 256
DEPTH = 2

N_META = 16
GRID_W = 64
EPS = 1e-6
NA_HEADS = 8
NA_DIM = 128
NA_WIDTH = NA_HEADS * NA_DIM
WIN_H = 8
WIN_W = 16
NA_QB = 16
NA_KSPAN = NA_QB + WIN_W
ML_HEADS = 4
ML_QK = 128
ML_V = 256
ML_QK_WIDTH = ML_HEADS * ML_QK
ML_WIDTH = ML_HEADS * ML_V
ML_CHUNK = 64
MIX_WIDTH = NA_WIDTH + ML_WIDTH
EVEN_SIZES = (NA_WIDTH, NA_WIDTH, NA_WIDTH, ML_QK_WIDTH, ML_QK_WIDTH, ML_WIDTH, ML_WIDTH, 4 * ML_HEADS)
EVEN_IN = 3 * NA_WIDTH + 2 * ML_QK_WIDTH + 2 * ML_WIDTH + 4 * ML_HEADS
GLA_HEADS = 4
GLA_DK = 256
GLA_DV = 512
GLA_KW = GLA_HEADS * GLA_DK
GLA_VW = GLA_HEADS * GLA_DV
GLA_RANK = 16
GLA_TAU = 16.0
GLA_CHUNK = 64
ODD_SIZES = (GLA_KW, GLA_KW, GLA_VW, GLA_VW, GLA_RANK, GLA_RANK)
ODD_IN = 2 * GLA_KW + 2 * GLA_VW + 2 * GLA_RANK
D_FF = 5632
CONV_W = 3
N_EVEN = (DEPTH + 1) // 2
N_ODD = DEPTH // 2

kernel_name = 'hybrid_natten_mlstm_gla_encoder'

def _rms(x, gain):
    xf = x.astype(jnp.float32)
    y = xf * lax.rsqrt(jnp.mean(xf * xf, axis=-1, keepdims=True) + EPS)
    return (y * gain.astype(jnp.float32)).astype(x.dtype)

def _head_rms(y, n_heads, gain):
    b, t, w = y.shape
    yh = y.reshape(b, t, n_heads, w // n_heads)
    return _rms(yh, gain.reshape(n_heads, w // n_heads)).reshape(b, t, w)

def _split(a, sizes):
    return jnp.split(a, np.cumsum(sizes)[:-1].tolist(), axis=-1)

def _na_columns():
    j = np.arange(GRID_W // NA_QB)
    starts = np.clip(j * NA_QB - WIN_W // 2, 0, GRID_W - NA_KSPAN)
    col_idx = starts[:, None] + np.arange(NA_KSPAN)
    q_col = j[:, None] * NA_QB + np.arange(NA_QB)
    c0 = np.clip(q_col - WIN_W // 2, 0, GRID_W - WIN_W)[..., None]
    kc = col_idx[:, None, :]
    mask = (kc >= c0) & (kc < c0 + WIN_W)
    dc_idx = np.clip(kc - q_col[..., None] + WIN_W - 1, 0, 2 * WIN_W - 2)
    return col_idx, mask, dc_idx

def _neighbourhood_attention(q, k, v, rel_bias):
    b, t, h, d = q.shape
    n_real = t - N_META
    rows = n_real // GRID_W
    win_h = min(WIN_H, rows)
    n_cb = GRID_W // NA_QB
    scale = d ** -0.5
    qm, km, vm = q[:, :N_META], k[:, :N_META], v[:, :N_META]
    qg = q[:, N_META:].reshape(b, rows, GRID_W, h, d)
    kg = k[:, N_META:].reshape(b, rows, GRID_W, h, d)
    vg = v[:, N_META:].reshape(b, rows, GRID_W, h, d)
    s_mm = jnp.einsum('bqhd,bkhd->bhqk', qm, km) * scale
    y_meta = jnp.einsum('bhqk,bkhd->bqhd', jax.nn.softmax(s_mm, axis=-1), vm)
    col_idx, col_mask, dc_idx = _na_columns()
    n_loc = win_h * NA_KSPAN

    def one_row(r):
        r0 = jnp.clip(r - WIN_H // 2, 0, rows - win_h)
        kr = lax.dynamic_slice_in_dim(kg, r0, win_h, axis=1)
        vr = lax.dynamic_slice_in_dim(vg, r0, win_h, axis=1)
        kb = kr[:, :, col_idx]
        vb = vr[:, :, col_idx]
        qb = lax.dynamic_index_in_dim(qg, r, axis=1, keepdims=False).reshape(b, n_cb, NA_QB, h, d)
        s_loc = jnp.einsum('bjqhd,brjkhd->bhjqrk', qb, kb) * scale
        dr_idx = r0 - r + jnp.arange(win_h) + WIN_H - 1
        bias = jnp.transpose(rel_bias[:, dr_idx][:, :, dc_idx], (0, 2, 3, 1, 4))
        s_loc = jnp.where(col_mask[:, :, None, :], s_loc + bias, -jnp.inf).reshape(b, h, n_cb, NA_QB, n_loc)
        s_met = jnp.einsum('bjqhd,bmhd->bhjqm', qb, km) * scale
        p = jax.nn.softmax(jnp.concatenate([s_loc, s_met], axis=-1), axis=-1)
        p_loc = p[..., :n_loc].reshape(b, h, n_cb, NA_QB, win_h, NA_KSPAN)
        y = (jnp.einsum('bhjqrk,brjkhd->bjqhd', p_loc, vb)
             + jnp.einsum('bhjqm,bmhd->bjqhd', p[..., n_loc:], vm))
        return y.reshape(b, GRID_W, h, d)

    y_real = lax.map(one_row, jnp.arange(rows))
    y_real = jnp.moveaxis(y_real, 0, 1).reshape(b, n_real, h, d)
    return jnp.concatenate([y_meta, y_real], axis=1)

def _scan_chunks(step, state, xs, chunk):
    def split(a):
        bb, hh, tt = a.shape[:3]
        return jnp.moveaxis(a.reshape(bb, hh, tt // chunk, chunk, *a.shape[3:]), 2, 0)
    state, ys = lax.scan(step, state, tuple(split(a) for a in xs))
    n, bb, hh, c, e = ys.shape
    return state, jnp.moveaxis(ys, 0, 2).reshape(bb, hh, n * c, e)

def _bidirectional(step, init, xs_fwd, xs_bwd, chunk):
    meta = lambda xs: tuple(a[:, :, :N_META] for a in xs)
    real = lambda xs: tuple(a[:, :, N_META:] for a in xs)
    flip = lambda xs: tuple(jnp.flip(a, axis=2) for a in xs)
    s, y_meta_f = _scan_chunks(step, init, meta(xs_fwd), N_META)
    _, y_real_f = _scan_chunks(step, s, real(xs_fwd), chunk)
    s, y_real_b = _scan_chunks(step, init, flip(real(xs_bwd)), chunk)
    _, y_meta_b = _scan_chunks(step, s, flip(meta(xs_bwd)), N_META)
    y_f = jnp.concatenate([y_meta_f, y_real_f], axis=2)
    y_b = jnp.flip(jnp.concatenate([y_real_b, y_meta_b], axis=2), axis=2)
    return y_f + y_b

def _mlstm_chunk(state, inp):
    c_mat, n_vec, m = state
    q, k, v, ig, log_f = inp
    c = q.shape[2]
    tri = jnp.tril(jnp.ones((c, c), dtype=bool))
    bcum = jnp.cumsum(log_f, axis=-1)
    d_log = jnp.where(tri, bcum[..., :, None] - bcum[..., None, :] + ig[..., None, :], -jnp.inf)
    m_prev = bcum + m[..., None]
    m_t = jnp.maximum(m_prev, jnp.max(d_log, axis=-1))
    w_prev = jnp.exp(m_prev - m_t)
    p = jnp.exp(d_log - m_t[..., None]) * jnp.einsum('bhtd,bhsd->bhts', q, k)
    num = w_prev[..., None] * jnp.einsum('bhtd,bhde->bhte', q, c_mat) + jnp.einsum('bhts,bhse->bhte', p, v)
    den = w_prev * jnp.einsum('bhtd,bhd->bht', q, n_vec) + jnp.sum(p, axis=-1)
    h = num / jnp.maximum(jnp.abs(den), jnp.exp(-m_t))[..., None]
    g = bcum[..., -1:] - bcum + ig
    m_new = jnp.maximum(bcum[..., -1] + m, jnp.max(g, axis=-1))
    w_state = jnp.exp(bcum[..., -1] + m - m_new)
    w_tok = jnp.exp(g - m_new[..., None])
    c_new = w_state[..., None, None] * c_mat + jnp.einsum('bhs,bhsd,bhse->bhde', w_tok, k, v)
    n_new = w_state[..., None] * n_vec + jnp.einsum('bhs,bhsd->bhd', w_tok, k)
    return (c_new, n_new, m_new), h

def _gla_chunk(s_mat, inp):
    q, k, v, log_a = inp
    c = q.shape[2]
    tri = jnp.tril(jnp.ones((c, c), dtype=bool))
    bcum = jnp.cumsum(log_a, axis=2)
    decay = jnp.exp(jnp.where(tri[:, :, None], bcum[:, :, :, None, :] - bcum[:, :, None, :, :], -jnp.inf))
    a = jnp.einsum('bhtd,bhsd,bhtsd->bhts', q, k, decay)
    o = jnp.einsum('bhtd,bhde->bhte', q * jnp.exp(bcum), s_mat) + jnp.einsum('bhts,bhse->bhte', a, v)
    b_end = bcum[:, :, -1]
    s_new = (jnp.exp(b_end)[..., None] * s_mat
             + jnp.einsum('bhsd,bhse->bhde', k * jnp.exp(b_end[:, :, None] - bcum), v))
    return s_new, o

def _even_mixer(h, w_in, gate_bias, q_gain, k_gain, rel_bias, ml_gain, w_out):
    b, t, _ = h.shape
    f32 = jnp.float32
    q_na, k_na, v_na, q_ml, k_ml, v_ml, o_ml, g_ml = _split(h @ w_in, EVEN_SIZES)
    split_heads = lambda a, n: a.reshape(b, t, n, -1).astype(f32)
    y_na = _neighbourhood_attention(_rms(split_heads(q_na, NA_HEADS), q_gain),
                                    _rms(split_heads(k_na, NA_HEADS), k_gain),
                                    split_heads(v_na, NA_HEADS),
                                    rel_bias.astype(f32)).reshape(b, t, NA_WIDTH)
    to_bhtd = lambda a: split_heads(a, ML_HEADS).transpose(0, 2, 1, 3)
    gates = (g_ml.astype(f32) + gate_bias.astype(f32)).reshape(b, t, 4, ML_HEADS).transpose(2, 0, 3, 1)
    ig_f, fg_f, ig_b, fg_b = gates[0], gates[1], gates[2], gates[3]
    qh, kh, vh = to_bhtd(q_ml), to_bhtd(k_ml) * ML_QK ** -0.5, to_bhtd(v_ml)
    init = (jnp.zeros((b, ML_HEADS, ML_QK, ML_V), f32), jnp.zeros((b, ML_HEADS, ML_QK), f32),
            jnp.zeros((b, ML_HEADS), f32))
    h_ml = _bidirectional(_mlstm_chunk, init,
                          (qh, kh, vh, ig_f, jax.nn.log_sigmoid(fg_f)),
                          (qh, kh, vh, ig_b, jax.nn.log_sigmoid(fg_b)), ML_CHUNK)
    h_ml = h_ml.transpose(0, 2, 1, 3).reshape(b, t, ML_WIDTH)
    y_ml = _head_rms(h_ml, ML_HEADS, ml_gain) * jax.nn.sigmoid(o_ml.astype(f32))
    return jnp.concatenate([y_na, y_ml], axis=-1).astype(h.dtype) @ w_out

def _odd_mixer(h, w_in, gate_up, gate_bias, head_gain, w_out):
    b, t, _ = h.shape
    f32 = jnp.float32
    q, k, v, r, lr_f, lr_b = _split(h @ w_in, ODD_SIZES)
    to_bhtd = lambda a: a.reshape(b, t, GLA_HEADS, -1).astype(f32).transpose(0, 2, 1, 3)
    log_gate = lambda lr, j: jax.nn.log_sigmoid(lr.astype(f32) @ gate_up[j].astype(f32)
                                                + gate_bias[j].astype(f32)) / GLA_TAU
    qh, kh, vh = to_bhtd(q) * GLA_DK ** -0.5, to_bhtd(k), to_bhtd(v)
    init = jnp.zeros((b, GLA_HEADS, GLA_DK, GLA_DV), f32)
    o = _bidirectional(_gla_chunk, init,
                       (qh, kh, vh, to_bhtd(log_gate(lr_f, 0))),
                       (qh, kh, vh, to_bhtd(log_gate(lr_b, 1))), GLA_CHUNK)
    o = o.transpose(0, 2, 1, 3).reshape(b, t, GLA_VW)
    y = _head_rms(o, GLA_HEADS, head_gain) * jax.nn.silu(r.astype(f32))
    return y.astype(h.dtype) @ w_out

def _conv_ffn(h, w_up, conv_w, conv_b, w_down):
    u = h @ w_up
    t = u.shape[1]
    pad = CONV_W // 2
    up = jnp.pad(u, ((0, 0), (pad, CONV_W - 1 - pad), (0, 0)))
    acc = conv_b
    for i in range(CONV_W):
        acc = acc + up[:, i:i + t] * conv_w[i]
    g, val = jnp.split(acc, 2, axis=-1)
    return (jax.nn.silu(g) * val) @ w_down

def setup_inputs(seed: int = 0) -> dict:
    key = jax.random.key(seed)
    ks = jax.random.split(key, 24)
    nrm = lambda kk, shape, scale: jax.random.normal(kk, shape, jnp.float32) * scale
    gain = lambda kk, shape: 1.0 + nrm(kk, shape, 0.02)
    f_bias = jnp.linspace(3.0, 6.0, ML_HEADS, dtype=jnp.float32)
    zeros_h = jnp.zeros((ML_HEADS,), jnp.float32)
    gate_offset = jnp.concatenate([zeros_h, f_bias, zeros_h, f_bias])
    return {
        'x': nrm(ks[0], (BATCH, SEQ, D_MODEL), 1.0),
        'meta_tokens': nrm(ks[1], (N_META, D_MODEL), 1.0),
        'norm_mix': gain(ks[2], (DEPTH, D_MODEL)),
        'norm_ffn': gain(ks[3], (DEPTH, D_MODEL)),
        'ab_w_in': nrm(ks[4], (N_EVEN, D_MODEL, EVEN_IN), D_MODEL ** -0.5),
        'ab_gate_bias': nrm(ks[5], (N_EVEN, 4 * ML_HEADS), 0.01) + gate_offset,
        'ab_q_gain': gain(ks[6], (N_EVEN, NA_DIM)),
        'ab_k_gain': gain(ks[7], (N_EVEN, NA_DIM)),
        'ab_rel_bias': nrm(ks[8], (N_EVEN, NA_HEADS, 2 * WIN_H - 1, 2 * WIN_W - 1), 0.02),
        'ab_ml_gain': gain(ks[9], (N_EVEN, ML_WIDTH)),
        'ab_w_out': nrm(ks[10], (N_EVEN, MIX_WIDTH, D_MODEL), MIX_WIDTH ** -0.5),
        'c_w_in': nrm(ks[11], (N_ODD, D_MODEL, ODD_IN), D_MODEL ** -0.5),
        'c_gate_up': nrm(ks[12], (N_ODD, 2, GLA_RANK, GLA_KW), GLA_RANK ** -0.5),
        'c_gate_bias': nrm(ks[13], (N_ODD, 2, GLA_KW), 0.1),
        'c_head_gain': gain(ks[14], (N_ODD, GLA_VW)),
        'c_w_out': nrm(ks[15], (N_ODD, GLA_VW, D_MODEL), GLA_VW ** -0.5),
        'ffn_w_up': nrm(ks[16], (DEPTH, D_MODEL, 2 * D_FF), D_MODEL ** -0.5),
        'ffn_conv_w': nrm(ks[17], (DEPTH, CONV_W, 2 * D_FF), CONV_W ** -0.5),
        'ffn_conv_b': nrm(ks[18], (DEPTH, 2 * D_FF), 0.01),
        'ffn_w_down': nrm(ks[19], (DEPTH, D_FF, D_MODEL), D_FF ** -0.5),
    }

def reference(x, meta_tokens, norm_mix, norm_ffn, ab_w_in, ab_gate_bias, ab_q_gain, ab_k_gain,
              ab_rel_bias, ab_ml_gain, ab_w_out, c_w_in, c_gate_up, c_gate_bias, c_head_gain,
              c_w_out, ffn_w_up, ffn_conv_w, ffn_conv_b, ffn_w_down):
    b = x.shape[0]
    meta = jnp.broadcast_to(meta_tokens.astype(x.dtype)[None], (b, N_META, x.shape[-1]))
    h = jnp.concatenate([meta, x], axis=1)
    for i in range(DEPTH):
        j = i // 2
        hn = _rms(h, norm_mix[i])
        if i % 2 == 0:
            h = h + _even_mixer(hn, ab_w_in[j], ab_gate_bias[j], ab_q_gain[j], ab_k_gain[j],
                                ab_rel_bias[j], ab_ml_gain[j], ab_w_out[j])
        else:
            h = h + _odd_mixer(hn, c_w_in[j], c_gate_up[j], c_gate_bias[j], c_head_gain[j], c_w_out[j])
        h = h + _conv_ffn(_rms(h, norm_ffn[i]), ffn_w_up[i], ffn_conv_w[i], ffn_conv_b[i], ffn_w_down[i])
    return h[:, N_META:]


_drawn_inputs = setup_inputs


def setup_inputs(seed=0):
    import zlib

    import numpy as np

    out = dict(_drawn_inputs(seed))
    spreads = {}
    factors = {'ab_q_gain': 8.0,
     'ab_k_gain': 8.0,
     'ab_rel_bias': 49.058,
     'ab_ml_gain': 5.2,
     'c_gate_bias': 2.868,
     'c_head_gain': 19.691,
     'ffn_conv_b': 5.145,
     'norm_ffn': 4.345}
    for name, (base, spread) in spreads.items():
        noise = np.random.default_rng([zlib.crc32(name.encode()), seed]).standard_normal(out[name].shape)
        drawn = base * np.exp(spread * noise) if base else spread * noise
        out[name] = __import__('jax').numpy.asarray(drawn.astype(out[name].dtype))
    for name, factor in factors.items():
        out[name] = (out[name] * factor).astype(out[name].dtype)
    return out
```

```python
import numpy as np

import concourse.bass as bass
from concourse import mybir
from contextlib import ExitStack

F32 = mybir.dt.float32
F32R = mybir.dt.float32r
BF16 = mybir.dt.bfloat16
U16 = mybir.dt.uint16
ALU = mybir.AluOpType
ACT = mybir.ActivationFunctionType
AX = mybir.AxisListType

P = 128
D = 2048
KT = D // P
SEQ, META = 256, 16
T = SEQ + META
TILES = [(0, META), (META, P), (META + P, P)]
EPS = 1e-6
GRID_W, WIN_W, WIN_H, ROWS = 64, 16, 8, SEQ // 64
NA_HEADS, ML_HEADS, GLA_HEADS = 8, 4, 4
NA_SCALE = 128 ** -0.5
ML_SCALE = 128 ** -0.5
GLA_SCALE = 256 ** -0.5
GLA_TAU = 16.0
D_FF = 5632
FT = D_FF // P
PARTS = [16, 14, 14]
RANK = 16
NEG = -1.0e30
AB_COLS, C_COLS = 48 * P, 48 * P
GATES, LRS = 16, 2 * RANK

V_MIX, V_FFN, V_ML, V_GLA, V_QG, V_KG, V_GB = 0, 32, 64, 72, 88, 89, 90
V_N = 106

LEVELS = [("in", H) for H in (1, 2, 4, 8, 16, 32, 64)] + [("edge", META), ("edge", META + P)]
NL = len(LEVELS)


class Chain:

    def __init__(self, eng, sem):
        self.eng, self.sem, self.n, self.off = eng, sem, 0, 0

    def link(self, ins):
        ins.then_inc(self.sem, 1)
        self.n += 1
        self.eng.wait_ge(self.sem, self.off + self.n)

    def enter(self, i, per):
        self.off = i * per if per else 0

    def leave(self, rounds, per):
        self.off = 0
        self.n += (rounds - 1) * per


def build(nc, x, meta_tokens, norm_mix, norm_ffn, ab_w_in, ab_gate_bias, ab_q_gain, ab_k_gain,
          ab_rel_bias, ab_ml_gain, ab_w_out, c_w_in, c_gate_up, c_gate_bias, c_head_gain, c_w_out,
          ffn_w_up, ffn_conv_w, ffn_conv_b, ffn_w_down, out):
    gemms = []
    state = {"it": 0}

    def add(name, w, row0, kc, iters, col, evac, **kw):
        gemms.append(dict(name=name, w=w, row0=row0, kc=kc, iters=iters, col=col, evac=evac,
                          it0=state["it"], **kw))
        state["it"] += iters

    ab_in, c_in = ab_w_in[0], c_w_in[0]
    plain = (0, 256, 512)
    add("ab_in", ab_in, 0, 8, 12, plain, "store")
    add("ab_out", ab_w_out[0], 0, 8, 4, plain, "resid")

    def ffn(layer):
        t0 = 0
        for part, nt in enumerate(PARTS):
            add(f"up{layer}{part}", ffn_w_up[layer], 0, 8, nt // 2, (t0 * P, D_FF + t0 * P, 256),
                "conv", layer=layer, t0=t0)
            add(f"down{layer}{part}", ffn_w_down[layer], t0, nt // 2, 4, plain, "resid", mid=True)
            t0 += nt

    ffn(0)
    add("c_in", c_in, 0, 8, 12, plain, "store")
    add("c_out", c_w_out[0], 0, 8, 4, plain, "resid")
    ffn(1)
    G = {g["name"]: g for g in gemms}
    conv_it = 0
    for g in gemms:
        if g["evac"] == "conv":
            g["c0"] = conv_it
            conv_it += g["iters"]
        g["c_end"] = conv_it
    for a, b in zip(gemms, gemms[1:] + [None]):
        a["next"] = b

    ctx = ExitStack()
    with ctx:
        place = {"at": 16512}

        def sb(name, shape, dt=F32, at=None):
            size = int(np.prod(shape[1:])) * (2 if dt in (BF16, U16) else 4)
            if at is None:
                at = place["at"]
                place["at"] = (at + size + 31) // 32 * 32
            assert at + size <= 229344, (name, at, size)
            return nc.alloc_sbuf_tensor_at(name, shape, dt, offset=at)

        h = sb("h", [P, KT, T])
        at_act_hi = place["at"]
        act_hi = sb("act_hi", [P, KT, T], F32R)
        at_act_lo = place["at"]
        act_lo = sb("act_lo", [P, KT, T], F32R)
        y_raw = sb("y_raw", [P, KT, T], at=at_act_hi)
        q_rev = sb("q_rev", [P, NA_HEADS, T], at=at_act_hi + 8 * T * 4)
        raw = sb("raw", [P, 4, 8 * 256])
        w_hi = sb("w_hi", [P, 4, 8 * P], F32R)
        w_lo = sb("w_lo", [P, 4, 8 * P], F32R)
        ident = sb("ident", [P, P])
        ones = sb("ones", [P, P])
        vec = sb("vec", [P, V_N])
        conv = sb("conv", [P, 2, 4, 2 * FT])
        tail_w = sb("tail_w", [P, KT, GATES + LRS])
        tail = sb("tail", [LRS, T])
        gate_b = sb("gate_b", [GATES, 1])
        eps = sb("eps", [P, 1])
        ntmp = sb("ntmp", [P, 4, T])
        rstd = sb("rstd", [P, T])
        zone = place["at"]
        proj = sb("proj", [P, 48, T], at=zone)
        v_tok = sb("v_tok", [P, 3, D], at=zone + 48 * T * 4)
        misc = zone + 48 * T * 4 + 3 * D * 4
        vreg0 = zone + 16 * T * 4
        vreg1 = zone + 32 * T * 4
        sq2 = sb("sq2", [P, 2, 2, T], at=vreg0)
        rt2 = sb("rt2", [P, 2, 2, T], at=vreg1)
        e_sq = sb("e_sq", [P, 2, 2, T], at=vreg0)
        e_rr = sb("e_rr", [P, 4, T], at=vreg0 + 4 * T * 4)
        negmask = sb("negmask", [P, 3, 2, T], at=vreg1)
        a = at_act_lo
        na_s = sb("na_s", [P, 2, T], at=a)
        na_p = sb("na_p", [P, 2, T], at=a + 2 * T * 4)
        pt = sb("pt", [P, 2, 2, T], at=a + 4 * T * 4)
        pt_m = sb("pt_m", [META, 2, T], at=a + 8 * T * 4)
        na_m = sb("na_m", [META, NA_HEADS, META], at=a + 10 * T * 4)
        na_mt = sb("na_mt", [META, NA_HEADS, META], at=a + 11 * T * 4)
        col = sb("col", [P, 64], at=a + 12 * T * 4)
        winmask = sb("winmask", [P, GRID_W], at=a + 12 * T * 4 + 256)
        bias = sb("bias", [P, 3, T], at=a + 13 * T * 4)
        ml_x = sb("ml_x", [P, 2, 2, T], at=a)
        ml_p = sb("ml_p", [P, 2, T], at=a + 10 * T * 4)
        ml_pt = sb("ml_pt", [P, T], at=a + 12 * T * 4 + 512)
        rows = sb("rows", [ML_HEADS, 7, 2, T], at=zone)
        cols = sb("cols", [P, 3, 2, 2, ML_HEADS], at=zone + 14 * T * 4)
        selrow = sb("selrow", [ML_HEADS, ML_HEADS, P], at=vreg1 + 6 * T * 4)
        den = sb("den", [P, 8], at=vreg1 + 6 * T * 4 + 2048)
        gup = sb("gup", [LRS, 2, 8 * P], at=at_act_hi)
        ge = sb("ge", [P, 8, T], at=at_act_lo)
        bc = sb("bc", [P, 2, 8, T], at=vreg0)
        gl_e = sb("gl_e", [P, 2, 2, T], at=a)
        gl_x = sb("gl_x", [P, 2, 2, T], at=a + 4 * T * 4)
        at_t = sb("at_t", [P, 2, 2, T], at=a + 8 * T * 4)
        at_m = sb("at_m", [META, 2, T], at=a + 12 * T * 4)
        lmask = sb("lmask", [P, 2, 7, P], BF16, at=misc)
        o_sq = sb("o_sq", [P, 16, T], at=zone)
        o_rr = sb("o_rr", [P, 4, T], at=vreg0)
        g_hi = sb("g_hi", [P, max(PARTS), T], F32R, at=zone)
        g_lo = sb("g_lo", [P, max(PARTS), T], F32R, at=zone + max(PARTS) * T * 4)
        f0 = zone + 2 * max(PARTS) * T * 4
        acc = sb("acc", [P, 2, 2, T], at=f0)
        sg = sb("sg", [P, 2, T], at=f0 + 4 * T * 4)
        gp = sb("gp", [P, 2, T], at=f0 + 6 * T * 4)
        sq = sb("sq", [P, KT, T], at=zone)
        tok = sb("tok", [P, 3, D], at=zone)
        stage = sb("stage", [P, 9, P], at=zone + 3 * D * 4)
        ostage = sb("ostage", [P, 2, D], at=zone)

        ps = ctx.enter_context(nc.psum_tensor("ps", [P, 8, 512], F32))
        pm = [ps[:, 4 + b, :] for b in range(4)]

        names = {}

        def S(name):
            if name not in names:
                names[name] = ctx.enter_context(nc.semaphore(name))
            return names[name]

        landed = [S(f"weights_landed{j}") for j in range(4)]
        all_sems = """const_done tok_in param_in tail_in gup_in hi_done split_done used bank_free conv_mid gates_done
            silu_done mid_done act_chain dve_chain pool_chain xT_done h_built par_done par_evac
            sq_ready ss_ready rt_ready n_ready nhi_done act_ready tail_done tail_read tail_evac mid_split
            vt_done vt_ab vt_m qk_sq qk_ss qk_rt qk_ready bias_in0 bias_in1 bias_in2 bias_ready bias_used
            na_scores na_biased na_max na_exp na_norm na_ptdone na_ptcopied na_pv na_stored mask_done
            nm_scores nm_max nm_exp nm_norm nm_ptdone nm_ptcopied
            ml_sel ml_rows ml_ln ml_c ml_nm ml_en ml_cols ml_colc ml_cb ml_scores ml_x_done ml_w_done ml_pn ml_used
            ml_ptdone ml_ptcopied ml_pv ml_stored po_sq po_ss po_rt po_gate q_scaled
            gu_mm gu_x gu_ln b_done gl_diag gl_dsub gl_psub gl_exp gl_dmul gl_pmul gl_g gl_cp gl_at gl_pv gl_stored
            lmask_done out_done out_evac out_sent sel_done""".split()
        for n in all_sems:
            S(n)

        def bcast(ap, n, at=1):
            dims = [list(v) for v in ap.ap]
            dims.insert(at, [0, n])
            return bass.AP(ap.tensor, ap.offset, dims)

        def strided(ap, dims):
            return bass.AP(ap.tensor, ap.offset, [list(ap.ap[0])] + dims)

        units = [(hd, d, l) for hd in range(GLA_HEADS) for d in range(2) for l in range(NL)]

        def level_span(l):
            kind, H = LEVELS[l]
            if kind == "in":
                return (0, T) if H <= 8 else (META, T)
            return (0, META + P) if H == META else (0, T)

        def halves(ap, l, d, side):
            kind, H = LEVELS[l]
            t0, t1 = level_span(l)
            right = (side == "q") != (d == 1)
            if kind == "in":
                v = ap[:, :, t0:t1].rearrange("p a (g b) -> p a g b", b=2 * H)
                r = H if d else H - 1
                return (v[:, :, :, H:2 * H] if right else v[:, :, :, 0:H]), v[:, :, :, r:r + 1], H
            r = H if d else H - 1
            return (ap[:, :, H:t1] if right else ap[:, :, 0:H]), ap[:, :, r:r + 1], None

        def level_views(hd, d, l, side, u):
            b, ref, H = halves(bc[:, d, 2 * hd:2 * hd + 2, :], l, d, side)
            o, _, _ = halves(gl_e[:, u % 2, :, :], l, d, side)
            n = H if H else b.shape[2]
            dims = [list(v) for v in ref.ap]
            dims[-1] = [0, n]
            return [(o, b, bass.AP(ref.tensor, ref.offset, dims), None)]

        def level_muls(hd, d, l, side, u):
            e, _, _ = halves(gl_e[:, u % 2, :, :], l, d, side)
            xo, _, _ = halves(gl_x[:, u % 2, :, :], l, d, side)
            base = 0 if side == "q" else 8
            s, _, _ = halves(proj[:, base + 2 * hd:base + 2 * hd + 2, :], l, d, side)
            return [(e, xo, s)]

        E_V = list(range(16, 24)) + list(range(32, 40))
        O_V = list(range(16, 32))

        block = ctx.enter_context(nc.Block())

        @block.sync
        def _(sp):
            sp.dma_start(tok[0:META, 0, :], meta_tokens).then_inc(S("tok_in"), 16)
            for b in range(2):
                sp.dma_start(tok[:, 1 + b, :], x[0, b * P:(b + 1) * P, :]).then_inc(S("tok_in"), 16)

            def load(g, i, waits=True):
                n = g["w"].shape[1]
                for j in range(4):
                    grp, c = j // 2, j % 2
                    if waits:
                        sp.wait_ge(S("split_done"), (i + g["it0"]) * 8 + (2 * j - 6))
                    kc = g["kc"]
                    first = (g["row0"] + c * kc) * P * n + g["col"][grp]
                    src = bass.AP(g["w"].tensor, g["w"].offset + first + i * g["col"][2],
                                  [[n, P], [n * P, kc], [1, 256]])
                    dst = raw[:, j, 0:kc * 256].rearrange("p (k c) -> p k c", k=kc)
                    sp.dma_start(dst, src).then_inc(landed[j], 16)

            for g in gemms:
                start = 0
                if g["it0"] == 0:
                    load(g, 0, waits=False)
                    start = 1
                with sp.Fori(start, g["iters"]) as i:
                    load(g, i)
            for b in range(2):
                sp.wait_ge(S("out_evac"), 4 * (b + 1))
                sp.dma_start(out[0, b * P:(b + 1) * P, :], ostage[:, b, :]).then_inc(S("out_sent"), 16)
            sp.wait_ge(S("out_sent"), 32)

        @block.gpsimd
        def _(pool):
            chain = Chain(pool, S("pool_chain"))
            g_ = nc.gpsimd
            chain.link(g_.memset(ident[:, :], 0.0))
            g_.affine_select(out=ident[:, :], in_=ident[:, :], compare_op=ALU.not_equal, fill=1.0, base=0,
                             pattern=[[-1, P]], channel_multiplier=1).then_inc(S("const_done"), 1)

            pool.wait_ge(S("vt_ab"), 16)
            pool.wait_ge(S("act_ready"), 16)
            pool.wait_ge(S("used"), 8 * G["ab_out"]["it0"])
            chain.link(g_.memset(winmask[:, :], 0.0))
            for half in range(2):
                w = winmask[64 * half:64 * half + 64, 0:GRID_W - WIN_W]
                chain.link(g_.affine_select(out=w, in_=w, compare_op=ALU.is_ge, fill=NEG,
                                            base=WIN_W // 2 - (GRID_W - 1), pattern=[[1, GRID_W - WIN_W]],
                                            channel_multiplier=1))
                w = winmask[64 * half:64 * half + 64, WIN_W:GRID_W]
                chain.link(g_.affine_select(out=w, in_=w, compare_op=ALU.is_gt, fill=NEG,
                                            base=(GRID_W - 1) + WIN_W // 2 - WIN_W, pattern=[[-1, GRID_W - WIN_W]],
                                            channel_multiplier=-1))
            for b in range(3):
                chain.link(g_.memset(bias[:, b, 0:META], 0.0))
            for n in range(2 * NA_HEADS):
                pool.wait_ge(S(f"bias_in{n % 3}"), 32 * (n // 3 + 1))
                b = bias[:, n % 3, META:T].rearrange("p (r c) -> p r c", r=ROWS)
                g_.tensor_tensor(b, b, bcast(winmask[:, :], ROWS), ALU.add).then_inc(S("bias_ready"), 1)
            pool.wait_ge(S("qk_ready"), NA_HEADS)
            chain.link(g_.memset(negmask[:, :, :, :], 0.0))
            for tt, (t0, tn) in enumerate(TILES):
                for d in range(2):
                    m = negmask[0:tn, tt, d, :]
                    sgn = 1 - 2 * d
                    g_.affine_select(out=m, in_=m, compare_op=ALU.is_ge, fill=NEG, base=sgn * t0,
                                     pattern=[[-sgn, T]], channel_multiplier=sgn).then_inc(S("mask_done"), 1)
            pool.wait_ge(S("na_stored"), NA_HEADS)
            chain.link(g_.memset(selrow[:, :, :], 0.0))
            g_.affine_select(out=selrow[:, :, :], in_=selrow[:, :, :], compare_op=ALU.not_equal, fill=1.0, base=0,
                             pattern=[[-1, ML_HEADS], [0, P]], channel_multiplier=1).then_inc(S("sel_done"), 1)

            pool.wait_ge(S("na_biased"), 2 * NA_HEADS)
            for d in range(2):
                for l in range(7):
                    H = LEVELS[l][1]
                    m = lmask[:, d, l, :]
                    chain.link(g_.memset(m, 0.0))
                    half = m.rearrange("p (g b) -> p g b", b=2 * H)[:, :, (0 if d else H):(H if d else 2 * H)]
                    lo = H if d else 0
                    chain.link(g_.memset(half, 1.0))
                    chain.link(g_.affine_select(out=half, in_=half, compare_op=ALU.is_ge, fill=0.0, base=-lo,
                                                pattern=[[-2 * H, P // (2 * H)], [0, H]], channel_multiplier=1))
                    g_.affine_select(out=half, in_=half, compare_op=ALU.is_ge, fill=0.0, base=lo + H - 1,
                                     pattern=[[2 * H, P // (2 * H)], [0, H]],
                                     channel_multiplier=-1).then_inc(S("lmask_done"), 1)

            pool.wait_ge(S("b_done"), 2)

            def sub(u):
                hd, d, l = units[u]
                if u >= 2:
                    pool.wait_ge(S("gl_dmul"), u - 1)
                    pool.wait_ge(S("gl_pmul"), u - 1)
                for o, b, r, _ in level_views(hd, d, l, "k", u):
                    last = g_.tensor_tensor(o, r, b, ALU.subtract)
                last.then_inc(S("gl_psub"), 1)

            def mul(u):
                hd, d, l = units[u]
                if u >= 2:
                    pool.wait_ge(S("gl_g"), u - 1)
                pool.wait_ge(S("gl_exp"), u + 1)
                for o, xo, s in level_muls(hd, d, l, "k", u):
                    last = g_.tensor_tensor(xo, o, s, ALU.mult)
                last.then_inc(S("gl_pmul"), 1)

            sub(0)
            for u in range(len(units)):
                if u + 1 < len(units):
                    sub(u + 1)
                mul(u)

        @block.scalar
        def _(act):
            chain = Chain(act, S("act_chain"))
            A = nc.scalar.activation

            rows_of = [(norm_mix, 32), (norm_ffn, 32), (ab_ml_gain, 8), (c_head_gain, 16),
                       (ab_q_gain, 1), (ab_k_gain, 1), (c_gate_bias, 16)]
            at = 0
            for v, n in rows_of:
                act.dma_start(stage[at:at + n, 8, :], bass.AP(v.tensor, v.offset, [[P, n], [1, P]])).then_inc(S("param_in"), 16)
                at += n
            for layer in range(2):
                for tap in range(4):
                    v = ffn_conv_w[layer, tap] if tap < 3 else ffn_conv_b[layer]
                    act.dma_start(stage[0:2 * FT, 4 * layer + tap, :],
                                  v.rearrange("(m p) -> m p", p=P)).then_inc(S("param_in"), 16)
            act.dma_start(gate_b[:, :], ab_gate_bias.rearrange("a g -> g a")).then_inc(S("tail_in"), 16)
            for w, c0, n, o in ((ab_in, AB_COLS, GATES, 0), (c_in, C_COLS, LRS, GATES)):
                act.dma_start(tail_w[:, :, o:o + n], bass.AP(w.tensor, w.offset + c0,
                              [[w.shape[1], P], [w.shape[1] * P, KT], [1, n]])).then_inc(S("tail_in"), 16)

            def hi(g, it, s):
                j, m, kc = s // 2, s % 2, g["kc"]
                n = it + g["it0"]
                act.wait_ge(landed[j], (n + 1) * 16)
                act.wait_ge(S("used"), n * 8 + (s - 3))
                src = raw[:, j, 0:kc * 256].rearrange("p (k c) -> p k c", k=kc)[:, :, m * P:(m + 1) * P]
                dst = w_hi[:, s % 4, 0:kc * P].rearrange("p (k c) -> p k c", k=kc)
                A(dst, src, ACT.Copy).then_inc(S("hi_done"), 1)

            def evac(g, i, grp):
                n = i + g["it0"]
                banks = ps[:, 2 * grp:2 * grp + 2, 0:T]
                if g["evac"] == "resid":
                    return
                act.wait_ge(S("used"), n * 8 + 4 * (grp + 1))
                if g["evac"] == "store":
                    A(proj[:, bass.ds(i * 4 + 2 * grp, 2), :], banks, ACT.Copy).then_inc(S("bank_free"), 1)
                    return
                c = i + g["c0"]
                if grp == 0:
                    act.wait_ge(S("mid_done"), c)
                for m in range(2):
                    mt = i * 2 + (grp * FT + g["t0"] + m)
                    ins = A(acc[:, grp, m, :], ps[:, 2 * grp + m, 0:T], ACT.Identity,
                            bias=conv[:, g["layer"], 3, bass.ds(mt, 1)], scale=conv[:, g["layer"], 1, bass.ds(mt, 1)])
                ins.then_inc(S("conv_mid"), 1)
                if grp == 1:
                    act.wait_ge(S("gates_done"), c + 1)
                    A(sg[:, :, :], acc[:, 0, :, :], ACT.Silu).then_inc(S("silu_done"), 1)

            def gemm(g):
                if g["it0"] == 0:
                    for s in range(3):
                        j, m, kc = s // 2, s % 2, g["kc"]
                        act.wait_ge(landed[j], 16)
                        src = raw[:, j, 0:kc * 256].rearrange("p (k c) -> p k c", k=kc)[:, :, m * P:(m + 1) * P]
                        A(w_hi[:, s, 0:kc * P].rearrange("p (k c) -> p k c", k=kc), src, ACT.Copy).then_inc(S("hi_done"), 1)

                def body(i, nxt, ni):
                    for s in range(3, 7):
                        hi(g, i, s)
                    evac(g, i, 0)
                    hi(g, i, 7)
                    if nxt:
                        for s in range(3):
                            hi(nxt, ni, s)
                    evac(g, i, 1)

                with act.Fori(0, g["iters"] - 1) as i:
                    body(i, g, i + 1)
                body(g["iters"] - 1, g["next"], 0)

            def hi_tiles(e):
                for k in range(KT):
                    act.wait_ge(S("n_ready"), e * KT + k + 1)
                    A(act_hi[:, k, :], ntmp[:, k % 4, :], ACT.Copy).then_inc(S("nhi_done"), 1)

            def norm(n, e):
                for q in range(4):
                    A(sq[:, 4 * q:4 * q + 4, :], h[:, 4 * q:4 * q + 4, :], ACT.Square).then_inc(S("sq_ready"), 1)
                act.wait_ge(S("ss_ready"), n + 1)
                A(rstd[:, :], pm[0][:, 0:T], ACT.Sqrt, bias=eps[:, :], scale=1.0 / D).then_inc(S("rt_ready"), 1)
                hi_tiles(e)
                if n in (0, 2):
                    act.wait_ge(S("tail_done"), n // 2 + 1)
                    if n == 0:
                        A(tail[0:GATES, :], pm[1][0:GATES, 0:T], ACT.Identity, bias=gate_b[:, :]).then_inc(S("tail_evac"), 1)
                    else:
                        A(tail[:, :], pm[1][0:LRS, 0:T], ACT.Copy).then_inc(S("tail_evac"), 1)

            def gl_store(hd):
                for e in range(4):
                    n = 4 * hd + e
                    act.wait_ge(S("gl_pv"), n + 1)
                    A(y_raw[:, n, :], pm[2 + n % 2][:, 0:T], ACT.Copy).then_inc(S("gl_stored"), 1)

            def v_tokens(r, tiles):
                for n in range(len(tiles)):
                    act.wait_ge(S("vt_done"), 16 * r + n + 1)
                    A(v_tok[:, 1:3, n * P:(n + 1) * P], strided(pm[n % 4], [[P, 2], [1, P]]), ACT.Copy).then_inc(S("vt_ab"), 1)

            for b in range(2):
                act.wait_ge(S("par_done"), b + 1)
                if b == 0:
                    A(conv[:, :, :, :].rearrange("p a b c -> p (a b c)")[:, 0:440], pm[0][:, 0:440], ACT.Copy).then_inc(S("par_evac"), 1)
                else:
                    A(conv[:, :, :, :].rearrange("p a b c -> p (a b c)")[:, 440:704], pm[1][:, 0:264], ACT.Copy).then_inc(S("par_evac"), 1)
                    A(vec[:, :], pm[1][:, 264:264 + V_N], ACT.Copy).then_inc(S("par_evac"), 1)
            for k in range(0, KT, 2):
                act.wait_ge(S("xT_done"), k + 2)
                A(h[:, k:k + 2, :], ps[:, k % 4:k % 4 + 2, 0:T], ACT.Copy).then_inc(S("h_built"), 1)
            act.wait_ge(S("h_built"), KT // 2)
            act.wait_ge(S("const_done"), 3)
            act.wait_ge(S("tail_in"), 48)
            norm(0, 0)
            gemm(G["ab_in"])

            act.wait_ge(S("bank_free"), 2 + 2 * G["ab_out"]["it0"])
            v_tokens(0, E_V)
            def load_bias(n):
                hd, qt = n // 2, n % 2
                if n >= 3:
                    act.wait_ge(S("na_biased"), n - 2)
                for rr in range(2):
                    r = 2 * qt + 1 - rr
                    dst = bias[64 * rr:64 * rr + 64, n % 3, META:T].rearrange("p (r c) -> p r c", r=ROWS)
                    off = ab_rel_bias.offset + hd * 15 * 31 + (WIN_H - 1 - r) * 31 + (WIN_W - 1) - (GRID_W - 1)
                    act.dma_start(dst, bass.AP(ab_rel_bias.tensor, off, [[1, GRID_W], [31, ROWS], [1, GRID_W]])).then_inc(S(f"bias_in{n % 3}"), 16)
            for n in range(3):
                load_bias(n)
            qk = proj[:, 0:16, :].rearrange("p (g h) t -> p g h t", h=NA_HEADS)
            act.wait_ge(S("vt_m"), 16)
            for hd in range(NA_HEADS + 1):
                if hd < NA_HEADS:
                    if hd >= 2:
                        act.wait_ge(S("qk_ss"), hd - 1)
                    A(sq2[:, hd % 2, :, :], qk[:, :, hd, :], ACT.Square).then_inc(S("qk_sq"), 1)
                if hd >= 1:
                    u = hd - 1
                    act.wait_ge(S("qk_ss"), u + 1)
                    if u >= 2:
                        act.wait_ge(S("qk_ready"), u - 1)
                    A(rt2[:, u % 2, :, :], ps[:, 4 + 2 * (u % 2):6 + 2 * (u % 2), 0:T], ACT.Sqrt, bias=eps[:, :], scale=1.0 / P).then_inc(S("qk_rt"), 1)
            act.wait_ge(S("nm_max"), 1)
            A(na_m[:, :, :], na_m[:, :, :], ACT.Exp).then_inc(S("nm_exp"), 1)
            act.wait_ge(S("nm_ptdone"), 1)
            A(na_mt[:, :, :], pm[3][0:META, P:2 * P], ACT.Copy).then_inc(S("nm_ptcopied"), 1)
            act.wait_ge(S("nm_ptcopied"), 1)

            def na_exp(n):
                act.wait_ge(S("na_max"), n + 1)
                A(na_p[:, n % 2, :], na_s[:, n % 2, :], ACT.Exp, bias=col[:, n % 2:n % 2 + 1],
                  accum_out=col[:, 2 + n % 2:3 + n % 2]).then_inc(S("na_exp"), 1)

            N = 2 * NA_HEADS
            na_exp(0)
            for n in range(N):
                hd, qt = n // 2, n % 2
                if n + 3 < N:
                    load_bias(n + 3)
                if n + 1 < N:
                    na_exp(n + 1)
                t0 = TILES[1 + qt][0]
                act.wait_ge(S("na_ptdone"), n + 1)
                if hd >= 2:
                    act.wait_ge(S("na_pv"), hd - 1)
                if qt == 0:
                    A(pt_m[:, hd % 2, 0:META], na_mt[:, hd, :], ACT.Copy)
                A(pt_m[:, hd % 2, t0:t0 + P], pm[2][0:META, 2 * P:3 * P][:, ::-1], ACT.Copy)
                A(pt[:, hd % 2, :, t0:t0 + P], strided(pm[2][:, P - 1:P], [[P, 2], [-1, P]]), ACT.Copy).then_inc(S("na_ptcopied"), 1)
                if qt == 1:
                    act.wait_ge(S("na_pv"), hd + 1)
                    A(y_raw[:, hd, :], pm[3][:, 0:T], ACT.Copy).then_inc(S("na_stored"), 1)

            act.wait_ge(S("ml_sel"), 1)
            for j in range(4):
                ins = A(rows[:, j % 2, j // 2, :], pm[j][0:ML_HEADS, 0:T], ACT.Copy)
            chain.link(ins)
            fg, tmp = rows[:, 1, :, :], rows[:, 2, :, :]
            chain.link(A(tmp, fg, ACT.Abs))
            chain.link(A(tmp, tmp, ACT.Exp, scale=-1.0))
            A(tmp, tmp, ACT.Ln, bias=1.0).then_inc(S("ml_ln"), 1)
            act.wait_ge(S("ml_nm"), 1)
            A(rows[:, 6, :, :], rows[:, 2, :, :], ACT.Exp).then_inc(S("ml_en"), 1)
            act.wait_ge(S("ml_cols"), 1)
            A(cols[:, 1:3, :, :, :].rearrange("p a b c d -> p (a b c d)"), pm[0][:, 16:48], ACT.Copy)
            A(cols[0:META, 0, :, :, :].rearrange("p b c d -> p (b c d)"), pm[0][0:META, 0:16], ACT.Copy).then_inc(S("ml_colc"), 1)

            def ml_copy(u):
                hd, tt = u // 3, u % 3
                t0, tn = TILES[tt]
                act.wait_ge(S("ml_ptdone"), u + 1)
                if tt == 0 and hd >= 2:
                    act.wait_ge(S("ml_pv"), hd - 1)
                A(pt_m[:, hd % 2, t0:t0 + tn], pm[3][0:META, 2 * P:2 * P + tn], ACT.Copy)
                A(pt[:, hd % 2, :, t0:t0 + tn], strided(pm[3], [[P, 2], [1, tn]]), ACT.Copy).then_inc(S("ml_ptcopied"), 1)

            for u in range(12):
                hd, tt = u // 3, u % 3
                tn = TILES[tt][1]
                act.wait_ge(S("ml_x_done"), u + 1)
                A(ml_x[0:tn, u % 2, :, :], ml_x[0:tn, u % 2, :, :], ACT.Exp).then_inc(S("ml_w_done"), 1)
                if tt >= 1:
                    ml_copy(u - 1)
                if tt == 2:
                    ml_copy(u)
                    act.wait_ge(S("ml_pv"), hd + 1)
                    A(y_raw[:, 8 + 2 * hd:10 + 2 * hd, :], ps[:, 4:6, 0:T], ACT.Copy).then_inc(S("ml_stored"), 1)
            act.wait_ge(S("ml_stored"), 4)
            for hd in range(4):
                if hd >= 2:
                    act.wait_ge(S("po_ss"), hd - 1)
                A(e_sq[:, hd % 2, :, :], y_raw[:, 8 + 2 * hd:10 + 2 * hd, :], ACT.Square).then_inc(S("po_sq"), 1)
            act.wait_ge(S("po_ss"), 4)
            for hd in range(4):
                ins = A(e_rr[:, hd, :], pm[hd][:, 0:T], ACT.Sqrt, bias=eps[:, :], scale=1.0 / 256)
            ins.then_inc(S("po_rt"), 1)
            A(proj[:, 40:48, :], proj[:, 40:48, :], ACT.Sigmoid).then_inc(S("po_gate"), 1)
            hi_tiles(1)
            gemm(G["ab_out"])

            def ffn_stage(layer, n, e):
                act.wait_ge(S("bank_free"), 2 + 2 * G[f"up{layer}0"]["it0"])
                norm(n, e)
                for part in range(3):
                    gemm(G[f"up{layer}{part}"])
                    gemm(G[f"down{layer}{part}"])

            ffn_stage(0, 1, 2)
            act.wait_ge(S("bank_free"), 2 + 2 * G["c_in"]["it0"])
            norm(2, 3)
            gemm(G["c_in"])

            act.wait_ge(S("bank_free"), 2 + 2 * G["c_out"]["it0"])
            A(proj[:, 0:8, :], proj[:, 0:8, :], ACT.Copy, scale=GLA_SCALE).then_inc(S("q_scaled"), 1)
            v_tokens(1, O_V)
            act.wait_ge(S("gup_in"), 1)
            for j in range(2):
                act.dma_start(gup[RANK * j:RANK * (j + 1), j, :], c_gate_up[0, j]).then_inc(S("gup_in"), 16)
            act.wait_ge(S("vt_m"), 32)
            for j in range(2):
                for k in range(8):
                    n = 8 * j + k
                    act.wait_ge(S("gu_mm"), n + 1)
                    ins = A(bc[:, j, k, :], pm[n % 4][:, 0:T], ACT.Identity, bias=vec[:, V_GB + n:V_GB + n + 1])
                    ins.then_inc(S("gu_x"), 1)
                act.wait_ge(S("gu_x"), 8 * (j + 1))
                if j == 1:
                    act.wait_ge(S("b_done"), 1)
                chain.link(A(ge[:, :, :], bc[:, j, :, :], ACT.Abs))
                chain.link(A(ge[:, :, :], ge[:, :, :], ACT.Exp, scale=-1.0))
                A(ge[:, :, :], ge[:, :, :], ACT.Ln, bias=1.0).then_inc(S("gu_ln"), 1)
            for u, (hd, d, l) in enumerate(units):
                t0, t1 = level_span(l)
                act.wait_ge(S("gl_dsub"), u + 1)
                act.wait_ge(S("gl_psub"), u + 1)
                e = gl_e[:, u % 2, :, t0:t1]
                A(e, e, ACT.Exp, scale=1.0 / GLA_TAU).then_inc(S("gl_exp"), 1)
                if u % (2 * NL) == 5 and hd >= 1:
                    gl_store(hd - 1)
            gl_store(3)
            act.wait_ge(S("gl_stored"), 16)
            for hd in range(4):
                A(o_sq[:, 4 * hd:4 * hd + 4, :], y_raw[:, 4 * hd:4 * hd + 4, :], ACT.Square).then_inc(S("po_sq"), 1)
            act.wait_ge(S("po_ss"), 8)
            for hd in range(4):
                ins = A(o_rr[:, hd, :], pm[hd][:, 0:T], ACT.Sqrt, bias=eps[:, :], scale=1.0 / 512)
            ins.then_inc(S("po_rt"), 1)
            A(proj[:, 32:48, :], proj[:, 32:48, :], ACT.Silu).then_inc(S("po_gate"), 1)
            hi_tiles(4)
            gemm(G["c_out"])
            ffn_stage(1, 3, 5)
            for b in range(2):
                for q in range(4):
                    n = 4 * b + q
                    act.wait_ge(S("out_done"), n + 1)
                    A(ostage[:, b, 512 * q:512 * (q + 1)], pm[n % 4][:, :], ACT.Copy).then_inc(S("out_evac"), 1)

        @block.vector
        def _(dve):
            chain = Chain(dve, S("dve_chain"))
            V = nc.vector
            link = chain.link
            V.memset(ones[:, :], 1.0).then_inc(S("const_done"), 1)
            V.memset(eps[:, :], EPS).then_inc(S("const_done"), 1)
            dve.sem_inc(S("bank_free"), 2)

            def lo(g, it, s):
                j, m, kc = s // 2, s % 2, g["kc"]
                dve.wait_ge(S("hi_done"), (it + g["it0"]) * 8 + (s + 1))
                src = raw[:, j, 0:kc * 256].rearrange("p (k c) -> p k c", k=kc)[:, :, m * P:(m + 1) * P]
                hi = w_hi[:, s % 4, 0:kc * P].bitcast(F32).rearrange("p (k c) -> p k c", k=kc)
                dst = w_lo[:, s % 4, 0:kc * P].rearrange("p (k c) -> p k c", k=kc)
                V.tensor_tensor(dst, src, hi, ALU.subtract).then_inc(S("split_done"), 1)

            PER = 7

            def evac(g, i, grp):
                n = i + g["it0"]
                if g["evac"] == "store":
                    return
                if g["evac"] == "resid":
                    dve.wait_ge(S("used"), n * 8 + 4 * (grp + 1))
                    hh = h[:, bass.ds(i * 4 + 2 * grp, 2), :]
                    V.tensor_tensor(hh, ps[:, 2 * grp:2 * grp + 2, 0:T], hh, ALU.add).then_inc(S("bank_free"), 1)
                    return
                c = i + g["c0"]
                dve.wait_ge(S("conv_mid"), c * 2 + (grp + 1))
                wt = [conv[:, g["layer"], tap, :] for tap in range(4)]
                mt = [i * 2 + (grp * FT + g["t0"] + m) for m in range(2)]
                for m in range(2):
                    ins = V.scalar_tensor_tensor(acc[:, grp, m, 1:T], ps[:, 2 * grp + m, 0:T - 1],
                                                 wt[0][:, bass.ds(mt[m], 1)], acc[:, grp, m, 1:T], ALU.mult, ALU.add)
                link(ins)
                for m in range(2):
                    ins = V.scalar_tensor_tensor(acc[:, grp, m, 0:T - 1], ps[:, 2 * grp + m, 1:T],
                                                 wt[2][:, bass.ds(mt[m], 1)], acc[:, grp, m, 0:T - 1], ALU.mult, ALU.add)
                if grp == 0:
                    ins.then_inc(S("gates_done"), 1)
                    dve.wait_ge(S("gates_done"), c + 1)
                    dve.sem_inc(S("bank_free"), 1)
                    return
                link(ins)
                dve.sem_inc(S("bank_free"), 1)
                dve.wait_ge(S("silu_done"), c + 1)
                link(V.tensor_tensor(gp[:, :, :], sg[:, :, :], acc[:, 1, :, :], ALU.mult))
                dve.sem_inc(S("mid_done"), 1)
                ghi = g_hi[:, bass.ds(i * 2, 2), :]
                link(V.tensor_copy(ghi, gp[:, :, :]))
                link(V.tensor_tensor(g_lo[:, bass.ds(i * 2, 2), :], gp[:, :, :],
                                     g_hi[:, bass.ds(i * 2, 2), :].bitcast(F32), ALU.subtract))
                dve.sem_inc(S("mid_split"), 1)

            def gemm(g):
                if g["it0"] == 0:
                    for s in range(3):
                        lo(g, 0, s)
                per = {"store": 0, "resid": 0, "conv": 6}[g["evac"]]

                def body(i, nxt, ni):
                    n0 = chain.n
                    for s in range(3, 7):
                        lo(g, i, s)
                    evac(g, i, 0)
                    lo(g, i, 7)
                    if nxt:
                        for s in range(3):
                            lo(nxt, ni, s)
                    evac(g, i, 1)
                    assert chain.n - n0 == per, (chain.n - n0, per)

                with dve.Fori(0, g["iters"] - 1) as i:
                    chain.enter(i, per)
                    body(i, g, i + 1)
                chain.leave(g["iters"] - 1, per)
                body(g["iters"] - 1, g["next"], 0)

            def lo_tiles(e, make):
                def low(k):
                    dve.wait_ge(S("nhi_done"), e * KT + k + 1)
                    V.tensor_tensor(act_lo[:, k, :], ntmp[:, k % 4, :], act_hi[:, k, :].bitcast(F32),
                                    ALU.subtract).then_inc(S("act_ready"), 1)
                for k in range(KT):
                    if e or k >= 4:
                        dve.wait_ge(S("act_ready"), e * KT + max(k - 3, 0))
                    make(k)
                    if k >= 2:
                        low(k - 2)
                low(KT - 2)
                low(KT - 1)

            def norm(n, e):
                dve.wait_ge(S("rt_ready"), n + 1)
                link(V.reciprocal(rstd[:, :], rstd[:, :]))
                v0 = [V_MIX, V_FFN, V_MIX + KT, V_FFN + KT][n]

                def make(k):
                    if n in (0, 2) and k >= 4:
                        dve.wait_ge(S("tail_read"), (n // 2) * KT + k - 3)
                    V.scalar_tensor_tensor(ntmp[:, k % 4, :], h[:, k, :], vec[:, v0 + k:v0 + k + 1], rstd[:, :],
                                           ALU.mult, ALU.mult).then_inc(S("n_ready"), 1)
                lo_tiles(e, make)

            def v_tokens(r):
                for n in range(16):
                    dve.wait_ge(S("vt_ab"), 16 * r + n + 1)
                    V.tensor_copy(v_tok[0:META, 0, n * P:(n + 1) * P], pm[n % 4][0:META, 2 * P:3 * P]).then_inc(S("vt_m"), 1)

            dve.wait_ge(S("par_evac"), 3)
            norm(0, 0)
            gemm(G["ab_in"])

            v_tokens(0)
            for u in range(NA_HEADS):
                b = u % 2
                dve.wait_ge(S("qk_rt"), u + 1)
                link(V.reciprocal(rt2[:, b, :, :], rt2[:, b, :, :]))
                for o, i in ((q_rev[:, u, 0:META], slice(0, META)),
                             (q_rev[:, u, META:T].rearrange("p (a b) -> p a b", b=P)[:, :, ::-1], slice(META, T))):
                    q_, r_ = proj[:, u, i], rt2[:, b, 0, i]
                    if i.stop == T:
                        q_, r_ = (v.rearrange("p (a b) -> p a b", b=P) for v in (q_, r_))
                    V.scalar_tensor_tensor(o, q_, vec[:, V_QG:V_QG + 1], r_, ALU.mult, ALU.mult)
                V.scalar_tensor_tensor(proj[:, 8 + u, :], proj[:, 8 + u, :], vec[:, V_KG:V_KG + 1], rt2[:, b, 1, :],
                                       ALU.mult, ALU.mult).then_inc(S("qk_ready"), 1)
            dve.wait_ge(S("nm_scores"), 1)
            s3 = pm[3][0:META, 0:P].rearrange("p (h q) -> p h q", q=META)
            link(V.tensor_scalar(na_m[:, :, :], s3, NA_SCALE, None, ALU.mult))
            mx = col[0:META, 8:16]
            link(V.tensor_reduce(mx, na_m[:, :, :], AX.X, ALU.max))
            V.tensor_tensor(na_m[:, :, :], na_m[:, :, :], bcast(mx, META, 2), ALU.subtract).then_inc(S("nm_max"), 1)
            dve.wait_ge(S("nm_exp"), 1)
            link(V.tensor_reduce(mx, na_m[:, :, :], AX.X, ALU.add))
            link(V.reciprocal(mx, mx))
            V.tensor_tensor(na_m[:, :, :], na_m[:, :, :], bcast(mx, META, 2), ALU.mult).then_inc(S("nm_norm"), 1)
            V.memset(pt[:, :, :, 0:META], 0.0)

            def soft_a(n):
                dve.wait_ge(S("na_scores"), n + 1)
                dve.wait_ge(S("bias_ready"), n + 1)
                if n >= 2:
                    dve.wait_ge(S("na_exp"), n - 1)
                ins = V.scalar_tensor_tensor(na_s[:, n % 2, :], pm[n % 2][:, 0:T], NA_SCALE, bias[:, n % 3, :],
                                             ALU.mult, ALU.add)
                ins.then_inc(S("na_biased"), 1)
                dve.wait_ge(S("na_biased"), n + 1)
                V.tensor_reduce(col[:, n % 2:n % 2 + 1], na_s[:, n % 2, :], AX.X, ALU.max, negate=True).then_inc(S("na_max"), 1)

            def soft_b(n):
                dve.wait_ge(S("na_exp"), n + 1)
                c = col[:, 4 + n % 2:5 + n % 2]
                link(V.reciprocal(c, col[:, 2 + n % 2:3 + n % 2]))
                V.tensor_scalar(na_p[:, n % 2, :], na_p[:, n % 2, :], c, None, ALU.mult).then_inc(S("na_norm"), 1)

            N = 2 * NA_HEADS
            soft_a(0)
            for n in range(N):
                if n + 1 < N:
                    soft_a(n + 1)
                soft_b(n)

            dve.wait_ge(S("ml_ln"), 1)
            ig, fg, l_, B, c_, M = (rows[:, j, :, :] for j in range(6))
            lf = rows[:, 6, :, :]
            link(V.scalar_tensor_tensor(lf, fg, 0.0, l_, ALU.min, ALU.subtract))
            one = bass.AP(ones, 0, [[P, ML_HEADS], [0, T]])

            def turn(ap, d):
                return ap[:, d, ::-1] if d else ap[:, d, :]
            V.tensor_tensor_scan(turn(B, 0), one, turn(lf, 0), 0.0, ALU.mult, ALU.add)
            link(V.tensor_tensor_scan(turn(B, 1), one, turn(lf, 1), 0.0, ALU.mult, ALU.add))
            link(V.tensor_tensor(c_, ig, B, ALU.subtract))
            V.tensor_tensor_scan(turn(M, 0), one, turn(c_, 0), 0.0, ALU.mult, ALU.max)
            link(V.tensor_tensor_scan(turn(M, 1), one, turn(c_, 1), 0.0, ALU.mult, ALU.max))
            link(V.scalar_tensor_tensor(l_, B, -1.0, M, ALU.mult, ALU.subtract))
            V.tensor_scalar(M, M, -1.0, None, ALU.mult).then_inc(S("ml_nm"), 1)
            dve.wait_ge(S("ml_colc"), 1)
            dve.wait_ge(S("mask_done"), 6)

            def mix_x(u):
                hd, tt = u // 3, u % 3
                tn = TILES[tt][1]
                dve.wait_ge(S("ml_cb"), hd + 1)
                for d in range(2):
                    ins = V.scalar_tensor_tensor(ml_x[0:tn, u % 2, d, :], pm[d][0:tn, 0:T], cols[0:tn, tt, d, 0, hd:hd + 1],
                                                 negmask[0:tn, tt, d, :], ALU.add, ALU.min)
                ins.then_inc(S("ml_x_done"), 1)

            def mix_p(u):
                hd, tt = u // 3, u % 3
                tn = TILES[tt][1]
                dve.wait_ge(S("ml_scores"), u + 1)
                dve.wait_ge(S("ml_w_done"), u + 1)
                if u >= 1:
                    dve.wait_ge(S("ml_pn"), u)
                for d in range(2):
                    ins = V.scalar_tensor_tensor(ml_p[0:tn, d, :], pm[2][0:tn, 0:T], ML_SCALE, ml_x[0:tn, u % 2, d, :],
                                                 ALU.mult, ALU.mult, accum_out=den[0:tn, d:d + 1])
                ins.then_inc(S("ml_used"), 1)
                dve.wait_ge(S("ml_used"), u + 1)
                link(V.scalar_tensor_tensor(den[0:tn, 2:4], den[0:tn, 0:2], -1.0, den[0:tn, 0:2], ALU.mult, ALU.max))
                link(V.tensor_tensor(den[0:tn, 2:4], den[0:tn, 2:4], cols[0:tn, tt, :, 1, hd], ALU.max))
                link(V.reciprocal(den[0:tn, 4:6], den[0:tn, 2:4]))
                if u >= 1:
                    dve.wait_ge(S("ml_ptdone"), u)
                link(V.tensor_scalar(ml_pt[0:tn, :], ml_p[0:tn, 0, :], den[0:tn, 4:5], None, ALU.mult))
                V.scalar_tensor_tensor(ml_pt[0:tn, :], ml_p[0:tn, 1, :], den[0:tn, 5:6], ml_pt[0:tn, :],
                                       ALU.mult, ALU.add).then_inc(S("ml_pn"), 1)

            for hd in range(4):
                mix_x(3 * hd)
                for tt in range(3):
                    u = 3 * hd + tt
                    if tt < 2:
                        mix_x(u + 1)
                    mix_p(u)
            dve.wait_ge(S("po_rt"), 1)
            link(V.reciprocal(e_rr[:, :, :], e_rr[:, :, :]))
            dve.wait_ge(S("po_gate"), 1)

            def make_even(k):
                o = ntmp[:, k % 4, :]
                if k < 8:
                    V.tensor_copy(o, y_raw[:, k, :]).then_inc(S("n_ready"), 1)
                    return
                link(V.scalar_tensor_tensor(o, y_raw[:, k, :], vec[:, V_ML + k - 8:V_ML + k - 7], e_rr[:, (k - 8) // 2, :],
                                            ALU.mult, ALU.mult))
                V.tensor_tensor(o, o, proj[:, 32 + k, :], ALU.mult).then_inc(S("n_ready"), 1)
            lo_tiles(1, make_even)
            gemm(G["ab_out"])
            norm(1, 2)
            for part in range(3):
                gemm(G[f"up0{part}"])
                gemm(G[f"down0{part}"])
            norm(2, 3)
            gemm(G["c_in"])

            dve.wait_ge(S("vt_done"), 17)
            V.memset(gup[:, :, :], 0.0).then_inc(S("gup_in"), 1)
            v_tokens(1)
            for j in range(2):
                dve.wait_ge(S("gu_ln"), j + 1)
                link(V.scalar_tensor_tensor(bc[:, j, :, :].rearrange("p k t -> p (k t)"), bc[:, j, :, :].rearrange("p k t -> p (k t)"),
                                            0.0, ge[:, :, :].rearrange("p k t -> p (k t)"), ALU.min, ALU.subtract))
                onesT = bass.AP(ones, 0, [[P, P], [0, T]])
                for k in range(8):
                    v = turn(bc[:, :, k, :], j)
                    ins = V.tensor_tensor_scan(v, onesT, v, 0.0, ALU.mult, ALU.add)
                ins.then_inc(S("b_done"), 1)
            dve.wait_ge(S("b_done"), 2)
            dve.wait_ge(S("q_scaled"), 1)

            def sub(u):
                hd, d, l = units[u]
                if u >= 2:
                    dve.wait_ge(S("gl_pmul"), u - 1)
                    dve.wait_ge(S("gl_dmul"), u - 1)
                for o, b, r, _ in level_views(hd, d, l, "q", u):
                    last = V.tensor_tensor(o, b, r, ALU.subtract)
                last.then_inc(S("gl_dsub"), 1)

            def mul(u):
                hd, d, l = units[u]
                if u >= 2:
                    dve.wait_ge(S("gl_g"), u - 1)
                dve.wait_ge(S("gl_exp"), u + 1)
                for o, xo, s in level_muls(hd, d, l, "q", u):
                    last = V.tensor_tensor(xo, o, s, ALU.mult)
                last.then_inc(S("gl_dmul"), 1)

            def take(u):
                hd, d, l = units[u]
                kind, H = LEVELS[l]
                b, s = pm[u % 2], hd % 2
                dve.wait_ge(S("gl_g"), u + 1)
                dve.wait_ge(S("gl_at"), hd + 1)
                if u >= 1:
                    dve.wait_ge(S("gl_cp"), u)
                if kind == "in":
                    mk = lmask[:, d, l, :].bitcast(U16)
                    if H <= 8:
                        V.copy_predicated(at_m[:, s, 0:META], mk[0:META, 0:META], b[0:META, 2 * P:2 * P + META])
                    o = strided(at_t[:, s, 0, META:META + P], [[T + P, 2], [1, P]])
                    ins = V.copy_predicated(o, bcast(mk, 2), strided(b, [[P, 2], [1, P]]))
                elif H == META:
                    if d == 0:
                        ins = V.tensor_copy(at_m[:, s, META:META + P], b[0:META, 0:P])
                    else:
                        ins = V.tensor_copy(at_t[:, s, 0, 0:META], b[:, 0:META])
                elif d == 0:
                    V.tensor_copy(at_m[:, s, META + P:T], b[0:META, 0:P])
                    ins = V.tensor_copy(at_t[:, s, 0, META + P:T], b[:, P:2 * P])
                else:
                    ins = V.tensor_copy(at_t[:, s, 1, 0:META + P], b[:, 0:META + P])
                ins.then_inc(S("gl_cp"), 1)

            dve.wait_ge(S("lmask_done"), 14)

            def start_head(hd):
                dve.wait_ge(S("gl_diag"), hd + 1)
                s = hd % 2
                if hd >= 2:
                    dve.wait_ge(S("gl_pv"), 4 * (hd - 1))
                V.scalar_tensor_tensor(at_m[:, s, 0:META], pm[3][0:META, 2 * P:2 * P + META], 2.0, ident[0:META, 0:META],
                                       ALU.mult, ALU.mult)
                o = strided(at_t[:, s, 0, META:META + P], [[T + P, 2], [1, P]])
                V.scalar_tensor_tensor(o, strided(pm[3], [[P, 2], [1, P]]), 2.0, bcast(ident[:, :], 2),
                                       ALU.mult, ALU.mult).then_inc(S("gl_at"), 1)

            U = len(units)
            sub(0)
            for u in range(U):
                if u + 1 < U:
                    sub(u + 1)
                mul(u)
                if u >= 1:
                    take(u - 1)
                if u % (2 * NL) == 0:
                    start_head(units[u][0])
            take(U - 1)
            dve.wait_ge(S("po_rt"), 2)
            link(V.reciprocal(o_rr[:, :, :], o_rr[:, :, :]))
            dve.wait_ge(S("po_gate"), 2)

            def make_odd(k):
                o = ntmp[:, k % 4, :]
                link(V.scalar_tensor_tensor(o, y_raw[:, k, :], vec[:, V_GLA + k:V_GLA + k + 1], o_rr[:, k // 4, :],
                                            ALU.mult, ALU.mult))
                V.tensor_tensor(o, o, proj[:, 32 + k, :], ALU.mult).then_inc(S("n_ready"), 1)
            lo_tiles(4, make_odd)
            gemm(G["c_out"])
            norm(3, 5)
            for part in range(3):
                gemm(G[f"up1{part}"])
                gemm(G[f"down1{part}"])

        @block.tensor
        def _(pe):
            mm = nc.tensor.matmul
            tr = nc.tensor.transpose

            def gemm(g, e):
                mid = g.get("mid")
                xh, xl = (g_hi, g_lo) if mid else (act_hi, act_lo)
                kc = g["kc"]
                if not mid:
                    pe.wait_ge(S("act_ready"), KT * e)
                else:
                    pe.wait_ge(S("mid_split"), g["c_end"])
                with pe.Fori(0, g["iters"]) as i:
                    n = i + g["it0"]
                    for grp in range(2):
                        pe.wait_ge(S("bank_free"), n * 2 + (grp + 1))
                        for c in range(2):
                            for m in range(2):
                                s = 4 * grp + 2 * c + m
                                pe.wait_ge(S("split_done"), n * 8 + (s + 1))
                                o = ps[:, 2 * grp + m, 0:T]
                                for k in range(kc):
                                    kk = c * kc + k
                                    wh = w_hi[:, s % 4, k * P:(k + 1) * P]
                                    wl = w_lo[:, s % 4, k * P:(k + 1) * P]
                                    end = c == 1 and k == kc - 1
                                    mm(o, wh, xh[:, kk, :], start=(c == 0 and k == 0), stop=False)
                                    mm(o, wh, xl[:, kk, :], start=False, stop=False)
                                    ins = mm(o, wl, xh[:, kk, :], start=False, stop=end)
                                ins.then_inc(S("used"), 1)

            def norm(n):
                for k in range(KT):
                    pe.wait_ge(S("sq_ready"), 4 * n + k // 4 + 1)
                    ins = mm(pm[0][:, 0:T], ones[:, :], sq[:, k, :], start=(k == 0), stop=(k == KT - 1))
                ins.then_inc(S("ss_ready"), 1)
                if n in (0, 2):
                    e = [0, None, 3][n]
                    o, w = (0, GATES) if n == 0 else (GATES, LRS)
                    if n == 0:
                        pe.wait_ge(S("tail_in"), 48)
                    for k in range(KT):
                        pe.wait_ge(S("n_ready"), e * KT + k + 1)
                        mm(pm[1][0:w, 0:T], tail_w[:, k, o:o + w], ntmp[:, k % 4, :], start=(k == 0),
                           stop=(k == KT - 1)).then_inc(S("tail_read"), 1)
                    pe.wait_ge(S("tail_read"), (n // 2 + 1) * KT)
                    pe.sem_inc(S("tail_done"), 1)

            def v_tokens(r, tiles):
                for n, vt in enumerate(tiles):
                    if n >= 4:
                        pe.wait_ge(S("vt_m"), 16 * r + n - 3)
                    b = pm[n % 4]
                    tr(b[0:META, 2 * P:3 * P], proj[:, vt, 0:META], ident[:, :])
                    tr(b[:, 0:P], proj[:, vt, META:META + P], ident[:, :])
                    tr(b[:, P:2 * P], proj[:, vt, META + P:T], ident[:, :]).then_inc(S("vt_done"), 1)

            def weigh(o, v0, ptt, ptm):
                mm(o, v_tok[0:META, 0, v0:v0 + P], ptm, start=True, stop=False)
                mm(o, v_tok[:, 1, v0:v0 + P], ptt[:, 0, :], start=False, stop=False)
                return mm(o, v_tok[:, 2, v0:v0 + P], ptt[:, 1, :], start=False, stop=True)

            pe.wait_ge(S("const_done"), 3)
            pe.wait_ge(S("param_in"), 16 * 15)
            for j in range(5):
                ins = tr(pm[0][:, 88 * j:88 * (j + 1)], stage[0:88, j, :], ident[0:88, 0:88])
            ins.then_inc(S("par_done"), 1)
            for j in range(5, 8):
                tr(pm[1][:, 88 * (j - 5):88 * (j - 4)], stage[0:88, j, :], ident[0:88, 0:88])
            tr(pm[1][:, 264:264 + V_N], stage[0:V_N, 8, :], ident[0:V_N, 0:V_N]).then_inc(S("par_done"), 1)
            pe.wait_ge(S("tok_in"), 48)
            for k in range(KT):
                if k >= 4:
                    pe.wait_ge(S("h_built"), k // 2 - 1)
                for tt, (t0, tn) in enumerate(TILES):
                    ins = tr(ps[:, k % 4, t0:t0 + tn], tok[0:tn, tt, k * P:(k + 1) * P], ident[0:tn, 0:tn])
                ins.then_inc(S("xT_done"), 1)
            pe.wait_ge(S("par_evac"), 3)
            norm(0)
            gemm(G["ab_in"], 1)

            pe.wait_ge(S("bank_free"), 2 + 2 * G["ab_out"]["it0"])
            pe.wait_ge(S("tail_evac"), 1)
            v_tokens(0, E_V)
            pe.wait_ge(S("vt_m"), 16)
            for u in range(NA_HEADS):
                pe.wait_ge(S("qk_sq"), u + 1)
                if u >= 2:
                    pe.wait_ge(S("qk_rt"), u - 1)
                for j in range(2):
                    ins = mm(pm[2 * (u % 2) + j][:, 0:T], ones[:, :], sq2[:, u % 2, j, :], start=True, stop=True)
                ins.then_inc(S("qk_ss"), 1)
            pe.wait_ge(S("qk_ready"), NA_HEADS)
            for hd in range(NA_HEADS):
                ins = mm(pm[3][0:META, META * hd:META * (hd + 1)], q_rev[:, hd, 0:META], proj[:, 8 + hd, 0:META], start=True, stop=True)
            ins.then_inc(S("nm_scores"), 1)
            pe.wait_ge(S("nm_norm"), 1)
            for hd in range(NA_HEADS):
                ins = tr(pm[3][0:META, P + META * hd:P + META * (hd + 1)], na_m[:, hd, :], ident[0:META, 0:META])
            ins.then_inc(S("nm_ptdone"), 1)

            def scores(n):
                hd, qt = n // 2, n % 2
                t0 = TILES[1 + qt][0]
                if n >= 2:
                    pe.wait_ge(S("na_biased"), n - 1)
                mm(pm[n % 2][:, 0:T], q_rev[:, hd, t0:t0 + P], proj[:, 8 + hd, :], start=True, stop=True).then_inc(S("na_scores"), 1)

            N = 2 * NA_HEADS
            scores(0)
            for n in range(N):
                hd, qt = n // 2, n % 2
                if n + 1 < N:
                    scores(n + 1)
                pe.wait_ge(S("na_norm"), n + 1)
                if n >= 1:
                    pe.wait_ge(S("na_ptcopied"), n)
                b = pm[2]
                tr(b[0:META, 2 * P:3 * P], na_p[:, n % 2, 0:META], ident[:, :])
                tr(b[:, 0:P], na_p[:, n % 2, META:META + P], ident[:, :])
                tr(b[:, P:2 * P], na_p[:, n % 2, META + P:T], ident[:, :]).then_inc(S("na_ptdone"), 1)
                if qt == 1:
                    pe.wait_ge(S("na_ptcopied"), n + 1)
                    pe.wait_ge(S("nm_ptcopied"), 1)
                    if hd >= 1:
                        pe.wait_ge(S("na_stored"), hd)
                    weigh(pm[3][:, 0:T], hd * P, pt[:, hd % 2], pt_m[:, hd % 2, :]).then_inc(S("na_pv"), 1)
            pe.wait_ge(S("na_stored"), NA_HEADS)
            for j in range(4):
                ins = mm(pm[j][0:ML_HEADS, 0:T], ident[0:GATES, 4 * j:4 * j + 4], tail[0:GATES, :], start=True, stop=True)
            ins.then_inc(S("ml_sel"), 1)
            pe.wait_ge(S("ml_nm"), 1)
            pe.wait_ge(S("ml_en"), 1)
            for tt, (t0, tn) in enumerate(TILES):
                for d in range(2):
                    for q, row in enumerate((5, 6)):
                        o = ((tt * 2 + d) * 2 + q) * 4
                        ins = mm(pm[0][0:tn, o:o + 4], rows[:, row, d, t0:t0 + tn], ident[0:4, 0:4], start=True, stop=True)
            ins.then_inc(S("ml_cols"), 1)
            pe.wait_ge(S("ml_colc"), 1)
            pe.wait_ge(S("sel_done"), 1)

            def ml_t(u):
                hd, tt = u // 3, u % 3
                tn = TILES[tt][1]
                pe.wait_ge(S("ml_pn"), u + 1)
                if u >= 1:
                    pe.wait_ge(S("ml_ptcopied"), u)
                b = pm[3]
                tr(b[0:META, 2 * P:2 * P + tn], ml_pt[0:tn, 0:META], ident[0:tn, 0:tn])
                tr(b[:, 0:tn], ml_pt[0:tn, META:META + P], ident[0:tn, 0:tn])
                tr(b[:, P:P + tn], ml_pt[0:tn, META + P:T], ident[0:tn, 0:tn]).then_inc(S("ml_ptdone"), 1)

            for hd in range(4):
                if hd >= 1:
                    pe.wait_ge(S("ml_stored"), hd)
                for d in range(2):
                    ins = mm(pm[d][:, 0:T], selrow[:, hd, :], rows[:, 4, d, :], start=True, stop=True)
                ins.then_inc(S("ml_cb"), 1)
                for tt, (t0, tn) in enumerate(TILES):
                    u = 3 * hd + tt
                    if u >= 1:
                        pe.wait_ge(S("ml_used"), u)
                    mm(pm[2][0:tn, 0:T], proj[:, 24 + hd, t0:t0 + tn], proj[:, 28 + hd, :], start=True, stop=True).then_inc(S("ml_scores"), 1)
                    if tt >= 1:
                        ml_t(u - 1)
                ml_t(3 * hd + 2)
                pe.wait_ge(S("ml_ptcopied"), 3 * hd + 3)
                for e in range(2):
                    ins = weigh(pm[e][:, 0:T], 1024 + hd * 256 + e * P, pt[:, hd % 2], pt_m[:, hd % 2, :])
                ins.then_inc(S("ml_pv"), 1)
            pe.wait_ge(S("ml_stored"), 4)
            for hd in range(4):
                pe.wait_ge(S("po_sq"), hd + 1)
                for j in range(2):
                    ins = mm(pm[hd][:, 0:T], ones[:, :], e_sq[:, hd % 2, j, :], start=(j == 0), stop=(j == 1))
                ins.then_inc(S("po_ss"), 1)
            gemm(G["ab_out"], 2)
            pe.wait_ge(S("po_rt"), 1)
            norm(1)
            for part in range(3):
                gemm(G[f"up0{part}"], 3)
                gemm(G[f"down0{part}"], 3)
            norm(2)
            gemm(G["c_in"], 4)

            pe.wait_ge(S("bank_free"), 2 + 2 * G["c_out"]["it0"])
            pe.wait_ge(S("tail_evac"), 2)
            v_tokens(1, O_V)
            pe.wait_ge(S("vt_m"), 32)
            pe.wait_ge(S("gup_in"), 33)
            for n in range(16):
                if n >= 4:
                    pe.wait_ge(S("gu_x"), n - 3)
                j, k = n // 8, n % 8
                mm(pm[n % 4][:, 0:T], gup[:, j, k * P:(k + 1) * P], tail[:, :], start=True, stop=True).then_inc(S("gu_mm"), 1)
            pe.wait_ge(S("gu_x"), 16)
            pe.wait_ge(S("q_scaled"), 1)

            def gram(o, l0, ln, r0, rn, L, R):
                for j in range(2):
                    ins = mm(o, L[:, j, l0:l0 + ln], R[:, j, r0:r0 + rn], start=(j == 0), stop=(j == 1))
                return ins

            def diag(hd):
                if hd >= 2:
                    pe.wait_ge(S("gl_stored"), 4 * (hd - 1))
                q_, k_ = proj[:, 2 * hd:2 * hd + 2, :], proj[:, 8 + 2 * hd:10 + 2 * hd, :]
                gram(pm[3][0:META, 2 * P:2 * P + META], 0, META, 0, META, k_, q_)
                gram(pm[3][:, 0:P], META, P, META, P, k_, q_)
                gram(pm[3][:, P:2 * P], META + P, P, META + P, P, k_, q_).then_inc(S("gl_diag"), 1)

            def weigh_head(hd):
                pe.wait_ge(S("gl_cp"), 2 * NL * (hd + 1))
                if hd < GLA_HEADS - 1:
                    pe.wait_ge(S("gl_at"), hd + 2)
                for e in range(4):
                    n = 4 * hd + e
                    if n >= 2:
                        pe.wait_ge(S("gl_stored"), n - 1)
                    weigh(pm[2 + n % 2][:, 0:T], n * P, at_t[:, hd % 2], at_m[:, hd % 2, :]).then_inc(S("gl_pv"), 1)

            for u, (hd, d, l) in enumerate(units):
                if u % (2 * NL) == 0:
                    diag(hd)
                if u >= 2:
                    pe.wait_ge(S("gl_cp"), u - 1)
                pe.wait_ge(S("gl_dmul"), u + 1)
                pe.wait_ge(S("gl_pmul"), u + 1)
                X, b = gl_x[:, u % 2], pm[u % 2]
                kind, H = LEVELS[l]
                if kind == "in":
                    if H <= 8:
                        gram(b[0:META, 2 * P:2 * P + META], 0, META, 0, META, X, X)
                    gram(b[:, 0:P], META, P, META, P, X, X)
                    ins = gram(b[:, P:2 * P], META + P, P, META + P, P, X, X)
                elif H == META:
                    ins = gram(b[0:META, 0:P], 0, META, META, P, X, X) if d == 0 else gram(b[:, 0:META], META, P, 0, META, X, X)
                elif d == 0:
                    gram(b[0:META, 0:P], 0, META, META + P, P, X, X)
                    ins = gram(b[:, P:2 * P], META, P, META + P, P, X, X)
                else:
                    ins = gram(b[:, 0:META + P], META + P, P, 0, META + P, X, X)
                ins.then_inc(S("gl_g"), 1)
                if u % (2 * NL) == 4 and hd >= 1:
                    weigh_head(hd - 1)
            weigh_head(3)
            pe.wait_ge(S("gl_stored"), 16)
            for hd in range(4):
                pe.wait_ge(S("po_sq"), 4 + hd + 1)
                for j in range(4):
                    ins = mm(pm[hd][:, 0:T], ones[:, :], o_sq[:, 4 * hd + j, :], start=(j == 0), stop=(j == 3))
                ins.then_inc(S("po_ss"), 1)
            gemm(G["c_out"], 5)
            pe.wait_ge(S("po_rt"), 2)
            norm(3)
            for part in range(3):
                gemm(G[f"up1{part}"], 6)
                gemm(G[f"down1{part}"], 6)
            pe.wait_ge(S("bank_free"), 2 + 2 * state["it"])
            for b in range(2):
                t0 = TILES[1 + b][0]
                for q in range(4):
                    n = 4 * b + q
                    if n >= 4:
                        pe.wait_ge(S("out_evac"), n - 3)
                    for j in range(4):
                        ins = tr(pm[n % 4][:, j * P:(j + 1) * P], h[:, 4 * q + j, t0:t0 + P], ident[:, :])
                    ins.then_inc(S("out_done"), 1)


_INS = ["x", "meta_tokens", "norm_mix", "norm_ffn", "ab_w_in", "ab_gate_bias", "ab_q_gain", "ab_k_gain",
        "ab_rel_bias", "ab_ml_gain", "ab_w_out", "c_w_in", "c_gate_up", "c_gate_bias", "c_head_gain",
        "c_w_out", "ffn_w_up", "ffn_conv_w", "ffn_conv_b", "ffn_w_down"]


def kernel(**inputs):
    import numpy as _np
    import concourse.bacc as _bacc
    from concourse import mybir as _mybir
    from concourse.bass_utils import run_bass_kernel_spmd as _run

    nc = _bacc.Bacc("TRN2", target_bir_lowering=False, num_devices=1)
    arrays, args = {}, []
    for name in _INS:
        v = _np.ascontiguousarray(inputs[name])
        arrays[f"in_{name}"] = v
        args.append(nc.dram_tensor(f"in_{name}", v.shape, _mybir.dt.from_np(v.dtype), kind="ExternalInput").ap())
    args.append(nc.dram_tensor("out_y", (1, SEQ, D), _mybir.dt.float32, kind="ExternalOutput").ap())
    build(nc, *args)
    r = _run(nc, [arrays], core_ids=[0])
    return r.results[0]["out_y"]
```

```python
import numpy as np

import concourse.bass as bass
from concourse import mybir
from contextlib import ExitStack

F32 = mybir.dt.float32
F32R = mybir.dt.float32r
BF16 = mybir.dt.bfloat16
U16 = mybir.dt.uint16
ALU = mybir.AluOpType
ACT = mybir.ActivationFunctionType
AX = mybir.AxisListType

P = 128
D = 2048
KT = D // P
SEQ, META = 256, 16
T = SEQ + META
TILES = [(0, META), (META, P), (META + P, P)]
EPS = 1e-6
GRID_W, WIN_W, WIN_H, ROWS = 64, 16, 8, SEQ // 64
NA_HEADS, ML_HEADS, GLA_HEADS = 8, 4, 4
NA_SCALE = 128 ** -0.5
ML_SCALE = 128 ** -0.5
GLA_SCALE = 256 ** -0.5
GLA_TAU = 16.0
D_FF = 5632
FT = D_FF // P
PARTS = [16, 14, 14]
RANK = 16
NEG = -1.0e30
AB_COLS, C_COLS = 48 * P, 48 * P
GATES, LRS = 16, 2 * RANK

V_MIX, V_FFN, V_ML, V_GLA, V_QG, V_KG, V_GB = 0, 32, 64, 72, 88, 89, 90
V_N = 106

LEVELS = [("in", H) for H in (1, 2, 4, 8, 16, 32, 64)] + [("edge", META), ("edge", META + P)]
NL = len(LEVELS)


class Chain:

    def __init__(self, eng, sem):
        self.eng, self.sem, self.n, self.off = eng, sem, 0, 0

    def link(self, ins):
        ins.then_inc(self.sem, 1)
        self.n += 1
        self.eng.wait_ge(self.sem, self.off + self.n)

    def enter(self, rounds_before, per):
        self.off = rounds_before * per if per else 0

    def leave(self, rounds, per):
        self.off = 0
        self.n += (rounds - 1) * per


def build(nc, x, meta_tokens, norm_mix, norm_ffn, ab_w_in, ab_gate_bias, ab_q_gain, ab_k_gain,
          ab_rel_bias, ab_ml_gain, ab_w_out, c_w_in, c_gate_up, c_gate_bias, c_head_gain, c_w_out,
          ffn_w_up, ffn_conv_w, ffn_conv_b, ffn_w_down, out):
    gemms = []
    state = {"it": 0, "gr": 0}

    def add(name, w, ks, iters, evac, row0=0, col0=0, x0=0, t0=0, **kw):
        ng = 8 // len(ks)
        gemms.append(dict(name=name, w=w, row0=row0, ks=ks, ng=ng, gs=len(ks), iters=iters, col0=col0, evac=evac,
                          x0=x0, t0=t0, it0=state["it"], gr0=state["gr"], **kw))
        state["it"] += iters
        state["gr"] += iters * ng

    full, half = [4, 4, 4, 4], [4, 4]
    add("ml_in", ab_w_in[0], full, 6, "store", col0=24 * P, p0=24, ready=0)
    add("na_in", ab_w_in[0], full, 6, "store", p0=0, ready=0)
    add("ml_out", ab_w_out[0], half, 2, "resid", row0=8, x0=8, ready=16)
    add("na_out", ab_w_out[0], half, 2, "resid", ready=24)

    def ffn(layer, ready, up_t0, down_t0):
        f0 = 0
        for part, nt in enumerate(PARTS):
            add(f"up{layer}{part}", ffn_w_up[layer], full, nt // 2, "conv", col0=f0 * P, t0=up_t0,
                layer=layer, f0=f0, ready=ready)
            add(f"down{layer}{part}", ffn_w_down[layer], full if nt == 16 else [4, 4, 3, 3], 4, "resid",
                row0=f0, t0=down_t0, mid=True)
            f0 += nt

    ffn(0, 32, 0, 0)
    add("qk_in", c_w_in[0], full, 4, "store", p0=0, ready=48)
    add("vr_in", c_w_in[0], full, 8, "store", col0=16 * P, p0=16, ready=48, v_groups=8)
    add("gl_out", c_w_out[0], full, 4, "resid", ready=64, t0=META - 2)
    ffn(1, 80, META - 2, META)
    G = {g["name"]: g for g in gemms}
    conv_it = 0
    for g in gemms:
        g["c0"] = conv_it
        if g["evac"] == "conv":
            conv_it += g["iters"]
    for g, before in zip(gemms[1:], gemms):
        if g.get("mid"):
            g["c0"] = before["c0"]
    for a, b in zip(gemms, gemms[1:] + [None]):
        a["next"] = b

    ctx = ExitStack()
    with ctx:
        place = {"at": 16512}

        def sb(name, shape, dt=F32, at=None):
            size = int(np.prod(shape[1:])) * (2 if dt in (BF16, U16) else 4)
            if at is None:
                at = place["at"]
                place["at"] = (at + size + 31) // 32 * 32
            assert at + size <= 229344, (name, at, size)
            return nc.alloc_sbuf_tensor_at(name, shape, dt, offset=at)

        h = sb("h", [P, KT, T])
        act_hi = sb("act_hi", [P, KT, T], F32R)
        act_lo = sb("act_lo", [P, KT, T], F32R)
        raw = sb("raw", [P, 4, 4 * 256])
        w_hi = sb("w_hi", [P, 4, 4 * 256], F32R)
        w_lo = sb("w_lo", [P, 4, 4 * 256], F32R)
        ident = sb("ident", [P, P])
        ones = sb("ones", [P, P])
        vec = sb("vec", [P, V_N])
        conv = sb("conv", [P, 2, 4, 2 * FT])
        tail_w = sb("tail_w", [P, KT, GATES + LRS])
        tail = sb("tail", [LRS, T])
        gate_b = sb("gate_b", [GATES, 1])
        eps = sb("eps", [P, 1])
        ntmp = sb("ntmp", [P, 4, T])
        rstd = sb("rstd", [P, T])
        zone = place["at"]
        TB = T * 4
        proj = sb("proj", [P, 48, T], at=zone)
        v_tok = sb("v_tok", [P, 3, D], at=zone + 48 * TB)
        M = zone + 48 * TB + 3 * D * 4
        row_c = sb("row_c", [ML_HEADS, 2, T], at=M)
        row_f = sb("row_f", [ML_HEADS, 2, T], at=M + 2 * TB)
        row_l = sb("row_l", [ML_HEADS, 2, T], at=M + 4 * TB)
        row_b = sb("row_b", [ML_HEADS, 2, T], at=M + 6 * TB)
        row_m = sb("row_m", [ML_HEADS, 2, T], at=M + 8 * TB)
        ml_x = sb("ml_x", [P, 2, T], at=M + 2 * TB)
        ml_p = sb("ml_p", [P, 2, T], at=M + 4 * TB)
        ml_ptt = sb("ml_ptt", [P, 2, T], at=M + 6 * TB)
        ml_ptm = sb("ml_ptm", [META, T], at=M + 8 * TB)
        ml_sum = sb("ml_sum", [P, T], at=M + 9 * TB)
        e_sq = sb("e_sq", [P, 2, 2, T], at=M + 2 * TB)
        e_rr = sb("e_rr", [P, 4, T], at=M + 6 * TB)
        SW = META + 2 * P + P + META
        strip = sb("strip", [P, 2, SW], at=M + 10 * TB)
        selrow = sb("selrow", [ML_HEADS, ML_HEADS, P], at=M + 10 * TB + 2 * SW * 4)
        cols = sb("cols", [P, 3, 2, 2, ML_HEADS], at=M + 10 * TB + 2 * SW * 4 + 2048)
        den = sb("den", [P, 8], at=M + 10 * TB + 2 * SW * 4 + 2048 + 192)
        y_ml = sb("y_ml", [P, 8, T], at=zone + 32 * TB)
        q_rev = sb("q_rev", [P, NA_HEADS, T], at=zone + 24 * TB)
        sq2 = sb("sq2", [P, 2, T], at=zone + 32 * TB)
        rt2 = sb("rt2", [P, 2, T], at=zone + 34 * TB)
        na_s = sb("na_s", [P, 2, T], at=zone + 36 * TB)
        na_p = sb("na_p", [P, 2, T], at=zone + 38 * TB)
        pt = sb("pt", [P, 2, 2, T], at=zone + 40 * TB)
        bias = sb("bias", [P, 4, T], at=zone + 44 * TB)
        pt_m = sb("pt_m", [META, 2, T], at=M + 2 * TB)
        na_m = sb("na_m", [META, NA_HEADS, META], at=M + 4 * TB)
        na_mt = sb("na_mt", [META, NA_HEADS, META], at=M + 5 * TB)
        col = sb("col", [P, 64], at=M)
        winmask = sb("winmask", [P, GRID_W], at=M + 256)
        bc = sb("bc", [P, 2, 8, T], at=zone + 16 * TB)
        gup = sb("gup", [LRS, 2, 8 * P], at=zone + 32 * TB)
        ge = sb("ge", [P, 2, T], at=zone + 40 * TB)
        gl_e = sb("gl_e", [P, 2, 2, T], at=M)
        gl_x = sb("gl_x", [P, 2, 2, T], at=M + 4 * TB)
        at_t = sb("at_t", [P, 2, 2, T], at=M + 8 * TB)
        at_m = sb("at_m", [META, 2, T], at=M + 12 * TB)
        lmask = sb("lmask", [P, 2, 7, P], BF16, at=M + 14 * TB)
        MT = max(PARTS)
        g_hi = sb("g_hi", [P, MT, T], F32R, at=zone)
        g_lo = sb("g_lo", [P, MT, T], F32R, at=zone + MT * TB)
        acc = sb("acc", [P, 2, 2, T], at=zone + 2 * MT * TB)
        sg = sb("sg", [P, 2, T], at=zone + (2 * MT + 4) * TB)
        gp = sb("gp", [P, 2, T], at=zone + (2 * MT + 6) * TB)
        un = sb("un", [P, 2, 2, T], at=zone + (2 * MT + 8) * TB)
        sq = sb("sq", [P, KT, T], at=zone + 48 * TB)
        tok = sb("tok", [P, 3, D], at=zone)
        stage = sb("stage", [P, 9, P], at=zone + 3 * D * 4)
        ostage = sb("ostage", [P, 2, D], at=zone)

        ps = ctx.enter_context(nc.psum_tensor("ps", [P, 8, 512], F32))
        pm = [ps[:, 4 + b, :] for b in range(4)]

        names = {}

        def S(name):
            if name not in names:
                names[name] = ctx.enter_context(nc.semaphore(name))
            return names[name]

        landed = [S(f"weights_landed{j}") for j in range(4)]
        all_sems = """const_done tok_in param_in tail_in gup_in hi_done split_done used bank_free u_ready conv_mid gates_done
            silu_done mid_done mid_split act_chain dve_chain pool_chain xT_done h_built par_done par_evac
            sq_ready sq_added ss_ready rt_ready rs_ready x_hi act_ready n_ready tail_scaled tail_done tail_evac
            vt_done vt_copied vg_stored qk_sq qk_ss qk_rt qk_ready bias_in0 bias_in1 bias_in2 bias_in3 bias_ready
            na_scores na_biased na_max na_exp na_norm na_ptdone na_ptcopied na_pv na_stored mask_done
            nm_scores nm_max nm_exp nm_norm nm_ptdone nm_ptcopied
            ml_sel ml_ln ml_nm ml_en ml_cols ml_colc ml_cb ml_scores ml_x_done ml_w_done ml_pn ml_used
            ml_ptdone ml_ptcopied ml_pv ml_stored ml_made po_sq po_ss po_ssc po_rt po_gate q_scaled
            gu_mm gu_x gu_ln b_done gl_dsub gl_psub gl_exp gl_dmul gl_pmul gl_g gl_cp gl_pv gl_stored
            lmask_done out_done out_evac out_sent sel_done""".split()
        for n in all_sems:
            S(n)

        def bcast(ap, n, at=1):
            dims = [list(v) for v in ap.ap]
            dims.insert(at, [0, n])
            return bass.AP(ap.tensor, ap.offset, dims)

        def strided(ap, dims):
            return bass.AP(ap.tensor, ap.offset, [list(ap.ap[0])] + dims)

        units = []
        for hd in range(GLA_HEADS):
            units.append((hd, None, None))
            units += [(hd, d, l) for d in range(2) for l in range(NL)]
        UH = 1 + 2 * NL
        levels_before = [sum(x[1] is not None for x in units[:u]) for u in range(len(units) + 1)]

        def level_span(l):
            kind, H = LEVELS[l]
            if kind == "in":
                return (0, T) if H <= 8 else (META, T)
            return (0, META + P) if H == META else (0, T)

        def halves(ap, l, d, side):
            kind, H = LEVELS[l]
            t0, t1 = level_span(l)
            right = (side == "q") != (d == 1)
            r = H if d else H - 1
            if kind == "in":
                v = ap[:, :, t0:t1].rearrange("p a (g b) -> p a g b", b=2 * H)
                return (v[:, :, :, H:2 * H] if right else v[:, :, :, 0:H]), v[:, :, :, r:r + 1]
            return (ap[:, :, H:t1] if right else ap[:, :, 0:H]), ap[:, :, r:r + 1]

        def level_sub(u, side):
            hd, d, l = units[u]
            b, ref = halves(bc[:, d, 2 * hd:2 * hd + 2, :], l, d, side)
            o, _ = halves(gl_e[:, levels_before[u] % 2, :, :], l, d, side)
            dims = [list(v) for v in ref.ap]
            dims[-1] = [0, b.shape[-1]]
            return o, b, bass.AP(ref.tensor, ref.offset, dims)

        def level_mul(u, side):
            hd, d, l = units[u]
            v = levels_before[u] % 2
            e, _ = halves(gl_e[:, v, :, :], l, d, side)
            o, _ = halves(gl_x[:, v, :, :], l, d, side)
            base = 2 * hd if side == "q" else 8 + 2 * hd
            s, _ = halves(proj[:, base:base + 2, :], l, d, side)
            return o, e, s

        def o_tile(n):
            hd, e = n // 4, n % 4
            return proj[:, (2 * hd + e) if e < 2 else (8 + 2 * hd + e - 2), :]

        E_ML, E_NA = list(range(32, 40)), list(range(16, 24))

        GL_TICKS = 82
        WEIGH = {}
        for k in range(4):
            WEIGH[34 + k], WEIGH[38 + k], WEIGH[58 + k], WEIGH[77 + k] = k, 4 + k, 8 + k, 12 + k
        SQUARE = {43: 0, 45: 1, 63: 2}

        NORM_V = [V_MIX, V_FFN, V_MIX + KT, V_FFN + KT]
        NORM_READY = [0, 32, 48, 80]
        VT_COL = [1024 + P * n for n in range(8)] + [P * n for n in range(8)] + [P * n for n in range(16)]
        ML_VT = {1: (0, 1), 2: (2, 3), 3: (4,), 4: (5,), 5: (6,), 6: (7,)}

        def advance(side):
            next(side, None)

        def finish(side):
            for _ in side:
                pass

        block = ctx.enter_context(nc.Block())

        @block.sync
        def _(sp):
            sp.dma_start(tok[0:META, 0, :], meta_tokens).then_inc(S("tok_in"), 16)
            for b in range(2):
                sp.dma_start(tok[:, 1 + b, :], x[0, b * P:(b + 1) * P, :]).then_inc(S("tok_in"), 16)

            def load(g, i, first=False):
                n = g["w"].shape[1]
                for s in range(8):
                    grp, c = s // g["gs"], s % g["gs"]
                    kc = g["ks"][c]
                    if not first or s >= 4:
                        sp.wait_ge(S("split_done"), (i + g["it0"]) * 8 + (s - 3))
                    row = (g["row0"] + sum(g["ks"][:c])) * P
                    if g["evac"] == "conv":
                        off, step = g["col0"] + grp * D_FF, 256
                    else:
                        off, step = g["col0"] + grp * 256, g["ng"] * 256
                    src = bass.AP(g["w"].tensor, g["w"].offset + row * n + off + i * step,
                                  [[n, P], [n * P, kc], [1, 256]])
                    dst = raw[:, s % 4, 0:kc * 256].rearrange("p (k c) -> p k c", k=kc)
                    sp.dma_start(dst, src).then_inc(landed[s % 4], 16)

            for g in gemms:
                start = 0
                if g["it0"] == 0:
                    load(g, 0, first=True)
                    start = 1
                with sp.Fori(start, g["iters"]) as i:
                    load(g, i)
            for b in range(2):
                sp.wait_ge(S("out_evac"), 4 * (b + 1))
                sp.dma_start(out[0, b * P:(b + 1) * P, :], ostage[:, b, :]).then_inc(S("out_sent"), 16)
            sp.wait_ge(S("out_sent"), 32)

        @block.gpsimd
        def _(pool):
            chain = Chain(pool, S("pool_chain"))
            g_ = nc.gpsimd
            chain.link(g_.memset(ident[:, :], 0.0))
            g_.affine_select(out=ident[:, :], in_=ident[:, :], compare_op=ALU.not_equal, fill=1.0, base=0,
                             pattern=[[-1, P]], channel_multiplier=1).then_inc(S("const_done"), 1)

            def norm(n):
                pool.wait_ge(S("sq_ready"), 4 * n + 1)
                for q in range(1, 4):
                    pool.wait_ge(S("sq_ready"), 4 * n + q + 1)
                    g_.tensor_tensor(sq[:, 0:4, :], sq[:, 0:4, :], sq[:, 4 * q:4 * q + 4, :], ALU.add).then_inc(S("sq_added"), 1)
                    pool.wait_ge(S("sq_added"), 3 * n + q)

            norm(0)
            pool.wait_ge(S("act_ready"), KT)
            pool.wait_ge(S("ss_ready"), 1)
            chain.link(g_.memset(strip[:, :, :], 0.0))
            for d in range(2):
                sgn = 1 - 2 * d
                g_.affine_select(out=strip[:, d, :], in_=strip[:, d, :], compare_op=ALU.is_ge, fill=NEG,
                                 base=sgn * (META + P), pattern=[[-sgn, SW]],
                                 channel_multiplier=sgn).then_inc(S("mask_done"), 1)
            chain.link(g_.memset(selrow[:, :, :], 0.0))
            g_.affine_select(out=selrow[:, :, :], in_=selrow[:, :, :], compare_op=ALU.not_equal, fill=1.0, base=0,
                             pattern=[[-1, ML_HEADS], [0, P]], channel_multiplier=1).then_inc(S("sel_done"), 1)

            pool.wait_ge(S("act_ready"), 24)
            chain.link(g_.memset(winmask[:, :], 0.0))
            for half_ in range(2):
                w = winmask[64 * half_:64 * half_ + 64, 0:GRID_W - WIN_W]
                chain.link(g_.affine_select(out=w, in_=w, compare_op=ALU.is_ge, fill=NEG,
                                            base=WIN_W // 2 - (GRID_W - 1), pattern=[[1, GRID_W - WIN_W]],
                                            channel_multiplier=1))
                w = winmask[64 * half_:64 * half_ + 64, WIN_W:GRID_W]
                chain.link(g_.affine_select(out=w, in_=w, compare_op=ALU.is_gt, fill=NEG,
                                            base=(GRID_W - 1) + WIN_W // 2 - WIN_W, pattern=[[-1, GRID_W - WIN_W]],
                                            channel_multiplier=-1))
            for b in range(4):
                chain.link(g_.memset(bias[:, b, 0:META], 0.0))
            for n in range(2 * NA_HEADS):
                pool.wait_ge(S(f"bias_in{n % 4}"), 32 * (n // 4 + 1))
                b = bias[:, n % 4, META:T].rearrange("p (r c) -> p r c", r=ROWS)
                g_.tensor_tensor(b, b, bcast(winmask[:, :], ROWS), ALU.add).then_inc(S("bias_ready"), 1)
            norm(1)

            for d in range(2):
                for l in range(7):
                    H = LEVELS[l][1]
                    m = lmask[:, d, l, :]
                    chain.link(g_.memset(m, 0.0))
                    hf = m.rearrange("p (g b) -> p g b", b=2 * H)[:, :, (0 if d else H):(H if d else 2 * H)]
                    lo = H if d else 0
                    chain.link(g_.memset(hf, 1.0))
                    chain.link(g_.affine_select(out=hf, in_=hf, compare_op=ALU.is_ge, fill=0.0, base=-lo,
                                                pattern=[[-2 * H, P // (2 * H)], [0, H]], channel_multiplier=1))
                    g_.affine_select(out=hf, in_=hf, compare_op=ALU.is_ge, fill=0.0, base=lo + H - 1,
                                     pattern=[[2 * H, P // (2 * H)], [0, H]],
                                     channel_multiplier=-1).then_inc(S("lmask_done"), 1)
            norm(2)

            pool.wait_ge(S("b_done"), 8)
            lev = [u for u in range(len(units)) if units[u][1] is not None]

            def sub(v):
                if v >= 2:
                    pool.wait_ge(S("gl_dmul"), v - 1)
                    pool.wait_ge(S("gl_pmul"), v - 1)
                o, b, r = level_sub(lev[v], "k")
                g_.tensor_tensor(o, r, b, ALU.subtract).then_inc(S("gl_psub"), 1)

            sub(0)
            for v, u in enumerate(lev):
                if v + 1 < len(lev):
                    sub(v + 1)
                if v >= 2:
                    pool.wait_ge(S("gl_g"), lev[v - 2] + 1)
                pool.wait_ge(S("gl_exp"), v + 1)
                o, e, k_ = level_mul(u, "k")
                g_.tensor_tensor(o, e, k_, ALU.mult).then_inc(S("gl_pmul"), 1)
            norm(3)

        @block.scalar
        def _(act):
            chain = Chain(act, S("act_chain"))
            A = nc.scalar.activation

            rows_of = [(norm_mix, 32), (norm_ffn, 32), (ab_ml_gain, 8), (c_head_gain, 16),
                       (ab_q_gain, 1), (ab_k_gain, 1), (c_gate_bias, 16)]
            at = 0
            for v, n in rows_of:
                act.dma_start(stage[at:at + n, 8, :], bass.AP(v.tensor, v.offset, [[P, n], [1, P]])).then_inc(S("param_in"), 16)
                at += n
            for layer in range(2):
                for tap in range(4):
                    v = ffn_conv_w[layer, tap] if tap < 3 else ffn_conv_b[layer]
                    act.dma_start(stage[0:2 * FT, 4 * layer + tap, :],
                                  v.rearrange("(m p) -> m p", p=P)).then_inc(S("param_in"), 16)
            act.dma_start(gate_b[:, :], ab_gate_bias.rearrange("a g -> g a")).then_inc(S("tail_in"), 16)
            for w, c0, n, o in ((ab_w_in[0], AB_COLS, GATES, 0), (c_w_in[0], C_COLS, LRS, GATES)):
                act.dma_start(tail_w[:, :, o:o + n], bass.AP(w.tensor, w.offset + c0,
                              [[w.shape[1], P], [w.shape[1] * P, KT], [1, n]])).then_inc(S("tail_in"), 16)

            def hi(g, it, s):
                n = it + g["it0"]
                kc = g["ks"][s % g["gs"]]
                act.wait_ge(landed[s % 4], n * 32 + 16 * (s // 4 + 1))
                act.wait_ge(S("used"), n * 8 + (s - 3))
                A(w_hi[:, s % 4, 0:kc * 256], raw[:, s % 4, 0:kc * 256], ACT.Copy).then_inc(S("hi_done"), 1)

            def evac(g, i, grp):
                if g["evac"] != "conv":
                    return
                c = i + g["c0"]
                o0 = META if g["t0"] else 0
                if grp == 0:
                    act.wait_ge(S("mid_done"), c)
                act.wait_ge(S("u_ready"), c * 2 + (grp + 1))
                for m in range(2):
                    mt = i * 2 + (grp * FT + g["f0"] + m)
                    ins = A(acc[:, grp, m, o0:T], un[:, grp, m, o0:T], ACT.Identity,
                            bias=conv[:, g["layer"], 3, bass.ds(mt, 1)], scale=conv[:, g["layer"], 1, bass.ds(mt, 1)])
                ins.then_inc(S("conv_mid"), 1)
                if grp == 1:
                    act.wait_ge(S("gates_done"), c + 1)
                    A(sg[:, :, o0:T], acc[:, 0, :, o0:T], ACT.Silu).then_inc(S("silu_done"), 1)

            def gemm(g, first=None, beside=None):
                if g["it0"] == 0:
                    for s in range(3):
                        act.wait_ge(landed[s], 16)
                        A(w_hi[:, s, :], raw[:, s, :], ACT.Copy).then_inc(S("hi_done"), 1)

                def body(i, nxt, ni, side=None, late=False):
                    for s in range(8):
                        if s + 3 < 8:
                            hi(g, i, s + 3)
                        elif nxt:
                            hi(nxt, ni, s + 3 - 8)
                        if late:
                            if s >= 6:
                                evac(g, i, s - 6)
                        elif s % g["gs"] == g["gs"] - 1:
                            evac(g, i, s // g["gs"])
                        if side:
                            advance(side)

                last, start = g["iters"] - 1, 0
                if first:
                    body(0, g, 1, first, late=True)
                    finish(first)
                    start = 1
                if beside:
                    for i in range(start, last):
                        body(i, g, i + 1, beside)
                else:
                    with act.Fori(start, last) as i:
                        body(i, g, i + 1)
                body(last, g["next"], 0, beside)
                if beside:
                    finish(beside)

            def norm(n):
                v0, base = NORM_V[n], NORM_READY[n]
                for k in range(KT):
                    A(act_hi[:, k, :], h[:, k, :], ACT.Copy, scale=vec[:, v0 + k:v0 + k + 1]).then_inc(S("x_hi"), 1)

            def norm_side(n):
                for q in range(4):
                    A(sq[:, 4 * q:4 * q + 4, :], h[:, 4 * q:4 * q + 4, :], ACT.Square).then_inc(S("sq_ready"), 1)
                    yield
                yield
                act.wait_ge(S("ss_ready"), n + 1)
                A(rstd[:, :], pm[0][:, 0:T], ACT.Sqrt, bias=eps[:, :], scale=1.0 / D).then_inc(S("rt_ready"), 1)
                yield

            def vt_copy(n, b):
                act.wait_ge(S("vt_done"), n + 1)
                c = VT_COL[n]
                A(v_tok[0:META, 0, c:c + P], pm[b][0:META, 2 * P:3 * P], ACT.Copy)
                A(v_tok[:, 1:3, c:c + P], strided(pm[b], [[P, 2], [1, P]]), ACT.Copy).then_inc(S("vt_copied"), 1)

            def mlstm():
                for t in range(9):
                    if t == 1:
                        act.wait_ge(S("ml_sel"), 1)
                        for j in range(4):
                            ins = A((row_f if j % 2 else row_c)[:, j // 2, :], pm[j][0:ML_HEADS, 0:T], ACT.Copy)
                        chain.link(ins)
                        chain.link(A(row_l[:, :, :], row_f[:, :, :], ACT.Abs))
                        chain.link(A(row_l[:, :, :], row_l[:, :, :], ACT.Exp, scale=-1.0))
                        A(row_l[:, :, :], row_l[:, :, :], ACT.Ln, bias=1.0).then_inc(S("ml_ln"), 1)
                    if t == 3:
                        act.wait_ge(S("ml_nm"), 1)
                        A(row_f[:, :, :], row_l[:, :, :], ACT.Exp).then_inc(S("ml_en"), 1)
                    if t == 4:
                        act.wait_ge(S("ml_cols"), 1)
                        A(cols[:, 1:3, :, :, :].rearrange("p a b c d -> p (a b c d)"), pm[0][:, 16:48], ACT.Copy)
                        A(cols[0:META, 0, :, :, :].rearrange("p b c d -> p (b c d)"), pm[0][0:META, 0:16],
                          ACT.Copy).then_inc(S("ml_colc"), 1)
                    for n in ML_VT.get(t - 1, ()):
                        vt_copy(n, 2 + n % 2)
                    yield

                def ptc(u):
                    t0, tn = TILES[u % 3]
                    act.wait_ge(S("ml_ptdone"), u + 1)
                    if u % 3 == 0 and u:
                        act.wait_ge(S("ml_pv"), u // 3)
                    A(ml_ptm[:, t0:t0 + tn], pm[3][0:META, 2 * P:2 * P + tn], ACT.Copy)
                    A(ml_ptt[:, :, t0:t0 + tn], strided(pm[3], [[P, 2], [1, tn]]), ACT.Copy).then_inc(S("ml_ptcopied"), 1)

                for hd in range(4):
                    for j in range(8):
                        if j == 0 and hd:
                            store_ml(hd - 1)
                        if j in (1, 3, 5):
                            u = 3 * hd + j // 2
                            tn = TILES[u % 3][1]
                            act.wait_ge(S("ml_x_done"), u + 1)
                            A(ml_x[0:tn, :, :], ml_x[0:tn, :, :], ACT.Exp).then_inc(S("ml_w_done"), 1)
                        if j in (3, 5, 7):
                            ptc(3 * hd + j // 2 - 1)
                        yield
                store_ml(3)
                yield
                act.wait_ge(S("ml_stored"), 4)
                for hd in range(4):
                    if hd >= 2:
                        act.wait_ge(S("po_ss"), hd - 1)
                    A(e_sq[:, hd % 2, :, :], y_ml[:, 2 * hd:2 * hd + 2, :], ACT.Square).then_inc(S("po_sq"), 1)
                    if hd % 2:
                        yield
                act.wait_ge(S("po_ss"), 4)
                for hd in range(4):
                    ins = A(e_rr[:, hd, :], pm[hd][:, 0:T], ACT.Sqrt, bias=eps[:, :], scale=1.0 / 256)
                ins.then_inc(S("po_rt"), 1)
                yield
                A(proj[:, 40:48, :], proj[:, 40:48, :], ACT.Sigmoid).then_inc(S("po_gate"), 1)

            def store_ml(hd):
                act.wait_ge(S("ml_pv"), hd + 1)
                A(y_ml[:, 2 * hd:2 * hd + 2, :], ps[:, 4:6, 0:T], ACT.Copy).then_inc(S("ml_stored"), 1)

            def load_bias(n):
                hd, qt = n // 2, n % 2
                if n >= 4:
                    act.wait_ge(S("na_biased"), n - 3)
                for rr in range(2):
                    r = 2 * qt + 1 - rr
                    dst = bias[64 * rr:64 * rr + 64, n % 4, META:T].rearrange("p (r c) -> p r c", r=ROWS)
                    off = ab_rel_bias.offset + hd * 15 * 31 + (WIN_H - 1 - r) * 31 + (WIN_W - 1) - (GRID_W - 1)
                    act.dma_start(dst, bass.AP(ab_rel_bias.tensor, off, [[1, GRID_W], [31, ROWS], [1, GRID_W]])).then_inc(S(f"bias_in{n % 4}"), 16)

            def attention():
                qk = proj[:, 0:16, :].rearrange("p (g h) t -> p g h t", h=NA_HEADS)
                for n in range(4):
                    load_bias(n)
                for t in range(9):
                    if t >= 1:
                        vt_copy(8 + t - 1, (t - 1) % 2)
                        act.wait_ge(S("qk_ss"), t)
                        if t >= 2:
                            act.wait_ge(S("qk_ready"), t - 1)
                        A(rt2[:, :, :], ps[:, 6:8, 0:T], ACT.Sqrt, bias=eps[:, :], scale=1.0 / P).then_inc(S("qk_rt"), 1)
                    if t < 8:
                        A(sq2[:, :, :], qk[:, :, t, :], ACT.Square).then_inc(S("qk_sq"), 1)
                    yield
                act.wait_ge(S("nm_max"), 1)
                A(na_m[:, :, :], na_m[:, :, :], ACT.Exp).then_inc(S("nm_exp"), 1)
                yield
                act.wait_ge(S("nm_ptdone"), 1)
                A(na_mt[:, :, :], pm[3][0:META, P:2 * P], ACT.Copy).then_inc(S("nm_ptcopied"), 1)
                act.wait_ge(S("nm_ptcopied"), 1)

                def stored(hd):
                    k = 24 + hd
                    act.wait_ge(S("na_pv"), hd + 1)
                    if hd >= 4:
                        act.wait_ge(S("act_ready"), k - 3)
                    A(ntmp[:, hd % 4, :], pm[3][:, 0:T], ACT.Copy).then_inc(S("na_stored"), 1)
                    act.wait_ge(S("na_stored"), hd + 1)
                    A(act_hi[:, hd, :], ntmp[:, hd % 4, :], ACT.Copy).then_inc(S("x_hi"), 1)

                N = 2 * NA_HEADS
                for t in range(N + 3):
                    n = t - 1
                    if 0 <= n < N:
                        act.wait_ge(S("na_max"), n + 1)
                        A(na_p[:, n % 2, :], na_s[:, n % 2, :], ACT.Exp, bias=col[:, n % 2:n % 2 + 1],
                          accum_out=col[:, 2 + n % 2:3 + n % 2]).then_inc(S("na_exp"), 1)
                        if n + 4 < N:
                            load_bias(n + 4)
                    n = t - 2
                    if 0 <= n < N:
                        hd, qt = n // 2, n % 2
                        t0 = TILES[1 + qt][0]
                        act.wait_ge(S("na_ptdone"), n + 1)
                        if hd >= 2:
                            act.wait_ge(S("na_pv"), hd - 1)
                        if qt == 0:
                            A(pt_m[:, hd % 2, 0:META], na_mt[:, hd, :], ACT.Copy)
                        A(pt_m[:, hd % 2, t0:t0 + P], pm[2][0:META, 2 * P:3 * P][:, ::-1], ACT.Copy)
                        A(pt[:, hd % 2, :, t0:t0 + P], strided(pm[2][:, P - 1:P], [[P, 2], [-1, P]]),
                          ACT.Copy).then_inc(S("na_ptcopied"), 1)
                    n = t - 3
                    if n >= 1 and n % 2:
                        stored(n // 2)
                    yield

            for b in range(2):
                act.wait_ge(S("par_done"), b + 1)
                flat = conv[:, :, :, :].rearrange("p a b c -> p (a b c)")
                if b == 0:
                    A(flat[:, 0:440], pm[0][:, 0:440], ACT.Copy).then_inc(S("par_evac"), 1)
                else:
                    A(flat[:, 440:704], pm[1][:, 0:264], ACT.Copy).then_inc(S("par_evac"), 1)
                    A(vec[:, :], pm[1][:, 264:264 + V_N], ACT.Copy).then_inc(S("par_evac"), 1)
            for k in range(0, KT, 2):
                act.wait_ge(S("xT_done"), k + 2)
                A(h[:, k:k + 2, :], ps[:, k % 4:k % 4 + 2, 0:T], ACT.Copy).then_inc(S("h_built"), 1)
            act.wait_ge(S("h_built"), KT // 2)
            act.wait_ge(S("par_evac"), 3)
            act.wait_ge(S("const_done"), 3)
            norm(0)
            gemm(G["ml_in"], first=norm_side(0))
            gemm(G["na_in"], beside=mlstm())
            act.wait_ge(S("used"), 8 * G["ml_out"]["it0"])
            for k in range(8):
                act.wait_ge(S("ml_made"), k + 1)
                A(act_hi[:, 8 + k, :], y_ml[:, k, :], ACT.Copy).then_inc(S("x_hi"), 1)
            act.wait_ge(S("act_ready"), 24)
            gemm(G["ml_out"], beside=attention())
            gemm(G["na_out"])

            def ffn_stage(layer, n):
                act.wait_ge(S("bank_free"), 2 + G[f"up{layer}0"]["gr0"])
                norm(n)
                gemm(G[f"up{layer}0"], first=norm_side(n))
                gemm(G[f"down{layer}0"])
                for part in (1, 2):
                    gemm(G[f"up{layer}{part}"])
                    gemm(G[f"down{layer}{part}"])

            ffn_stage(0, 1)
            act.wait_ge(S("bank_free"), 2 + G["qk_in"]["gr0"])
            norm(2)

            def gates_side():
                yield from norm_side(2)
                yield
                act.wait_ge(S("gup_in"), 1)
                for j in range(2):
                    act.dma_start(gup[RANK * j:RANK * (j + 1), j, :], c_gate_up[0, j]).then_inc(S("gup_in"), 16)
                yield

            def decays():
                for q in range(8):
                    j, k = q // 4, 2 * (q % 4)
                    yield
                    act.wait_ge(S("gu_mm"), q + 1)
                    if q:
                        act.wait_ge(S("b_done"), q)
                    for m in range(2):
                        n = 8 * j + k + m
                        ins = A(bc[:, j, k + m, :], pm[2 * (q % 2) + m][:, 0:T], ACT.Identity, bias=vec[:, V_GB + n:V_GB + n + 1])
                    ins.then_inc(S("gu_x"), 1)
                    act.wait_ge(S("gu_x"), q + 1)
                    chain.link(A(ge[:, :, :], bc[:, j, k:k + 2, :], ACT.Abs))
                    yield
                    chain.link(A(ge[:, :, :], ge[:, :, :], ACT.Exp, scale=-1.0))
                    A(ge[:, :, :], ge[:, :, :], ACT.Ln, bias=1.0).then_inc(S("gu_ln"), 1)
                    yield

            def gla():
                A(proj[:, 0:8, :], proj[:, 0:8, :], ACT.Copy, scale=GLA_SCALE).then_inc(S("q_scaled"), 1)
                ahead = 0
                for t in range(GL_TICKS):
                    n = levels_before[min(t + 1, len(units))]
                    while ahead < min(n + 1, 8 * NL):
                        u = [u for u in range(len(units)) if units[u][1] is not None][ahead]
                        t0, t1 = level_span(units[u][2])
                        act.wait_ge(S("gl_dsub"), ahead + 1)
                        act.wait_ge(S("gl_psub"), ahead + 1)
                        e = gl_e[:, ahead % 2, :, t0:t1]
                        A(e, e, ACT.Exp, scale=1.0 / GLA_TAU).then_inc(S("gl_exp"), 1)
                        ahead += 1
                    if t % 4 == 1 and 5 <= t <= 33:
                        for m in range(2):
                            vt_copy(16 + (t - 5) // 2 + m, 2 + m)
                    if t - 1 in WEIGH:
                        n = WEIGH[t - 1]
                        act.wait_ge(S("gl_pv"), n + 1)
                        A(o_tile(n), pm[2 + n % 2][:, 0:T], ACT.Copy).then_inc(S("gl_stored"), 1)
                    if t in SQUARE:
                        square(SQUARE[t])
                    if t - 1 in SQUARE:
                        keep(SQUARE[t - 1])
                    yield
                square(3)
                keep(3)

            def square(hd):
                act.wait_ge(S("gl_stored"), 4 * hd + 4)
                for j in range(2):
                    b = 2 * hd if j == 0 else 8 + 2 * hd
                    ins = A(bc[:, j, 2 * hd:2 * hd + 2, :], proj[:, b:b + 2, :], ACT.Square)
                ins.then_inc(S("po_sq"), 1)

            def keep(hd):
                act.wait_ge(S("po_ss"), 4 + hd + 1)
                A(bc[:, 0, 2 * hd, :], pm[2 + hd % 2][:, 0:T], ACT.Copy).then_inc(S("po_ssc"), 1)

            gemm(G["qk_in"], first=gates_side(), beside=decays())
            gemm(G["vr_in"], beside=gla())
            act.wait_ge(S("po_ssc"), 4)
            rr = bc[:, 0, 0:8:2, :]
            A(rr, rr, ACT.Sqrt, bias=eps[:, :], scale=1.0 / 512).then_inc(S("po_rt"), 1)
            for q in range(4):
                A(proj[:, 32 + 4 * q:36 + 4 * q, :], proj[:, 32 + 4 * q:36 + 4 * q, :], ACT.Silu).then_inc(S("po_gate"), 1)
            act.wait_ge(S("used"), 8 * G["gl_out"]["it0"])
            for k in range(KT):
                act.wait_ge(S("n_ready"), k + 1)
                A(act_hi[:, k, :], ntmp[:, k % 4, :], ACT.Copy).then_inc(S("x_hi"), 1)
            gemm(G["gl_out"])
            ffn_stage(1, 3)
            for b in range(2):
                for q in range(4):
                    n = 4 * b + q
                    act.wait_ge(S("out_done"), n + 1)
                    A(ostage[:, b, 512 * q:512 * (q + 1)], pm[n % 4][:, :], ACT.Copy).then_inc(S("out_evac"), 1)

        @block.vector
        def _(dve):
            chain = Chain(dve, S("dve_chain"))
            V = nc.vector
            link = chain.link
            V.memset(ones[:, :], 1.0).then_inc(S("const_done"), 1)
            V.memset(eps[:, :], EPS).then_inc(S("const_done"), 1)
            dve.sem_inc(S("bank_free"), 2)

            def lo(g, it, s):
                kc = g["ks"][s % g["gs"]]
                dve.wait_ge(S("hi_done"), (it + g["it0"]) * 8 + (s + 1))
                V.tensor_tensor(w_lo[:, s % 4, 0:kc * 256], raw[:, s % 4, 0:kc * 256],
                                w_hi[:, s % 4, 0:kc * 256].bitcast(F32), ALU.subtract).then_inc(S("split_done"), 1)

            def evac(g, i, grp):
                n = i + g["it0"]
                pair = grp % 2
                t0 = g["t0"]
                banks = ps[:, 2 * pair:2 * pair + 2, 0:T - t0]
                dve.wait_ge(S("used"), n * 8 + g["gs"] * (grp + 1))
                if g["evac"] == "resid":
                    hh = h[:, bass.ds(i * (2 * g["ng"]) + 2 * grp, 2), t0:T]
                    V.tensor_tensor(hh, banks, hh, ALU.add).then_inc(S("bank_free"), 1)
                    return
                rs = bcast(rstd[:, t0:T], 2)
                if g["evac"] == "store":
                    gi = g["ng"] * i + grp if isinstance(i, int) else None
                    if g.get("v_groups") and gi < g["v_groups"]:
                        if gi >= 2:
                            dve.wait_ge(S("vt_done"), 16 + 2 * gi - 2)
                        V.tensor_tensor(ntmp[:, 2 * (gi % 2):2 * (gi % 2) + 2, :], banks, rs, ALU.mult).then_inc(S("bank_free"), 1)
                        return
                    o = proj[:, bass.ds(i * 4 + (g["p0"] + 2 * grp), 2), :]
                    V.tensor_tensor(o, banks, rs, ALU.mult).then_inc(S("bank_free"), 1)
                    return
                c = i + g["c0"]
                o0 = META if t0 else 0
                b1 = max(o0, 1)
                V.tensor_tensor(un[:, grp, :, t0:T], banks, rs, ALU.mult).then_inc(S("u_ready"), 1)
                dve.wait_ge(S("u_ready"), c * 2 + (grp + 1))
                dve.sem_inc(S("bank_free"), 1)
                dve.wait_ge(S("conv_mid"), c * 2 + (grp + 1))
                wt = [conv[:, g["layer"], tap, :] for tap in range(4)]
                mt = [i * 2 + (grp * FT + g["f0"] + m) for m in range(2)]
                for m in range(2):
                    ins = V.scalar_tensor_tensor(acc[:, grp, m, b1:T], un[:, grp, m, b1 - 1:T - 1],
                                                 wt[0][:, bass.ds(mt[m], 1)], acc[:, grp, m, b1:T], ALU.mult, ALU.add)
                link(ins)
                for m in range(2):
                    ins = V.scalar_tensor_tensor(acc[:, grp, m, o0:T - 1], un[:, grp, m, o0 + 1:T],
                                                 wt[2][:, bass.ds(mt[m], 1)], acc[:, grp, m, o0:T - 1], ALU.mult, ALU.add)
                if grp == 0:
                    ins.then_inc(S("gates_done"), 1)
                    dve.wait_ge(S("gates_done"), c + 1)
                    return
                link(ins)
                dve.wait_ge(S("silu_done"), c + 1)
                V.tensor_tensor(gp[:, :, o0:T], sg[:, :, o0:T], acc[:, 1, :, o0:T], ALU.mult).then_inc(S("mid_done"), 1)
                dve.wait_ge(S("mid_done"), c + 1)
                link(V.tensor_copy(g_hi[:, bass.ds(i * 2, 2), o0:T], gp[:, :, o0:T]))
                V.tensor_tensor(g_lo[:, bass.ds(i * 2, 2), o0:T], gp[:, :, o0:T],
                                g_hi[:, bass.ds(i * 2, 2), o0:T].bitcast(F32), ALU.subtract).then_inc(S("mid_split"), 1)
                dve.wait_ge(S("mid_split"), c + 1)

            def gemm(g, first=None, beside=None):
                if g["it0"] == 0:
                    for s in range(3):
                        lo(g, 0, s)
                per = 4 if g["evac"] == "conv" else 0

                def body(i, nxt, ni, side=None, late=False):
                    for s in range(8):
                        if s + 3 < 8:
                            lo(g, i, s + 3)
                        elif nxt:
                            lo(nxt, ni, s + 3 - 8)
                        if late:
                            if s >= 6:
                                evac(g, i, s - 6)
                        elif s % g["gs"] == g["gs"] - 1:
                            evac(g, i, s // g["gs"])
                        if side:
                            advance(side)

                last, start = g["iters"] - 1, 0
                if first:
                    body(0, g, 1, first, late=True)
                    finish(first)
                    start = 1
                if beside:
                    for i in range(start, last):
                        body(i, g, i + 1, beside)
                else:
                    n0 = chain.n
                    with dve.Fori(start, last) as i:
                        chain.enter(i - start, per)
                        body(i, g, i + 1)
                    assert chain.n - n0 == per, (chain.n - n0, per)
                    chain.leave(last - start, per)
                body(last, g["next"], 0, beside)
                if beside:
                    finish(beside)

            def norm(n):
                v0, base = NORM_V[n], NORM_READY[n]
                if n in (0, 2):
                    o, w = (0, GATES) if n == 0 else (GATES, LRS)
                    dve.wait_ge(S("tail_in"), 48)
                    for k in range(KT):
                        ins = V.tensor_scalar(tail_w[:, k, o:o + w], tail_w[:, k, o:o + w], vec[:, v0 + k:v0 + k + 1], None, ALU.mult)
                for k in range(KT):
                    dve.wait_ge(S("x_hi"), base + k + 1)
                    V.scalar_tensor_tensor(act_lo[:, k, :], h[:, k, :], vec[:, v0 + k:v0 + k + 1], act_hi[:, k, :].bitcast(F32),
                                           ALU.mult, ALU.subtract).then_inc(S("act_ready"), 1)
                    if k == 3 and n in (0, 2):
                        dve.wait_ge(S("act_ready"), base + 4)
                        dve.sem_inc(S("tail_scaled"), 1)

            def norm_side(n):
                for t in range(5):
                    yield
                dve.wait_ge(S("rt_ready"), n + 1)
                V.reciprocal(rstd[:, :], rstd[:, :]).then_inc(S("rs_ready"), 1)
                dve.wait_ge(S("rs_ready"), n + 1)
                yield
                if n in (0, 2):
                    w = GATES if n == 0 else LRS
                    dve.wait_ge(S("tail_done"), n // 2 + 1)
                    ins = V.tensor_tensor(tail[0:w, :], pm[1][0:w, 0:T], rstd[0:w, :], ALU.mult)
                    if n == 0:
                        link(ins)
                        ins = V.tensor_scalar(tail[0:w, :], tail[0:w, :], gate_b[:, :], None, ALU.add)
                    ins.then_inc(S("tail_evac"), 1)
                    yield

            def turn(ap, d):
                return ap[:, d, ::-1] if d else ap[:, d, :]

            def mlstm():
                for t in range(9):
                    if t == 2:
                        dve.wait_ge(S("ml_ln"), 1)
                        one = bass.AP(ones, 0, [[P, ML_HEADS], [0, T]])
                        link(V.scalar_tensor_tensor(row_l[:, :, :], row_f[:, :, :], 0.0, row_l[:, :, :], ALU.min, ALU.subtract))
                        V.tensor_tensor_scan(turn(row_b, 0), one, turn(row_l, 0), 0.0, ALU.mult, ALU.add)
                        link(V.tensor_tensor_scan(turn(row_b, 1), one, turn(row_l, 1), 0.0, ALU.mult, ALU.add))
                        link(V.tensor_tensor(row_c[:, :, :], row_c[:, :, :], row_b[:, :, :], ALU.subtract))
                    if t == 3:
                        V.tensor_tensor_scan(turn(row_m, 0), one, turn(row_c, 0), 0.0, ALU.mult, ALU.max)
                        link(V.tensor_tensor_scan(turn(row_m, 1), one, turn(row_c, 1), 0.0, ALU.mult, ALU.max))
                        link(V.scalar_tensor_tensor(row_l[:, :, :], row_b[:, :, :], -1.0, row_m[:, :, :], ALU.mult, ALU.subtract))
                        V.tensor_scalar(row_m[:, :, :], row_m[:, :, :], -1.0, None, ALU.mult).then_inc(S("ml_nm"), 1)
                    yield
                dve.wait_ge(S("ml_colc"), 1)
                dve.wait_ge(S("mask_done"), 2)

                def mix_x(u):
                    hd, tt = u // 3, u % 3
                    t0, tn = TILES[tt]
                    if u:
                        dve.wait_ge(S("ml_used"), u)
                    dve.wait_ge(S("ml_cb"), hd + 1)
                    for d in range(2):
                        mk = strip[0:tn, d, META + P - t0:META + P - t0 + T]
                        ins = V.scalar_tensor_tensor(ml_x[0:tn, d, :], pm[d][0:tn, 0:T], cols[0:tn, tt, d, 0, hd:hd + 1],
                                                     mk, ALU.add, ALU.min)
                    ins.then_inc(S("ml_x_done"), 1)

                def mix_p(u):
                    hd, tt = u // 3, u % 3
                    tn = TILES[tt][1]
                    dve.wait_ge(S("ml_scores"), u + 1)
                    dve.wait_ge(S("ml_w_done"), u + 1)
                    if u >= 1:
                        dve.wait_ge(S("ml_pn"), u)
                    for d in range(2):
                        ins = V.scalar_tensor_tensor(ml_p[0:tn, d, :], pm[2][0:tn, 0:T], ML_SCALE, ml_x[0:tn, d, :],
                                                     ALU.mult, ALU.mult, accum_out=den[0:tn, d:d + 1])
                    ins.then_inc(S("ml_used"), 1)
                    dve.wait_ge(S("ml_used"), u + 1)
                    link(V.scalar_tensor_tensor(den[0:tn, 2:4], den[0:tn, 0:2], -1.0, den[0:tn, 0:2], ALU.mult, ALU.max))
                    link(V.tensor_tensor(den[0:tn, 2:4], den[0:tn, 2:4], cols[0:tn, tt, :, 1, hd], ALU.max))
                    link(V.reciprocal(den[0:tn, 4:6], den[0:tn, 2:4]))
                    if u >= 1:
                        dve.wait_ge(S("ml_ptdone"), u)
                    link(V.tensor_scalar(ml_sum[0:tn, :], ml_p[0:tn, 0, :], den[0:tn, 4:5], None, ALU.mult))
                    V.scalar_tensor_tensor(ml_sum[0:tn, :], ml_p[0:tn, 1, :], den[0:tn, 5:6], ml_sum[0:tn, :],
                                           ALU.mult, ALU.add).then_inc(S("ml_pn"), 1)

                for hd in range(4):
                    for j in range(8):
                        if j in (1, 3, 5):
                            mix_x(3 * hd + j // 2)
                        if j in (2, 4, 6):
                            mix_p(3 * hd + j // 2 - 1)
                        yield
                for _ in range(3):
                    yield
                dve.wait_ge(S("po_rt"), 1)
                link(V.reciprocal(e_rr[:, :, :], e_rr[:, :, :]))
                yield
                for k in range(8):
                    link(V.scalar_tensor_tensor(y_ml[:, k, :], y_ml[:, k, :], vec[:, V_ML + k:V_ML + k + 1], e_rr[:, k // 2, :],
                                                ALU.mult, ALU.mult))
                    if k == 0:
                        dve.wait_ge(S("po_gate"), 1)
                    V.tensor_tensor(y_ml[:, k, :], y_ml[:, k, :], proj[:, 40 + k, :], ALU.mult).then_inc(S("ml_made"), 1)
                    if k % 2:
                        yield

            def attention():
                for t in range(9):
                    if t >= 1:
                        u = t - 1
                        dve.wait_ge(S("qk_rt"), u + 1)
                        link(V.reciprocal(rt2[:, :, :], rt2[:, :, :]))
                        for o, i in ((q_rev[:, u, 0:META], slice(0, META)),
                                     (q_rev[:, u, META:T].rearrange("p (a b) -> p a b", b=P)[:, :, ::-1], slice(META, T))):
                            q_, r_ = proj[:, u, i], rt2[:, 0, i]
                            if i.stop == T:
                                q_, r_ = (v.rearrange("p (a b) -> p a b", b=P) for v in (q_, r_))
                            V.scalar_tensor_tensor(o, q_, vec[:, V_QG:V_QG + 1], r_, ALU.mult, ALU.mult)
                        V.scalar_tensor_tensor(proj[:, 8 + u, :], proj[:, 8 + u, :], vec[:, V_KG:V_KG + 1], rt2[:, 1, :],
                                               ALU.mult, ALU.mult).then_inc(S("qk_ready"), 1)
                    yield
                dve.wait_ge(S("nm_scores"), 1)
                s3 = pm[3][0:META, 0:P].rearrange("p (h q) -> p h q", q=META)
                link(V.tensor_scalar(na_m[:, :, :], s3, NA_SCALE, None, ALU.mult))
                mx = col[0:META, 8:16]
                link(V.tensor_reduce(mx, na_m[:, :, :], AX.X, ALU.max))
                V.tensor_tensor(na_m[:, :, :], na_m[:, :, :], bcast(mx, META, 2), ALU.subtract).then_inc(S("nm_max"), 1)
                dve.wait_ge(S("nm_exp"), 1)
                link(V.tensor_reduce(mx, na_m[:, :, :], AX.X, ALU.add))
                link(V.reciprocal(mx, mx))
                V.memset(pt[:, :, :, 0:META], 0.0)
                V.tensor_tensor(na_m[:, :, :], na_m[:, :, :], bcast(mx, META, 2), ALU.mult).then_inc(S("nm_norm"), 1)
                yield

                def soft_a(n):
                    dve.wait_ge(S("na_scores"), n + 1)
                    dve.wait_ge(S("bias_ready"), n + 1)
                    if n >= 2:
                        dve.wait_ge(S("na_exp"), n - 1)
                    V.scalar_tensor_tensor(na_s[:, n % 2, :], pm[n % 2][:, 0:T], NA_SCALE, bias[:, n % 4, :],
                                           ALU.mult, ALU.add).then_inc(S("na_biased"), 1)
                    dve.wait_ge(S("na_biased"), n + 1)
                    V.tensor_reduce(col[:, n % 2:n % 2 + 1], na_s[:, n % 2, :], AX.X, ALU.max, negate=True).then_inc(S("na_max"), 1)

                def soft_b(n):
                    dve.wait_ge(S("na_exp"), n + 1)
                    c = col[:, 4 + n % 2:5 + n % 2]
                    link(V.reciprocal(c, col[:, 2 + n % 2:3 + n % 2]))
                    V.tensor_scalar(na_p[:, n % 2, :], na_p[:, n % 2, :], c, None, ALU.mult).then_inc(S("na_norm"), 1)

                def low(hd):
                    dve.wait_ge(S("x_hi"), 24 + hd + 1)
                    V.tensor_tensor(act_lo[:, hd, :], ntmp[:, hd % 4, :], act_hi[:, hd, :].bitcast(F32),
                                    ALU.subtract).then_inc(S("act_ready"), 1)

                N = 2 * NA_HEADS
                for t in range(N + 3):
                    if 0 <= t - 1 < N:
                        soft_a(t - 1)
                        soft_b(t - 1)
                    n = t - 3
                    if n >= 1 and n % 2:
                        low(n // 2)
                    yield

            def decays():
                onesT = bass.AP(ones, 0, [[P, P], [0, T]])
                for q in range(8):
                    j, k = q // 4, 2 * (q % 4)
                    yield
                    yield
                    dve.wait_ge(S("gu_ln"), q + 1)
                    b2 = bc[:, j, k:k + 2, :]
                    link(V.scalar_tensor_tensor(b2, b2, 0.0, ge[:, :, :], ALU.min, ALU.subtract))
                    for m in range(2):
                        v = turn(bc[:, :, k + m, :], j)
                        ins = V.tensor_tensor_scan(v, onesT, v, 0.0, ALU.mult, ALU.add)
                    ins.then_inc(S("b_done"), 1)
                    yield

            def gates_side():
                dve.wait_ge(S("act_ready"), NORM_READY[2] + KT)
                V.memset(gup[:, :, :], 0.0).then_inc(S("gup_in"), 1)
                yield from norm_side(2)

            lev = [u for u in range(len(units)) if units[u][1] is not None]

            def gla():
                dve.wait_ge(S("q_scaled"), 1)
                dve.wait_ge(S("b_done"), 8)
                dve.wait_ge(S("lmask_done"), 14)

                def sub(v):
                    if v >= 2:
                        dve.wait_ge(S("gl_pmul"), v - 1)
                        dve.wait_ge(S("gl_dmul"), v - 1)
                    o, b, r = level_sub(lev[v], "q")
                    V.tensor_tensor(o, b, r, ALU.subtract).then_inc(S("gl_dsub"), 1)

                def mul(v):
                    if v >= 2:
                        dve.wait_ge(S("gl_g"), lev[v - 2] + 1)
                    dve.wait_ge(S("gl_exp"), v + 1)
                    o, e, q_ = level_mul(lev[v], "q")
                    V.tensor_tensor(o, e, q_, ALU.mult).then_inc(S("gl_dmul"), 1)

                def take(u):
                    hd, d, l = units[u]
                    b, s = pm[u % 2], hd % 2
                    dve.wait_ge(S("gl_g"), u + 1)
                    if u >= 1:
                        dve.wait_ge(S("gl_cp"), u)
                    diag = strided(at_t[:, s, 0, META:META + P], [[T + P, 2], [1, P]])
                    if d is None:
                        if hd >= 2:
                            dve.wait_ge(S("gl_pv"), 4 * (hd - 1))
                        V.scalar_tensor_tensor(at_m[:, s, 0:META], b[0:META, 2 * P:2 * P + META], 2.0, ident[0:META, 0:META],
                                               ALU.mult, ALU.mult)
                        ins = V.scalar_tensor_tensor(diag, strided(b, [[P, 2], [1, P]]), 2.0, bcast(ident[:, :], 2),
                                                     ALU.mult, ALU.mult)
                        ins.then_inc(S("gl_cp"), 1)
                        return
                    kind, H = LEVELS[l]
                    if kind == "in":
                        mk = lmask[:, d, l, :].bitcast(U16)
                        if H <= 8:
                            V.copy_predicated(at_m[:, s, 0:META], mk[0:META, 0:META], b[0:META, 2 * P:2 * P + META])
                        ins = V.copy_predicated(diag, bcast(mk, 2), strided(b, [[P, 2], [1, P]]))
                    elif H == META:
                        if d == 0:
                            ins = V.tensor_copy(at_m[:, s, META:META + P], b[0:META, 0:P])
                        else:
                            ins = V.tensor_copy(at_t[:, s, 0, 0:META], b[:, 0:META])
                    elif d == 0:
                        V.tensor_copy(at_m[:, s, META + P:T], b[0:META, 0:P])
                        ins = V.tensor_copy(at_t[:, s, 0, META + P:T], b[:, P:2 * P])
                    else:
                        ins = V.tensor_copy(at_t[:, s, 1, 0:META + P], b[:, 0:META + P])
                    ins.then_inc(S("gl_cp"), 1)

                subs = 0
                for t in range(GL_TICKS):
                    n = levels_before[min(t + 1, len(units))]
                    while subs < min(n + 1, len(lev)):
                        sub(subs)
                        subs += 1
                    if t < len(units) and units[t][1] is not None:
                        mul(levels_before[t])
                    if 1 <= t <= len(units):
                        take(t - 1)
                    yield

            dve.wait_ge(S("par_evac"), 3)
            norm(0)
            gemm(G["ml_in"], first=norm_side(0))
            gemm(G["na_in"], beside=mlstm())
            for k in range(8):
                dve.wait_ge(S("x_hi"), KT + k + 1)
                V.tensor_tensor(act_lo[:, 8 + k, :], y_ml[:, k, :], act_hi[:, 8 + k, :].bitcast(F32),
                                ALU.subtract).then_inc(S("act_ready"), 1)
            gemm(G["ml_out"], beside=attention())
            gemm(G["na_out"])

            def ffn_stage(layer, n):
                norm(n)
                gemm(G[f"up{layer}0"], first=norm_side(n))
                gemm(G[f"down{layer}0"])
                for part in (1, 2):
                    gemm(G[f"up{layer}{part}"])
                    gemm(G[f"down{layer}{part}"])

            ffn_stage(0, 1)
            norm(2)
            gemm(G["qk_in"], first=gates_side(), beside=decays())
            gemm(G["vr_in"], beside=gla())

            dve.wait_ge(S("po_rt"), 2)
            rr = bc[:, 0, 0:8:2, :]
            link(V.reciprocal(rr, rr))

            def make(k):
                o = ntmp[:, k % 4, :]
                if k >= 4:
                    dve.wait_ge(S("act_ready"), 64 + k - 3)
                link(V.scalar_tensor_tensor(o, o_tile(k), vec[:, V_GLA + k:V_GLA + k + 1], bc[:, 0, 2 * (k // 4), :],
                                            ALU.mult, ALU.mult))
                dve.wait_ge(S("po_gate"), 1 + k // 4 + 1)
                V.tensor_tensor(o, o, proj[:, 32 + k, :], ALU.mult).then_inc(S("n_ready"), 1)

            def low(k):
                dve.wait_ge(S("x_hi"), 64 + k + 1)
                V.tensor_tensor(act_lo[:, k, :], ntmp[:, k % 4, :], act_hi[:, k, :].bitcast(F32),
                                ALU.subtract).then_inc(S("act_ready"), 1)
            for k in range(KT):
                make(k)
                if k >= 1:
                    low(k - 1)
            low(KT - 1)
            gemm(G["gl_out"])
            ffn_stage(1, 3)

        @block.tensor
        def _(pe):
            mm = nc.tensor.matmul
            tr = nc.tensor.transpose

            def gemm(g, first=None, beside=None):
                mid = g.get("mid")
                xh, xl = (g_hi, g_lo) if mid else (act_hi, act_lo)
                t0 = g["t0"]

                def body(i, side=None):
                    n = i + g["it0"]
                    for s in range(8):
                        grp, c = s // g["gs"], s % g["gs"]
                        kc, k0 = g["ks"][c], sum(g["ks"][:c])
                        if c == 0:
                            pe.wait_ge(S("bank_free"), i * g["ng"] + (g["gr0"] + grp + 1))
                        if grp == 0:
                            if mid:
                                pe.wait_ge(S("mid_split"), g["c0"] + (k0 + kc + 1) // 2)
                            else:
                                pe.wait_ge(S("act_ready"), g["ready"] + k0 + kc)
                        pe.wait_ge(S("split_done"), n * 8 + (s + 1))
                        for m in range(2):
                            o = ps[:, 2 * (grp % 2) + m, 0:T - t0]
                            for k in range(kc):
                                kk = g["x0"] + k0 + k
                                w0 = k * 256 + m * P
                                wh, wl = w_hi[:, s % 4, w0:w0 + P], w_lo[:, s % 4, w0:w0 + P]
                                end = c == g["gs"] - 1 and k == kc - 1
                                mm(o, wh, xh[:, kk, t0:T], start=(c == 0 and k == 0), stop=False)
                                mm(o, wh, xl[:, kk, t0:T], start=False, stop=False)
                                ins = mm(o, wl, xh[:, kk, t0:T], start=False, stop=end)
                        ins.then_inc(S("used"), 1)
                        if side:
                            advance(side)

                start = 0
                if first:
                    body(0, first)
                    finish(first)
                    start = 1
                if beside:
                    for i in range(start, g["iters"]):
                        body(i, beside)
                    finish(beside)
                else:
                    with pe.Fori(start, g["iters"]) as i:
                        body(i)

            def norm_side(n):
                for t in range(4):
                    yield
                pe.wait_ge(S("sq_added"), 3 * n + 3)
                for k in range(4):
                    ins = mm(pm[0][:, 0:T], ones[:, :], sq[:, k, :], start=(k == 0), stop=(k == 3))
                ins.then_inc(S("ss_ready"), 1)
                yield
                if n in (0, 2):
                    o, w = (0, GATES) if n == 0 else (GATES, LRS)
                    pe.wait_ge(S("tail_scaled"), n // 2 + 1)
                    for k in range(KT):
                        ins = mm(pm[1][0:w, 0:T], tail_w[:, k, o:o + w], h[:, k, :], start=(k == 0), stop=(k == KT - 1))
                    ins.then_inc(S("tail_done"), 1)
                    yield

            def vt(n, src, b):
                tr(pm[b][0:META, 2 * P:3 * P], src[:, 0:META], ident[:, :])
                tr(pm[b][:, 0:P], src[:, META:META + P], ident[:, :])
                tr(pm[b][:, P:2 * P], src[:, META + P:T], ident[:, :]).then_inc(S("vt_done"), 1)

            def weigh(o, v0, ptt, ptm):
                mm(o, v_tok[0:META, 0, v0:v0 + P], ptm, start=True, stop=False)
                mm(o, v_tok[:, 1, v0:v0 + P], ptt[:, 0, :], start=False, stop=False)
                return mm(o, v_tok[:, 2, v0:v0 + P], ptt[:, 1, :], start=False, stop=True)

            def mlstm():
                for t in range(9):
                    if t == 0:
                        pe.wait_ge(S("tail_evac"), 1)
                        pe.wait_ge(S("bank_free"), 2 + G["na_in"]["gr0"])
                        for j in range(4):
                            ins = mm(pm[j][0:ML_HEADS, 0:T], ident[0:GATES, 4 * j:4 * j + 4], tail[0:GATES, :], start=True, stop=True)
                        ins.then_inc(S("ml_sel"), 1)
                    if t == 3:
                        pe.wait_ge(S("ml_nm"), 1)
                        pe.wait_ge(S("ml_en"), 1)
                        for tt, (t0, tn) in enumerate(TILES):
                            for d in range(2):
                                for q, row in enumerate((row_m, row_f)):
                                    o = ((tt * 2 + d) * 2 + q) * 4
                                    ins = mm(pm[0][0:tn, o:o + 4], row[:, d, t0:t0 + tn], ident[0:4, 0:4], start=True, stop=True)
                        ins.then_inc(S("ml_cols"), 1)
                    for n in ML_VT.get(t, ()):
                        if n < 2:
                            pe.wait_ge(S("ml_ln"), 1)
                        else:
                            pe.wait_ge(S("vt_copied"), n - 1)
                        vt(n, proj[:, E_ML[n], :], 2 + n % 2)
                    yield
                pe.wait_ge(S("ml_colc"), 1)
                pe.wait_ge(S("vt_copied"), 8)
                pe.wait_ge(S("sel_done"), 1)

                def scores(u):
                    hd, tt = u // 3, u % 3
                    t0, tn = TILES[tt]
                    if u >= 1:
                        pe.wait_ge(S("ml_used"), u)
                    mm(pm[2][0:tn, 0:T], proj[:, 24 + hd, t0:t0 + tn], proj[:, 28 + hd, :], start=True, stop=True).then_inc(S("ml_scores"), 1)

                def transposed(u):
                    tn = TILES[u % 3][1]
                    pe.wait_ge(S("ml_pn"), u + 1)
                    if u >= 1:
                        pe.wait_ge(S("ml_ptcopied"), u)
                    b = pm[3]
                    tr(b[0:META, 2 * P:2 * P + tn], ml_sum[0:tn, 0:META], ident[0:tn, 0:tn])
                    tr(b[:, 0:tn], ml_sum[0:tn, META:META + P], ident[0:tn, 0:tn])
                    tr(b[:, P:P + tn], ml_sum[0:tn, META + P:T], ident[0:tn, 0:tn]).then_inc(S("ml_ptdone"), 1)

                for hd in range(4):
                    for j in range(8):
                        if j == 0:
                            if hd >= 1:
                                pe.wait_ge(S("ml_stored"), hd)
                            for d in range(2):
                                ins = mm(pm[d][:, 0:T], selrow[:, hd, :], row_c[:, d, :], start=True, stop=True)
                            ins.then_inc(S("ml_cb"), 1)
                            scores(3 * hd)
                        if j in (2, 4, 6):
                            transposed(3 * hd + j // 2 - 1)
                            if j < 6:
                                scores(3 * hd + j // 2)
                        if j == 7:
                            pe.wait_ge(S("ml_ptcopied"), 3 * hd + 3)
                            for e in range(2):
                                ins = weigh(pm[e][:, 0:T], 1024 + hd * 256 + e * P, ml_ptt, ml_ptm[:, :])
                            ins.then_inc(S("ml_pv"), 1)
                        yield
                yield
                for hd in range(4):
                    pe.wait_ge(S("po_sq"), hd + 1)
                    if hd == 0:
                        pe.wait_ge(S("ml_stored"), 4)
                    for j in range(2):
                        ins = mm(pm[hd][:, 0:T], ones[:, :], e_sq[:, hd % 2, j, :], start=(j == 0), stop=(j == 1))
                    ins.then_inc(S("po_ss"), 1)
                    if hd % 2:
                        yield

            def attention():
                pe.wait_ge(S("po_rt"), 1)
                pe.wait_ge(S("bank_free"), 2 + G["ml_out"]["gr0"])
                for t in range(8):
                    if t >= 2:
                        pe.wait_ge(S("vt_copied"), 8 + t - 1)
                    vt(8 + t, proj[:, E_NA[t], :], t % 2)
                    pe.wait_ge(S("qk_sq"), t + 1)
                    if t >= 1:
                        pe.wait_ge(S("qk_rt"), t)
                    for j in range(2):
                        ins = mm(pm[2 + j][:, 0:T], ones[:, :], sq2[:, j, :], start=True, stop=True)
                    ins.then_inc(S("qk_ss"), 1)
                    yield
                pe.wait_ge(S("qk_ready"), NA_HEADS)
                pe.wait_ge(S("vt_copied"), 16)
                for hd in range(NA_HEADS):
                    ins = mm(pm[3][0:META, META * hd:META * (hd + 1)], q_rev[:, hd, 0:META], proj[:, 8 + hd, 0:META], start=True, stop=True)
                ins.then_inc(S("nm_scores"), 1)
                yield
                pe.wait_ge(S("nm_norm"), 1)
                for hd in range(NA_HEADS):
                    ins = tr(pm[3][0:META, P + META * hd:P + META * (hd + 1)], na_m[:, hd, :], ident[0:META, 0:META])
                ins.then_inc(S("nm_ptdone"), 1)
                yield

                N = 2 * NA_HEADS
                for t in range(N + 2):
                    n = t
                    if n < N:
                        hd, qt = n // 2, n % 2
                        t0 = TILES[1 + qt][0]
                        if n >= 2:
                            pe.wait_ge(S("na_biased"), n - 1)
                        mm(pm[n % 2][:, 0:T], q_rev[:, hd, t0:t0 + P], proj[:, 8 + hd, :], start=True, stop=True).then_inc(S("na_scores"), 1)
                    n = t - 1
                    if 0 <= n < N:
                        pe.wait_ge(S("na_norm"), n + 1)
                        if n >= 1:
                            pe.wait_ge(S("na_ptcopied"), n)
                        b = pm[2]
                        tr(b[0:META, 2 * P:3 * P], na_p[:, n % 2, 0:META], ident[:, :])
                        tr(b[:, 0:P], na_p[:, n % 2, META:META + P], ident[:, :])
                        tr(b[:, P:2 * P], na_p[:, n % 2, META + P:T], ident[:, :]).then_inc(S("na_ptdone"), 1)
                    n = t - 2
                    if n >= 0 and n % 2:
                        hd = n // 2
                        pe.wait_ge(S("na_ptcopied"), n + 1)
                        pe.wait_ge(S("nm_ptcopied"), 1)
                        if hd >= 1:
                            pe.wait_ge(S("na_stored"), hd)
                        weigh(pm[3][:, 0:T], hd * P, pt[:, hd % 2], pt_m[:, hd % 2, :]).then_inc(S("na_pv"), 1)
                    yield

            def decays():
                pe.wait_ge(S("tail_evac"), 2)
                pe.wait_ge(S("gup_in"), 33)
                for q in range(8):
                    j, k = q // 4, 2 * (q % 4)
                    if q >= 2:
                        pe.wait_ge(S("gu_x"), q - 1)
                    for m in range(2):
                        ins = mm(pm[2 * (q % 2) + m][:, 0:T], gup[:, j, (k + m) * P:(k + m + 1) * P], tail[:, :], start=True, stop=True)
                    ins.then_inc(S("gu_mm"), 1)
                    yield
                    yield
                    yield

            def gram(o, l0, ln, r0, rn, L, R):
                for j in range(2):
                    ins = mm(o, L[:, j, l0:l0 + ln], R[:, j, r0:r0 + rn], start=(j == 0), stop=(j == 1))
                return ins

            def gla():
                pe.wait_ge(S("q_scaled"), 1)
                pe.wait_ge(S("gu_x"), 8)
                for t in range(GL_TICKS):
                    if t < len(units):
                        unit(t)
                    if t % 4 == 0 and 4 <= t <= 32:
                        n = 16 + (t - 4) // 2
                        pe.wait_ge(S("bank_free"), 2 + G["vr_in"]["gr0"] + t // 4)
                        if n >= 18:
                            pe.wait_ge(S("vt_copied"), n)
                        for m in range(2):
                            vt(n + m, ntmp[:, (n + m) % 4, :], 2 + m)
                    if t in WEIGH:
                        n = WEIGH[t]
                        hd = n // 4
                        pe.wait_ge(S("vt_copied"), 32)
                        pe.wait_ge(S("gl_cp"), UH * (hd + 1))
                        if n >= 2:
                            pe.wait_ge(S("gl_stored"), n - 1)
                        if hd >= 2:
                            pe.wait_ge(S("po_ssc"), hd)
                        weigh(pm[2 + n % 2][:, 0:T], n * P, at_t[:, hd % 2], at_m[:, hd % 2, :]).then_inc(S("gl_pv"), 1)
                    if t in SQUARE:
                        squares(SQUARE[t])
                    yield
                squares(3)

            def squares(hd):
                pe.wait_ge(S("po_sq"), 4 + hd + 1)
                pe.wait_ge(S("gl_stored"), 4 * hd + 4)
                for j in range(4):
                    ins = mm(pm[2 + hd % 2][:, 0:T], ones[:, :], bc[:, j // 2, 2 * hd + j % 2, :], start=(j == 0), stop=(j == 3))
                ins.then_inc(S("po_ss"), 1)

            def unit(u):
                hd, d, l = units[u]
                b = pm[u % 2]
                if u >= 2:
                    pe.wait_ge(S("gl_cp"), u - 1)
                if d is None:
                    L, R = proj[:, 8 + 2 * hd:10 + 2 * hd, :], proj[:, 2 * hd:2 * hd + 2, :]
                    kind, H = "in", 1
                else:
                    v = levels_before[u]
                    pe.wait_ge(S("gl_dmul"), v + 1)
                    pe.wait_ge(S("gl_pmul"), v + 1)
                    L = R = gl_x[:, v % 2]
                    kind, H = LEVELS[l]
                if kind == "in":
                    if H <= 8:
                        gram(b[0:META, 2 * P:2 * P + META], 0, META, 0, META, L, R)
                    gram(b[:, 0:P], META, P, META, P, L, R)
                    ins = gram(b[:, P:2 * P], META + P, P, META + P, P, L, R)
                elif H == META:
                    ins = gram(b[0:META, 0:P], 0, META, META, P, L, R) if d == 0 else gram(b[:, 0:META], META, P, 0, META, L, R)
                elif d == 0:
                    gram(b[0:META, 0:P], 0, META, META + P, P, L, R)
                    ins = gram(b[:, P:2 * P], META, P, META + P, P, L, R)
                else:
                    ins = gram(b[:, 0:META + P], META + P, P, 0, META + P, L, R)
                ins.then_inc(S("gl_g"), 1)

            pe.wait_ge(S("const_done"), 3)
            pe.wait_ge(S("param_in"), 16 * 15)
            for j in range(5):
                ins = tr(pm[0][:, 88 * j:88 * (j + 1)], stage[0:88, j, :], ident[0:88, 0:88])
            ins.then_inc(S("par_done"), 1)
            for j in range(5, 8):
                tr(pm[1][:, 88 * (j - 5):88 * (j - 4)], stage[0:88, j, :], ident[0:88, 0:88])
            tr(pm[1][:, 264:264 + V_N], stage[0:V_N, 8, :], ident[0:V_N, 0:V_N]).then_inc(S("par_done"), 1)
            pe.wait_ge(S("tok_in"), 48)
            for k in range(KT):
                if k >= 4:
                    pe.wait_ge(S("h_built"), k // 2 - 1)
                for tt, (t0, tn) in enumerate(TILES):
                    ins = tr(ps[:, k % 4, t0:t0 + tn], tok[0:tn, tt, k * P:(k + 1) * P], ident[0:tn, 0:tn])
                ins.then_inc(S("xT_done"), 1)
            pe.wait_ge(S("par_evac"), 3)
            gemm(G["ml_in"], first=norm_side(0))
            gemm(G["na_in"], beside=mlstm())
            gemm(G["ml_out"], beside=attention())
            gemm(G["na_out"])

            def ffn_stage(layer, n):
                gemm(G[f"up{layer}0"], first=norm_side(n))
                gemm(G[f"down{layer}0"])
                for part in (1, 2):
                    gemm(G[f"up{layer}{part}"])
                    gemm(G[f"down{layer}{part}"])

            ffn_stage(0, 1)
            gemm(G["qk_in"], first=norm_side(2), beside=decays())
            gemm(G["vr_in"], beside=gla())
            gemm(G["gl_out"])
            ffn_stage(1, 3)
            pe.wait_ge(S("bank_free"), 2 + state["gr"])
            for b in range(2):
                t0 = TILES[1 + b][0]
                for q in range(4):
                    n = 4 * b + q
                    if n >= 4:
                        pe.wait_ge(S("out_evac"), n - 3)
                    for j in range(4):
                        ins = tr(pm[n % 4][:, j * P:(j + 1) * P], h[:, 4 * q + j, t0:t0 + P], ident[:, :])
                    ins.then_inc(S("out_done"), 1)


_INS = ["x", "meta_tokens", "norm_mix", "norm_ffn", "ab_w_in", "ab_gate_bias", "ab_q_gain", "ab_k_gain",
        "ab_rel_bias", "ab_ml_gain", "ab_w_out", "c_w_in", "c_gate_up", "c_gate_bias", "c_head_gain",
        "c_w_out", "ffn_w_up", "ffn_conv_w", "ffn_conv_b", "ffn_w_down"]


def kernel(**inputs):
    import numpy as _np
    import concourse.bacc as _bacc
    from concourse import mybir as _mybir
    from concourse.bass_utils import run_bass_kernel_spmd as _run

    nc = _bacc.Bacc("TRN2", target_bir_lowering=False, num_devices=1)
    arrays, args = {}, []
    for name in _INS:
        v = _np.ascontiguousarray(inputs[name])
        arrays[f"in_{name}"] = v
        args.append(nc.dram_tensor(f"in_{name}", v.shape, _mybir.dt.from_np(v.dtype), kind="ExternalInput").ap())
    args.append(nc.dram_tensor("out_y", (1, SEQ, D), _mybir.dt.float32, kind="ExternalOutput").ap())
    build(nc, *args)
    r = _run(nc, [arrays], core_ids=[0])
    return r.results[0]["out_y"]
```

```python
import numpy as np

import concourse.bass as bass
from concourse import mybir
from contextlib import ExitStack

F32 = mybir.dt.float32
F32R = mybir.dt.float32r
BF16 = mybir.dt.bfloat16
U16 = mybir.dt.uint16
ALU = mybir.AluOpType
ACT = mybir.ActivationFunctionType
AX = mybir.AxisListType

P = 128
D = 2048
KT = D // P
SEQ, META = 256, 16
T = SEQ + META
Q0 = META - 2
TILES = [(0, META), (META, P), (META + P, P)]
EPS = 1e-6
GRID_W, WIN_W, WIN_H, ROWS = 64, 16, 8, SEQ // 64
NA_HEADS, ML_HEADS, GLA_HEADS = 8, 4, 4
NA_UNITS = 2 * NA_HEADS
NA_SCALE = 128 ** -0.5
ML_SCALE = 128 ** -0.5
GLA_SCALE = 256 ** -0.5
GLA_TAU = 16.0
D_FF = 5632
FT = D_FF // P
PARTS = [16, 14, 14]
RANK = 16
NEG = -1.0e30
AB_COLS, C_COLS = 48 * P, 48 * P
GATES, LRS = 16, 2 * RANK

V_MIX, V_FFN, V_ML, V_GLA, V_QG, V_KG, V_GB = 0, 32, 64, 72, 88, 89, 90
V_N = 106

LEVELS = [("in", H) for H in (1, 2, 4, 8, 16, 32, 64)] + [("edge", META), ("edge", META + P)]
NL = len(LEVELS)


class Chain:

    def __init__(self, eng, sem):
        self.eng, self.sem, self.n, self.off = eng, sem, 0, 0

    def link(self, ins):
        ins.then_inc(self.sem, 1)
        self.n += 1
        self.eng.wait_ge(self.sem, self.off + self.n)

    def mark(self, ins):
        ins.then_inc(self.sem, 1)
        self.n += 1
        return self.n

    def wait(self, n):
        self.eng.wait_ge(self.sem, self.off + n)

    def enter(self, rounds_before, per):
        self.off = rounds_before * per if per else 0

    def leave(self, rounds, per):
        self.off = 0
        self.n += (rounds - 1) * per


def build(nc, x, meta_tokens, norm_mix, norm_ffn, ab_w_in, ab_gate_bias, ab_q_gain, ab_k_gain,
          ab_rel_bias, ab_ml_gain, ab_w_out, c_w_in, c_gate_up, c_gate_bias, c_head_gain, c_w_out,
          ffn_w_up, ffn_conv_w, ffn_conv_b, ffn_w_down, out):
    gemms = []
    state = {"it": 0, "gr": 0}

    def add(name, w, ks, iters, evac, row0=0, col0=0, x0=0, t0=0, **kw):
        ng = 8 // len(ks)
        gemms.append(dict(name=name, w=w, row0=row0, ks=ks, ng=ng, gs=len(ks), iters=iters, col0=col0, evac=evac,
                          x0=x0, t0=t0, it0=state["it"], gr0=state["gr"], **kw))
        state["it"] += iters
        state["gr"] += iters * ng

    full, half = [4, 4, 4, 4], [4, 4]
    add("ml_in", ab_w_in[0], full, 6, "store", col0=24 * P, p0=24, ready=0)
    add("na_in", ab_w_in[0], full, 6, "store", p0=0, ready=0)
    add("ml_out", ab_w_out[0], half, 2, "resid", row0=8, ready=16)
    add("na_out", ab_w_out[0], half, 2, "resid", x0=8, ready=24)

    def ffn(layer, ready, up_t0, down_t0):
        f0 = 0
        for part, nt in enumerate(PARTS):
            add(f"up{layer}{part}", ffn_w_up[layer], full, nt // 2, "conv", col0=f0 * P, t0=up_t0,
                layer=layer, f0=f0, ready=ready)
            add(f"down{layer}{part}", ffn_w_down[layer], full if nt == 16 else [4, 4, 3, 3], 4, "resid",
                row0=f0, t0=down_t0, mid=True)
            f0 += nt

    ffn(0, 32, 0, 0)
    add("q_in", c_w_in[0], full, 2, "store", p0=0, ready=48, t0=Q0)
    add("k_in", c_w_in[0], full, 2, "store", col0=8 * P, p0=8, ready=48)
    add("v_in", c_w_in[0], full, 4, "v", col0=16 * P, ready=48)
    add("r_in", c_w_in[0], full, 4, "store", col0=32 * P, p0=32, ready=48, t0=Q0)
    add("gl_out0", c_w_out[0], half, 2, "resid", ready=64, t0=Q0)
    add("gl_out1", c_w_out[0], half, 2, "resid", row0=8, x0=8, ready=72, t0=Q0)
    ffn(1, 80, Q0, META)
    G = {g["name"]: g for g in gemms}
    conv_it = 0
    for g in gemms:
        g["c0"] = conv_it
        if g["evac"] == "conv":
            conv_it += g["iters"]
    for g, before in zip(gemms[1:], gemms):
        if g.get("mid"):
            g["c0"] = before["c0"]
    for a, b in zip(gemms, gemms[1:] + [None]):
        a["next"] = b

    ctx = ExitStack()
    with ctx:
        place = {"at": 16512}

        def sb(name, shape, dt=F32, at=None):
            size = int(np.prod(shape[1:])) * (2 if dt in (BF16, U16) else 4)
            if at is None:
                at = place["at"]
                place["at"] = (at + size + 31) // 32 * 32
            assert at + size <= 229344, (name, at, size)
            return nc.alloc_sbuf_tensor_at(name, shape, dt, offset=at)

        h = sb("h", [P, KT, T])
        act_hi = sb("act_hi", [P, KT, T], F32R)
        act_lo = sb("act_lo", [P, KT, T], F32R)
        raw = sb("raw", [P, 4, 4 * 256])
        w_hi = sb("w_hi", [P, 4, 4 * 256], F32R)
        w_lo = sb("w_lo", [P, 4, 4 * 256], F32R)
        ident = sb("ident", [P, P])
        ones = sb("ones", [P, P])
        vec = sb("vec", [P, V_N])
        conv = sb("conv", [P, 2, 4, 2 * FT])
        tail_w = sb("tail_w", [P, KT, GATES + LRS])
        tail = sb("tail", [LRS, T])
        gate_b = sb("gate_b", [GATES, 1])
        eps = sb("eps", [P, 2])
        ntmp = sb("ntmp", [P, 4, T])
        rstd = sb("rstd", [P, T])
        zone = place["at"]
        TB = T * 4
        proj = sb("proj", [P, 48, T], at=zone)
        v_tok = sb("v_tok", [P, 3, D], at=zone + 48 * TB)
        M = zone + 48 * TB + 3 * D * 4
        row_c = sb("row_c", [ML_HEADS, 2, T], at=M)
        row_f = sb("row_f", [ML_HEADS, 2, T], at=M + 2 * TB)
        row_l = sb("row_l", [ML_HEADS, 2, T], at=M + 4 * TB)
        row_b = sb("row_b", [ML_HEADS, 2, T], at=M + 6 * TB)
        row_m = sb("row_m", [ML_HEADS, 2, T], at=M + 8 * TB)
        ml_x = sb("ml_x", [P, 2, T], at=M + 2 * TB)
        ml_p = sb("ml_p", [P, 2, T], at=M + 4 * TB)
        ml_ptt = sb("ml_ptt", [P, 2, T], at=M + 6 * TB)
        ml_ptm = sb("ml_ptm", [META, T], at=M + 8 * TB)
        ml_sum = sb("ml_sum", [P, T], at=M + 9 * TB)
        e_sq = sb("e_sq", [P, 2, T], at=M)
        e_rr = sb("e_rr", [P, T], at=M + 16 * TB)
        SW = META + 2 * P + P + META
        strip = sb("strip", [P, 2, SW], at=M + 10 * TB)
        selrow = sb("selrow", [ML_HEADS, ML_HEADS, P], at=M + 10 * TB + 2 * SW * 4)
        cols = sb("cols", [P, 3, 2, 2, ML_HEADS], at=M + 10 * TB + 2 * SW * 4 + 2048)
        den = sb("den", [P, 8], at=M + 10 * TB + 2 * SW * 4 + 2048 + 192)
        y_ml = sb("y_ml", [P, 8, T], at=zone + 32 * TB)
        q_rev = sb("q_rev", [P, NA_HEADS, T], at=zone + 24 * TB)
        sq2 = sb("sq2", [P, 2, T], at=M + 2 * TB)
        rt2 = sb("rt2", [P, 2, T], at=M + 4 * TB)
        na_s = sb("na_s", [P, 2, T], at=M + 6 * TB)
        na_p = sb("na_p", [P, 2, T], at=M + 8 * TB)
        pt = sb("pt", [P, 2, 2, T], at=zone + 40 * TB)
        bias = sb("bias", [P, 4, T], at=zone + 44 * TB)
        pt_m = sb("pt_m", [META, 2, T], at=M + 14 * TB)
        na_m = sb("na_m", [META, NA_HEADS, META], at=M + 16 * TB)
        na_mt = sb("na_mt", [META, NA_HEADS, META], at=M + 16 * TB + NA_HEADS * META * 4)
        col = sb("col", [P, 64], at=M)
        winmask = sb("winmask", [P, GRID_W], at=M + 256)
        bc = sb("bc", [P, 2, 8, T], at=zone + 16 * TB)
        gup = sb("gup", [LRS, 2, 8 * P], at=zone + 32 * TB)
        ge = sb("ge", [P, 2, T], at=zone + 40 * TB)
        gl_e = sb("gl_e", [P, 2, 2, 2, T], at=M)
        at_t = sb("at_t", [P, 2, 2, T], at=M + 8 * TB)
        at_m = sb("at_m", [META, 2, T], at=M + 12 * TB)
        lmask = sb("lmask", [P, 7, P], BF16, at=M + 14 * TB)
        MT = max(PARTS)
        g_hi = sb("g_hi", [P, MT, T], F32R, at=zone)
        g_lo = sb("g_lo", [P, MT, T], F32R, at=zone + MT * TB)
        acc = sb("acc", [P, 2, 2, T], at=zone + 2 * MT * TB)
        sg = sb("sg", [P, 2, T], at=zone + (2 * MT + 4) * TB)
        gp = sb("gp", [P, 2, T], at=zone + (2 * MT + 6) * TB)
        un = sb("un", [P, 2, 2, T], at=zone + (2 * MT + 8) * TB)
        sq = sb("sq", [P, KT, T], at=zone + 48 * TB)
        tok = sb("tok", [P, 3, D], at=zone)
        stage = sb("stage", [P, 9, P], at=M)
        ostage = sb("ostage", [P, 2, D], at=zone + 48 * TB)

        ps = ctx.enter_context(nc.psum_tensor("ps", [P, 8, 512], F32))
        pm = [ps[:, 4 + b, :] for b in range(4)]

        names = {}

        def S(name):
            if name not in names:
                names[name] = ctx.enter_context(nc.semaphore(name))
            return names[name]

        landed = [S(f"weights_landed{j}") for j in range(4)]
        all_sems = """const_done param_in conv_in tail_in gup_in hi_done split_done used bank_free u_ready conv_mid gates_done
            silu_done mid_done mid_split act_chain dve_chain pool_chain xT_done h_built par_done par_evac
            sq_ready sq_added ss_ready rt_ready rs_ready x_hi act_ready n_ready tail_scaled tail_done tail_evac
            vt_done vt_copied qk_sq qk_ss qk_rt qk_ready bias_ready
            na_scores na_biased na_max na_exp na_norm na_ptdone na_ptcopied na_pv na_stored mask_done
            nm_scores nm_max nm_exp nm_norm nm_ptdone nm_ptcopied
            ml_sel ml_c ml_cbk ml_ln ml_nm ml_en ml_cols ml_colc ml_cb ml_scores ml_x_done ml_w_done ml_pn ml_used
            ml_ptdone ml_ptcopied ml_pv ml_stored ml_made po_sq po_ss po_rt po_gate
            gu_mm gu_x gu_ln b_done gl_dsub gl_psub gl_exp gl_dmul gl_pmul gl_g gl_cp gl_pv gl_stored
            lmask_done out_done out_evac out_sent sel_done""".split()
        for n in all_sems:
            S(n)

        def bcast(ap, n, at=1):
            dims = [list(v) for v in ap.ap]
            dims.insert(at, [0, n])
            return bass.AP(ap.tensor, ap.offset, dims)

        def strided(ap, dims):
            return bass.AP(ap.tensor, ap.offset, [list(ap.ap[0])] + dims)

        units = [(hd, l) for hd in range(GLA_HEADS) for l in [None] + list(range(NL))]
        UH = 1 + NL
        level_units = [u for u in range(len(units)) if units[u][1] is not None]

        def level_span(l):
            kind, H = LEVELS[l]
            if kind == "in":
                return (0, T) if H <= 8 else (META, T)
            return (0, META + P) if H == META else (0, T)

        def halves(ap, l, d, side):
            kind, H = LEVELS[l]
            t0, t1 = level_span(l)
            right = (side == "q") != (d == 1)
            r = H if d else H - 1
            if kind == "in":
                v = ap[:, :, t0:t1].rearrange("p a (g b) -> p a g b", b=2 * H)
                return (v[:, :, :, H:2 * H] if right else v[:, :, :, 0:H]), v[:, :, :, r:r + 1]
            return (ap[:, :, H:t1] if right else ap[:, :, 0:H]), ap[:, :, r:r + 1]

        def level_sub(v, d, side):
            hd, l = units[level_units[v]]
            b, ref = halves(bc[:, d, 2 * hd:2 * hd + 2, :], l, d, side)
            o, _ = halves(gl_e[:, v % 2, 0 if side == "q" else 1, :, :], l, d, side)
            dims = [list(v_) for v_ in ref.ap]
            dims[-1] = [0, b.shape[-1]]
            return o, b, bass.AP(ref.tensor, ref.offset, dims)

        def level_mul(v, side):
            hd, l = units[level_units[v]]
            t0, t1 = level_span(l)
            base = 2 * hd if side == "q" else 8 + 2 * hd
            return gl_e[:, v % 2, 0 if side == "q" else 1, :, t0:t1], proj[:, base:base + 2, t0:t1]

        def o_tile(n):
            hd, e = n // 4, n % 4
            return proj[:, (2 * hd + e) if e < 2 else (8 + 2 * hd + e - 2), :]

        E_ML, E_NA = list(range(32, 40)), list(range(16, 24))

        GL_TICKS = 80
        UNITS_AT = [([u - 1] if units[u - 1][1] is None else []) + [u] for u in level_units]
        GL_VT = {4 * (k + 1): (2 * k, 2 * k + 1) for k in range(8)}
        WEIGH = {9: 0, 10: 1, 11: 2, 13: 3, 18: 4, 19: 5, 21: 6, 22: 7, 27: 8, 29: 9, 30: 10, 31: 11,
                 36: 12, 37: 13, 38: 14, 39: 15}
        SQUARE = {14: 0, 23: 1, 34: 2, 41: 3}
        SILU = {42: 0, 48: 1, 56: 2, 64: 3}
        MAKE = {t0 + k: n0 + k for t0, n0 in ((44, 0), (50, 4), (57, 8), (65, 12)) for k in range(4)}
        HIGH = {61: range(0, 4), 62: range(4, 8), 66: (8, 9), 67: (10, 11), 69: (12, 13), 70: (14, 15)}

        def before(t, table):
            return sum((len(v) if isinstance(v, tuple) else 1) for q, v in table.items() if q < t)

        NORM_V = [V_MIX, V_FFN, V_MIX + KT, V_FFN + KT]
        NORM_READY = [0, 32, 48, 80]
        NORM_EARLY = [0, 8, 12, 8]
        NORM_BEFORE = [None, "na_out", "down02", "gl_out1"]
        VT_COL = [1024 + P * n for n in range(8)] + [P * n for n in range(8)] + [P * n for n in range(16)]
        EVEN_TICKS = 72
        EVEN_VT = {2: ((0, 2), (1, 3)), 3: ((2, 2), (3, 3)), 4: ((4, 2),), 5: ((5, 3),), 6: ((6, 2),), 7: ((7, 3),),
                   48: ((8, 0), (9, 1)), 49: ((10, 0), (11, 1)), 57: ((12, 3),), 59: ((13, 3),), 61: ((14, 3),), 63: ((15, 3),)}
        CB0 = 5
        MIX0, UNIT, PER_HEAD = 9, 2, 6
        QK0 = 33
        BIAS0 = 44
        META0, NA0 = 51, 52
        Y_SPLIT = {53: range(0, 4), 54: range(4, 8)}

        def at_tick(t, start, every, count):
            n = (t - start) // every
            return n if (t - start) % every == 0 and 0 <= n < count else None

        def cb(hd, d):
            k = 2 * hd + d
            return v_tok[:, k // 3, (k % 3) * T:(k % 3 + 1) * T]

        def advance(side):
            next(side, None)

        def finish(side):
            for _ in side:
                pass

        block = ctx.enter_context(nc.Block())

        @block.sync
        def _(sp):
            def fetch(g, i, s, wait=True):
                n = g["w"].shape[1]
                grp, c = s // g["gs"], s % g["gs"]
                kc = g["ks"][c]
                if wait:
                    sp.wait_ge(S("split_done"), (i + g["it0"]) * 8 + (s - 3))
                row = (g["row0"] + sum(g["ks"][:c])) * P
                if g["evac"] == "conv":
                    off, step = g["col0"] + grp * D_FF, 256
                else:
                    off, step = g["col0"] + grp * 256, g["ng"] * 256
                src = bass.AP(g["w"].tensor, g["w"].offset + row * n + off + i * step,
                              [[n, P], [n * P, kc], [1, 256]])
                dst = raw[:, s % 4, 0:kc * 256].rearrange("p (k c) -> p k c", k=kc)
                sp.dma_start(dst, src).then_inc(landed[s % 4], 16)

            for q in range(4):
                c0 = q * 512
                sp.dma_start(tok[0:META, 0, c0:c0 + 512], meta_tokens[:, c0:c0 + 512]).then_inc(S(f"tok_in{q}"), 16)
                sp.dma_start(tok[:, 1:3, c0:c0 + 512],
                             bass.AP(x.tensor, x.offset + c0, [[D, P], [P * D, 2], [1, 512]])).then_inc(S(f"tok_in{q}"), 16)
                fetch(gemms[0], 0, q, wait=False)
            for s in range(4, 8):
                fetch(gemms[0], 0, s)
            for g in gemms:
                with sp.Fori(1 if g["it0"] == 0 else 0, g["iters"]) as i:
                    for s in range(8):
                        fetch(g, i, s)
            for n in range(8):
                q, b = n // 2, n % 2
                sp.wait_ge(S("out_evac"), n + 1)
                sp.dma_start(out[0, b * P:(b + 1) * P, 512 * q:512 * (q + 1)],
                             ostage[:, b, 512 * q:512 * (q + 1)]).then_inc(S("out_sent"), 16)
            sp.wait_ge(S("out_sent"), 16 * 8)

        @block.gpsimd
        def _(pool):
            chain = Chain(pool, S("pool_chain"))
            g_ = nc.gpsimd
            chain.link(g_.memset(ident[:, :], 0.0))
            g_.affine_select(out=ident[:, :], in_=ident[:, :], compare_op=ALU.not_equal, fill=1.0, base=0,
                             pattern=[[-1, P]], channel_multiplier=1).then_inc(S("const_done"), 1)

            def norm(n):
                pool.wait_ge(S("sq_ready"), 4 * n + 1)
                for q in range(1, 4):
                    pool.wait_ge(S("sq_ready"), 4 * n + q + 1)
                    g_.tensor_tensor(sq[:, 0:4, :], sq[:, 0:4, :], sq[:, 4 * q:4 * q + 4, :], ALU.add).then_inc(S("sq_added"), 1)
                    pool.wait_ge(S("sq_added"), 3 * n + q)

            norm(0)
            pool.wait_ge(S("act_ready"), KT)
            pool.wait_ge(S("ss_ready"), 1)
            chain.link(g_.memset(strip[:, :, :], 0.0))
            for d in range(2):
                sgn = 1 - 2 * d
                g_.affine_select(out=strip[:, d, :], in_=strip[:, d, :], compare_op=ALU.is_ge, fill=NEG,
                                 base=sgn * (META + P), pattern=[[-sgn, SW]],
                                 channel_multiplier=sgn).then_inc(S("mask_done"), 1)
            chain.link(g_.memset(selrow[:, :, :], 0.0))
            g_.affine_select(out=selrow[:, :, :], in_=selrow[:, :, :], compare_op=ALU.not_equal, fill=1.0, base=0,
                             pattern=[[-1, ML_HEADS], [0, P]], channel_multiplier=1).then_inc(S("sel_done"), 1)

            pool.wait_ge(S("ml_made"), 8)
            chain.link(g_.memset(winmask[:, :], 0.0))
            for half_ in range(2):
                w = winmask[64 * half_:64 * half_ + 64, 0:GRID_W - WIN_W]
                chain.link(g_.affine_select(out=w, in_=w, compare_op=ALU.is_ge, fill=NEG,
                                            base=WIN_W // 2 - (GRID_W - 1), pattern=[[1, GRID_W - WIN_W]],
                                            channel_multiplier=1))
                w = winmask[64 * half_:64 * half_ + 64, WIN_W:GRID_W]
                chain.link(g_.affine_select(out=w, in_=w, compare_op=ALU.is_gt, fill=NEG,
                                            base=(GRID_W - 1) + WIN_W // 2 - WIN_W, pattern=[[-1, GRID_W - WIN_W]],
                                            channel_multiplier=-1))
            for b in range(4):
                chain.link(g_.memset(bias[:, b, 0:META], 0.0))
            for n in range(2 * NA_HEADS):
                pool.wait_ge(S(f"bias_in{n % 4}"), 32 * (n // 4 + 1))
                b = bias[:, n % 4, META:T].rearrange("p (r c) -> p r c", r=ROWS)
                g_.tensor_tensor(b, b, bcast(winmask[:, :], ROWS), ALU.add).then_inc(S("bias_ready"), 1)
            norm(1)

            for l in range(7):
                H = LEVELS[l][1]
                m = lmask[:, l, :]
                for d in range(2):
                    hf = m.rearrange("p (g b) -> p g b", b=2 * H)[:, :, (0 if d else H):(H if d else 2 * H)]
                    lo = H if d else 0
                    chain.link(g_.memset(hf, 1.0))
                    chain.link(g_.affine_select(out=hf, in_=hf, compare_op=ALU.is_ge, fill=0.0, base=-lo,
                                                pattern=[[-2 * H, P // (2 * H)], [0, H]], channel_multiplier=1))
                    g_.affine_select(out=hf, in_=hf, compare_op=ALU.is_ge, fill=0.0, base=lo + H - 1,
                                     pattern=[[2 * H, P // (2 * H)], [0, H]],
                                     channel_multiplier=-1).then_inc(S("lmask_done"), 1)
            norm(2)

            pool.wait_ge(S("b_done"), 8)
            def sub(v):
                if v >= 2:
                    pool.wait_ge(S("gl_g"), level_units[v - 2] + 1)
                for d in range(2):
                    o, b, r = level_sub(v, d, "k")
                    ins = g_.tensor_tensor(o, r, b, ALU.subtract)
                ins.then_inc(S("gl_psub"), 1)

            sub(0)
            for v in range(len(level_units)):
                if v + 1 < len(level_units):
                    sub(v + 1)
                pool.wait_ge(S("gl_exp"), v + 1)
                e, k_ = level_mul(v, "k")
                g_.tensor_tensor(e, e, k_, ALU.mult).then_inc(S("gl_pmul"), 1)
            norm(3)

        @block.scalar
        def _(act):
            chain = Chain(act, S("act_chain"))
            A = nc.scalar.activation

            rows_of = [(norm_mix, 32), (norm_ffn, 32), (ab_ml_gain, 8), (c_head_gain, 16),
                       (ab_q_gain, 1), (ab_k_gain, 1), (c_gate_bias, 16)]
            at = 0
            for v, n in rows_of:
                act.dma_start(stage[at:at + n, 8, :], bass.AP(v.tensor, v.offset, [[P, n], [1, P]])).then_inc(S("param_in"), 16)
                at += n

            def load_more():
                act.dma_start(gate_b[:, :], ab_gate_bias.rearrange("a g -> g a")).then_inc(S("tail_in"), 16)
                for w, c0, n, o in ((ab_w_in[0], AB_COLS, GATES, 0), (c_w_in[0], C_COLS, LRS, GATES)):
                    act.dma_start(tail_w[:, :, o:o + n], bass.AP(w.tensor, w.offset + c0,
                                  [[w.shape[1], P], [w.shape[1] * P, KT], [1, n]])).then_inc(S("tail_in"), 16)
                for layer in range(2):
                    for tap in range(4):
                        v = ffn_conv_w[layer, tap] if tap < 3 else ffn_conv_b[layer]
                        act.dma_start(stage[0:2 * FT, 4 * layer + tap, :],
                                      v.rearrange("(m p) -> m p", p=P)).then_inc(S("conv_in"), 16)

            def hi(g, it, s):
                n = it + g["it0"]
                kc = g["ks"][s % g["gs"]]
                act.wait_ge(landed[s % 4], n * 32 + 16 * (s // 4 + 1))
                act.wait_ge(S("used"), n * 8 + (s - 3))
                A(w_hi[:, s % 4, 0:kc * 256], raw[:, s % 4, 0:kc * 256], ACT.Copy).then_inc(S("hi_done"), 1)

            def evac(g, i, grp):
                if g["evac"] != "conv":
                    return
                c = i + g["c0"]
                o0 = META if g["t0"] else 0
                if grp == 0 and not (isinstance(c, int) and c == 0):
                    act.wait_ge(S("mid_done"), c * 2)
                act.wait_ge(S("u_ready"), c * 2 + (grp + 1))
                for m in range(2):
                    mt = i * 2 + (grp * FT + g["f0"] + m)
                    ins = A(acc[:, grp, m, o0:T], un[:, grp, m, o0:T], ACT.Identity,
                            bias=conv[:, g["layer"], 3, bass.ds(mt, 1)], scale=conv[:, g["layer"], 1, bass.ds(mt, 1)])
                ins.then_inc(S("conv_mid"), 1)
                if grp == 1:
                    act.wait_ge(S("gates_done"), c + 1)
                    A(sg[:, :, o0:T], acc[:, 0, :, o0:T], ACT.Silu).then_inc(S("silu_done"), 1)

            def gemm(g, first=None, beside=None, last_beside=None):
                def body(i, nxt, ni, side=None, late=False):
                    for s in range(8):
                        if side:
                            advance(side)
                        if s + 3 < 8:
                            hi(g, i, s + 3)
                        elif nxt:
                            hi(nxt, ni, s + 3 - 8)
                        if late:
                            if s >= 6:
                                evac(g, i, s - 6)
                        elif s % g["gs"] == g["gs"] - 1:
                            evac(g, i, s // g["gs"])

                last, start = g["iters"] - 1, 0
                if first:
                    body(0, g, 1, first, late=True)
                    finish(first)
                    start = 1
                if beside:
                    for i in range(start, last):
                        body(i, g, i + 1, beside)
                else:
                    with act.Fori(start, last) as i:
                        body(i, g, i + 1)
                body(last, g["next"], 0, beside or last_beside)

            def norm_high(n, k):
                v0 = NORM_V[n]
                if n == 0:
                    act.wait_ge(S("h_built"), k // 2 + 1)
                else:
                    act.wait_ge(S("bank_free"), 2 + G[NORM_BEFORE[n]]["gr0"] + k // 2 + 1)
                A(act_hi[:, k, :], h[:, k, :], ACT.Copy, scale=vec[:, v0 + k:v0 + k + 1]).then_inc(S("x_hi"), 1)

            def norm_early(n):
                for k in range(0, NORM_EARLY[n], 2):
                    norm_high(n, k)
                    norm_high(n, k + 1)
                    yield

            def norm(n):
                g = G[NORM_BEFORE[n]]
                act.wait_ge(S("used"), 8 * (g["it0"] + g["iters"]))
                for k in range(NORM_EARLY[n], KT):
                    norm_high(n, k)

            def norm_side(n):
                for q in range(4):
                    A(sq[:, 4 * q:4 * q + 4, :], h[:, 4 * q:4 * q + 4, :], ACT.Square).then_inc(S("sq_ready"), 1)
                    yield
                yield
                act.wait_ge(S("ss_ready"), n + 1)
                A(rstd[:, :], pm[0][:, 0:T], ACT.Sqrt, bias=eps[:, 0:1], scale=1.0 / D).then_inc(S("rt_ready"), 1)
                yield
                if n == 0:
                    yield
                    act.wait_ge(S("par_done"), 2)
                    flat = conv[:, :, :, :].rearrange("p a b c -> p (a b c)")
                    A(flat[:, 0:440], pm[2][:, 0:440], ACT.Copy)
                    A(flat[:, 440:704], pm[3][:, 0:264], ACT.Copy).then_inc(S("par_evac"), 1)
                    yield

            def vt_copy(n, b):
                act.wait_ge(S("vt_done"), n + 1)
                c = VT_COL[n]
                A(v_tok[0:META, 0, c:c + P], pm[b][0:META, 2 * P:3 * P], ACT.Copy)
                A(v_tok[:, 1:3, c:c + P], strided(pm[b], [[P, 2], [1, P]]), ACT.Copy).then_inc(S("vt_copied"), 1)

            def load_bias(n):
                hd, qt = n // 2, n % 2
                if n >= 4:
                    act.wait_ge(S("na_biased"), n - 3)
                for rr in range(2):
                    r = 2 * qt + 1 - rr
                    dst = bias[64 * rr:64 * rr + 64, n % 4, META:T].rearrange("p (r c) -> p r c", r=ROWS)
                    off = ab_rel_bias.offset + hd * 15 * 31 + (WIN_H - 1 - r) * 31 + (WIN_W - 1) - (GRID_W - 1)
                    act.dma_start(dst, bass.AP(ab_rel_bias.tensor, off, [[1, GRID_W], [31, ROWS], [1, GRID_W]])).then_inc(S(f"bias_in{n % 4}"), 16)

            qk = proj[:, 0:16, :].rearrange("p (g h) t -> p g h t", h=NA_HEADS)

            def even():
                M_ = ML_HEADS
                for t in range(EVEN_TICKS):
                    for n, b in EVEN_VT.get(t - 1, ()):
                        vt_copy(n, b)
                    if t == 1:
                        act.wait_ge(S("ml_sel"), 1)
                        for j in range(4):
                            ins = A((row_f if j % 2 else row_c)[:, j // 2, :], pm[j][0:M_, 0:T], ACT.Copy)
                        chain.link(ins)
                        chain.link(A(row_l[:, :, :], row_f[:, :, :], ACT.Abs))
                        chain.link(A(row_l[:, :, :], row_l[:, :, :], ACT.Exp, scale=-1.0))
                        A(row_l[:, :, :], row_l[:, :, :], ACT.Ln, bias=1.0).then_inc(S("ml_ln"), 1)
                    if t == 3:
                        act.wait_ge(S("ml_nm"), 1)
                        A(row_f[:, :, :], row_l[:, :, :], ACT.Exp).then_inc(S("ml_en"), 1)
                    if t == 5:
                        act.wait_ge(S("ml_cols"), 1)
                        A(cols[:, 1:3, :, :, :].rearrange("p a b c d -> p (a b c d)"), pm[0][:, 16:48], ACT.Copy)
                        A(cols[0:META, 0, :, :, :].rearrange("p b c d -> p (b c d)"), pm[0][0:META, 0:16],
                          ACT.Copy).then_inc(S("ml_colc"), 1)
                    hd = at_tick(t, CB0 + 1, 1, M_)
                    if hd is not None:
                        act.wait_ge(S("ml_cb"), hd + 1)
                        for d in range(2):
                            ins = A(cb(hd, d), pm[d][:, 0:T], ACT.Copy)
                        ins.then_inc(S("ml_cbk"), 1)
                    u = at_tick(t, MIX0 + 3, UNIT, 3 * M_)
                    if u is not None:
                        t0, tn = TILES[u % 3]
                        act.wait_ge(S("ml_ptdone"), u + 1)
                        if u % 3 == 0 and u:
                            act.wait_ge(S("ml_pv"), u // 3)
                        A(ml_ptm[:, t0:t0 + tn], pm[3][0:META, 2 * P:2 * P + tn], ACT.Copy)
                        A(ml_ptt[:, :, t0:t0 + tn], strided(pm[3], [[P, 2], [1, tn]]), ACT.Copy).then_inc(S("ml_ptcopied"), 1)
                    hd = at_tick(t, MIX0 + 9, PER_HEAD, M_)
                    if hd is not None:
                        act.wait_ge(S("ml_pv"), hd + 1)
                        A(y_ml[:, 2 * hd:2 * hd + 2, :], ps[:, 4:6, 0:T], ACT.Copy).then_inc(S("ml_stored"), 1)
                        act.wait_ge(S("ml_stored"), hd + 1)
                        if hd:
                            act.wait_ge(S("po_ss"), hd)
                        A(e_sq[:, :, :], y_ml[:, 2 * hd:2 * hd + 2, :], ACT.Square).then_inc(S("po_sq"), 1)
                        act.wait_ge(S("bank_free"), 2 + G["na_in"]["gr0"])
                        o_ = proj[:, 40 + 2 * hd:42 + 2 * hd, :]
                        A(o_, o_, ACT.Sigmoid).then_inc(S("po_gate"), 1)
                    hd = at_tick(t, MIX0 + 10, PER_HEAD, M_)
                    if hd is not None:
                        act.wait_ge(S("po_ss"), hd + 1)
                        if hd:
                            act.wait_ge(S("ml_made"), 2 * hd)
                        A(e_rr[:, :], pm[0][:, 0:T], ACT.Sqrt, bias=eps[:, 0:1], scale=1.0 / 256).then_inc(S("po_rt"), 1)
                    u = at_tick(t, MIX0, UNIT, 3 * M_)
                    if u is not None:
                        tn = TILES[u % 3][1]
                        act.wait_ge(S("ml_x_done"), u + 1)
                        A(ml_x[0:tn, :, :], ml_x[0:tn, :, :], ACT.Exp).then_inc(S("ml_w_done"), 1)
                    k = at_tick(t, QK0 + 2, 2, NA_HEADS)
                    if k is not None:
                        act.wait_ge(S("qk_ss"), k + 1)
                        if k:
                            act.wait_ge(S("qk_ready"), k)
                        A(rt2[:, :, :], ps[:, 6:8, 0:T], ACT.Sqrt, bias=eps[:, 0:1], scale=1.0 / P).then_inc(S("qk_rt"), 1)
                    k = at_tick(t, QK0, 2, NA_HEADS)
                    if k is not None:
                        act.wait_ge(S("ml_used"), 3 * M_)
                        act.wait_ge(S("bank_free"), 2 + G["na_in"]["gr0"] + 4 + k // 2 + 1)
                        A(sq2[:, :, :], qk[:, :, k, :], ACT.Square).then_inc(S("qk_sq"), 1)
                    n = at_tick(t, BIAS0, 1, 4)
                    if n is not None:
                        if n == 0:
                            act.wait_ge(S("ml_made"), 8)
                        load_bias(n)
                    if t == META0 + 1:
                        act.wait_ge(S("nm_max"), 1)
                        A(na_m[:, :, :], na_m[:, :, :], ACT.Exp).then_inc(S("nm_exp"), 1)
                    if t == META0 + 2:
                        act.wait_ge(S("nm_ptdone"), 1)
                        A(na_mt[:, :, :], pm[3][0:META, P:2 * P], ACT.Copy).then_inc(S("nm_ptcopied"), 1)
                        act.wait_ge(S("nm_ptcopied"), 1)
                    n = at_tick(t, NA0 + 3, 1, NA_UNITS)
                    if n is not None:
                        hd, qt = n // 2, n % 2
                        t0 = TILES[1 + qt][0]
                        act.wait_ge(S("na_ptdone"), n + 1)
                        if hd >= 2:
                            act.wait_ge(S("na_pv"), hd - 1)
                        if qt == 0:
                            A(pt_m[:, hd % 2, 0:META], na_mt[:, hd, :], ACT.Copy)
                        A(pt_m[:, hd % 2, t0:t0 + P], pm[2][0:META, 2 * P:3 * P][:, ::-1], ACT.Copy)
                        A(pt[:, hd % 2, :, t0:t0 + P], strided(pm[2][:, P - 1:P], [[P, 2], [-1, P]]),
                          ACT.Copy).then_inc(S("na_ptcopied"), 1)
                    hd = at_tick(t, NA0 + 5, 2, NA_HEADS)
                    if hd is not None:
                        act.wait_ge(S("na_pv"), hd + 1)
                        if hd >= 4:
                            act.wait_ge(S("act_ready"), 24 + hd - 3)
                        A(ntmp[:, hd % 4, :], pm[3][:, 0:T], ACT.Copy).then_inc(S("na_stored"), 1)
                        act.wait_ge(S("na_stored"), hd + 1)
                        A(act_hi[:, 8 + hd, :], ntmp[:, hd % 4, :], ACT.Copy).then_inc(S("x_hi"), 1)
                    n = at_tick(t, NA0 + 1, 1, NA_UNITS)
                    if n is not None:
                        act.wait_ge(S("na_max"), n + 1)
                        if n >= 2:
                            act.wait_ge(S("na_ptdone"), n - 1)
                        A(na_p[:, n % 2, :], na_s[:, n % 2, :], ACT.Exp, bias=col[:, n % 2:n % 2 + 1],
                          accum_out=col[:, 2 + n % 2:3 + n % 2]).then_inc(S("na_exp"), 1)
                        if n + 4 < NA_UNITS:
                            load_bias(n + 4)
                    for k in Y_SPLIT.get(t, ()):
                        act.wait_ge(S("used"), 8 * (G["ml_out"]["it0"] - 1) + 5 + k // 4)
                        act.wait_ge(S("ml_made"), k + 1)
                        A(act_hi[:, k, :], y_ml[:, k, :], ACT.Copy).then_inc(S("x_hi"), 1)
                    yield

            act.wait_ge(S("const_done"), 3)
            for k in range(0, KT, 2):
                act.wait_ge(S("xT_done"), k + 2)
                A(h[:, k:k + 2, :], ps[:, k % 4:k % 4 + 2, 0:T], ACT.Copy).then_inc(S("h_built"), 1)
                if k == 2:
                    act.wait_ge(S("par_done"), 1)
                    A(vec[:, :], pm[0][:, 0:V_N], ACT.Copy).then_inc(S("par_evac"), 1)
                    act.wait_ge(S("par_evac"), 1)
                    norm_high(0, 0)
                    norm_high(0, 1)
                if k:
                    norm_high(0, k)
                    norm_high(0, k + 1)
                if k % 4 == 2 and k < 12:
                    s = k // 4
                    act.wait_ge(landed[s], 16)
                    A(w_hi[:, s, :], raw[:, s, :], ACT.Copy).then_inc(S("hi_done"), 1)
                if k == 2:
                    load_more()
            mixers = even()
            gemm(G["ml_in"], first=norm_side(0), last_beside=mixers)
            gemm(G["na_in"], beside=mixers)
            gemm(G["ml_out"], beside=mixers)
            finish(mixers)
            gemm(G["na_out"], last_beside=norm_early(1))

            def ffn_stage(layer, n):
                norm(n)
                gemm(G[f"up{layer}0"], first=norm_side(n))
                gemm(G[f"down{layer}0"])
                gemm(G[f"up{layer}1"])
                gemm(G[f"down{layer}1"])
                gemm(G[f"up{layer}2"])

            ffn_stage(0, 1)
            gemm(G["down02"], last_beside=norm_early(2))
            norm(2)

            def gates_side():
                yield from norm_side(2)
                yield
                act.wait_ge(S("gup_in"), 1)
                for j in range(2):
                    act.dma_start(gup[RANK * j:RANK * (j + 1), j, :], c_gate_up[0, j]).then_inc(S("gup_in"), 16)
                yield

            def decays():
                for q in range(8):
                    j, k = q // 4, 2 * (q % 4)
                    yield
                    act.wait_ge(S("gu_mm"), q + 1)
                    if q:
                        act.wait_ge(S("b_done"), q)
                    for m in range(2):
                        n = 8 * j + k + m
                        ins = A(bc[:, j, k + m, :], pm[2 * (q % 2) + m][:, 0:T], ACT.Identity, bias=vec[:, V_GB + n:V_GB + n + 1])
                    ins.then_inc(S("gu_x"), 1)
                    act.wait_ge(S("gu_x"), q + 1)
                    chain.link(A(ge[:, :, :], bc[:, j, k:k + 2, :], ACT.Abs))
                    yield
                    chain.link(A(ge[:, :, :], ge[:, :, :], ACT.Exp, scale=-1.0))
                    A(ge[:, :, :], ge[:, :, :], ACT.Ln, bias=1.0).then_inc(S("gu_ln"), 1)
                    yield

            def gla():
                for t in range(GL_TICKS):
                    for n in GL_VT.get(t - 1, ()):
                        vt_copy(16 + n, 2 + n % 2)
                    if t - 1 in WEIGH:
                        n = WEIGH[t - 1]
                        act.wait_ge(S("gl_pv"), n + 1)
                        A(o_tile(n)[:, Q0:T], pm[2 + n % 2][:, Q0:T], ACT.Copy).then_inc(S("gl_stored"), 1)
                    if t in SILU:
                        hd = SILU[t]
                        act.wait_ge(S("bank_free"), 2 + G["v_in"]["gr0"] + 8 + 2 * (hd + 1))
                        g4 = proj[:, 32 + 4 * hd:36 + 4 * hd, Q0:T]
                        A(g4, g4, ACT.Silu).then_inc(S("po_gate"), 1)
                    if t in SQUARE:
                        hd = SQUARE[t]
                        act.wait_ge(S("gl_stored"), 4 * hd + 4)
                        for j in range(2):
                            b = 2 * hd if j == 0 else 8 + 2 * hd
                            ins = A(bc[:, j, 2 * hd:2 * hd + 2, Q0:T], proj[:, b:b + 2, Q0:T], ACT.Square, scale=GLA_SCALE)
                        ins.then_inc(S("po_sq"), 1)
                    if t - 1 in SQUARE:
                        hd = SQUARE[t - 1]
                        act.wait_ge(S("po_ss"), 4 + hd + 1)
                        A(bc[:, 0, 2 * hd, Q0:T], pm[2 + hd % 2][:, Q0:T], ACT.Sqrt, bias=eps[:, 1:2],
                          scale=1.0 / (512 * GLA_SCALE ** 2)).then_inc(S("po_rt"), 1)
                    for v in ((0, 1) if t == 0 else (t + 1,)):
                        if v < len(level_units):
                            t0, t1 = level_span(units[level_units[v]][1])
                            act.wait_ge(S("gl_dsub"), v + 1)
                            act.wait_ge(S("gl_psub"), v + 1)
                            e = gl_e[:, v % 2, :, :, t0:t1]
                            A(e, e, ACT.Exp, scale=1.0 / GLA_TAU).then_inc(S("gl_exp"), 1)
                    for k in HIGH.get(t, ()):
                        high(k)
                    yield

            def high(k):
                act.wait_ge(S("n_ready"), k + 1)
                act.wait_ge(S("used"), 8 * (G["gl_out0"]["it0"] - 1) + 5 + k // 4)
                A(act_hi[:, k, Q0:T], o_tile(k)[:, Q0:T], ACT.Copy).then_inc(S("x_hi"), 1)

            decay = decays()
            gemm(G["q_in"], first=gates_side(), beside=decay)
            gemm(G["k_in"], beside=decay)
            finish(decay)
            mixer = gla()
            gemm(G["v_in"], beside=mixer)
            gemm(G["r_in"], beside=mixer)
            gemm(G["gl_out0"], beside=mixer)
            finish(mixer)
            gemm(G["gl_out1"], last_beside=norm_early(3))
            ffn_stage(1, 3)

            def ending():
                for t in range(8 * 4 + 6):
                    for b in range(2):
                        q = at_tick(t, 8 + 2 + 2 * b, 8, 4)
                        if q is not None:
                            n = 2 * q + b
                            act.wait_ge(S("out_done"), n + 1)
                            A(ostage[:, b, 512 * q:512 * (q + 1)], pm[n % 4][:, :], ACT.Copy).then_inc(S("out_evac"), 1)
                    yield

            end = ending()
            gemm(G["down12"], beside=end)
            finish(end)

        @block.vector
        def _(dve):
            chain = Chain(dve, S("dve_chain"))
            V = nc.vector
            link = chain.link
            V.memset(ones[:, :], 1.0).then_inc(S("const_done"), 1)
            V.memset(eps[:, 0:1], EPS)
            V.memset(eps[:, 1:2], EPS / GLA_SCALE ** 2).then_inc(S("const_done"), 1)
            dve.sem_inc(S("bank_free"), 2)

            def lo(g, it, s):
                kc = g["ks"][s % g["gs"]]
                dve.wait_ge(S("hi_done"), (it + g["it0"]) * 8 + (s + 1))
                V.tensor_tensor(w_lo[:, s % 4, 0:kc * 256], raw[:, s % 4, 0:kc * 256],
                                w_hi[:, s % 4, 0:kc * 256].bitcast(F32), ALU.subtract).then_inc(S("split_done"), 1)

            def evac(g, i, grp):
                n = i + g["it0"]
                pair = grp % 2
                t0 = g["t0"]
                banks = ps[:, 2 * pair:2 * pair + 2, 0:T - t0]
                dve.wait_ge(S("used"), n * 8 + g["gs"] * (grp + 1))
                if g["evac"] == "resid":
                    hh = h[:, bass.ds(i * (2 * g["ng"]) + 2 * grp, 2), t0:T]
                    V.tensor_tensor(hh, banks, hh, ALU.add).then_inc(S("bank_free"), 1)
                    return
                rs = bcast(rstd[:, t0:T], 2)
                if g["evac"] == "v":
                    gi = g["ng"] * i + grp
                    if gi >= 2:
                        dve.wait_ge(S("vt_done"), 16 + 2 * gi - 2)
                    V.tensor_tensor(ntmp[:, 2 * (gi % 2):2 * (gi % 2) + 2, :], banks, rs, ALU.mult).then_inc(S("bank_free"), 1)
                    return
                if g["evac"] == "store":
                    o = proj[:, bass.ds(i * 4 + (g["p0"] + 2 * grp), 2), t0:T]
                    V.tensor_tensor(o, banks, rs, ALU.mult).then_inc(S("bank_free"), 1)
                    return
                c = i + g["c0"]
                o0 = META if t0 else 0
                b1 = max(o0, 1)
                V.tensor_tensor(un[:, grp, :, t0:T], banks, rs, ALU.mult).then_inc(S("u_ready"), 1)
                dve.wait_ge(S("u_ready"), c * 2 + (grp + 1))
                dve.sem_inc(S("bank_free"), 1)
                dve.wait_ge(S("conv_mid"), c * 2 + (grp + 1))
                wt = [conv[:, g["layer"], tap, :] for tap in range(4)]
                mt = [i * 2 + (grp * FT + g["f0"] + m) for m in range(2)]
                first_taps = []
                for m in range(2):
                    first_taps.append(chain.mark(V.scalar_tensor_tensor(
                        acc[:, grp, m, b1:T], un[:, grp, m, b1 - 1:T - 1], wt[0][:, bass.ds(mt[m], 1)],
                        acc[:, grp, m, b1:T], ALU.mult, ALU.add)))
                for m in range(2):
                    chain.wait(first_taps[m])
                    ins = V.scalar_tensor_tensor(acc[:, grp, m, o0:T - 1], un[:, grp, m, o0 + 1:T],
                                                 wt[2][:, bass.ds(mt[m], 1)], acc[:, grp, m, o0:T - 1], ALU.mult, ALU.add)
                if grp == 0:
                    ins.then_inc(S("gates_done"), 1)
                    dve.wait_ge(S("gates_done"), c + 1)
                    return
                link(ins)
                dve.wait_ge(S("silu_done"), c + 1)
                for m in range(2):
                    V.tensor_tensor(gp[:, m, o0:T], sg[:, m, o0:T], acc[:, 1, m, o0:T], ALU.mult).then_inc(S("mid_done"), 1)
                high = []
                for m in range(2):
                    dve.wait_ge(S("mid_done"), c * 2 + (m + 1))
                    high.append(chain.mark(V.tensor_copy(g_hi[:, bass.ds(i * 2 + m, 1), o0:T], gp[:, m:m + 1, o0:T])))
                for m in range(2):
                    k = bass.ds(i * 2 + m, 1)
                    chain.wait(high[m])
                    ins = V.tensor_tensor(g_lo[:, k, o0:T], gp[:, m:m + 1, o0:T], g_hi[:, k, o0:T].bitcast(F32), ALU.subtract)
                ins.then_inc(S("mid_split"), 1)
                dve.wait_ge(S("mid_split"), c + 1)

            def gemm(g, first=None, beside=None, last_beside=None):
                per = 7 if g["evac"] == "conv" else 0

                def body(i, nxt, ni, side=None, late=False):
                    for s in range(8):
                        if side:
                            advance(side)
                        if s + 3 < 8:
                            lo(g, i, s + 3)
                        elif nxt:
                            lo(nxt, ni, s + 3 - 8)
                        if late:
                            if s >= 6:
                                evac(g, i, s - 6)
                        elif s % g["gs"] == g["gs"] - 1:
                            evac(g, i, s // g["gs"])

                last, start = g["iters"] - 1, 0
                if first:
                    body(0, g, 1, first, late=True)
                    finish(first)
                    start = 1
                if beside:
                    for i in range(start, last):
                        body(i, g, i + 1, beside)
                else:
                    n0 = chain.n
                    with dve.Fori(start, last) as i:
                        chain.enter(i - start, per)
                        body(i, g, i + 1)
                    assert chain.n - n0 == per, (chain.n - n0, per)
                    chain.leave(last - start, per)
                body(last, g["next"], 0, beside or last_beside)

            def norm_low(n, k):
                v0, base = NORM_V[n], NORM_READY[n]
                dve.wait_ge(S("x_hi"), base + k + 1)
                V.scalar_tensor_tensor(act_lo[:, k, :], h[:, k, :], vec[:, v0 + k:v0 + k + 1], act_hi[:, k, :].bitcast(F32),
                                       ALU.mult, ALU.subtract).then_inc(S("act_ready"), 1)

            def norm_early(n):
                for k in range(0, NORM_EARLY[n], 2):
                    norm_low(n, k)
                    norm_low(n, k + 1)
                    yield

            def norm(n):
                for k in range(NORM_EARLY[n], KT):
                    norm_low(n, k)

            def norm_side(n):
                for t in range(5):
                    if t == 1 and n in (0, 2):
                        o, w = (0, GATES) if n == 0 else (GATES, LRS)
                        dve.wait_ge(S("tail_in"), 48)
                        V.tensor_tensor(tail_w[:, :, o:o + w], tail_w[:, :, o:o + w],
                                        bcast(vec[:, NORM_V[n]:NORM_V[n] + KT], w, 2), ALU.mult).then_inc(S("tail_scaled"), 1)
                    yield
                dve.wait_ge(S("rt_ready"), n + 1)
                V.reciprocal(rstd[:, :], rstd[:, :]).then_inc(S("rs_ready"), 1)
                dve.wait_ge(S("rs_ready"), n + 1)
                yield
                if n in (0, 2):
                    w = GATES if n == 0 else LRS
                    dve.wait_ge(S("tail_done"), n // 2 + 1)
                    ins = V.tensor_tensor(tail[0:w, :], pm[1][0:w, 0:T], rstd[0:w, :], ALU.mult)
                    if n == 0:
                        link(ins)
                        ins = V.tensor_scalar(tail[0:w, :], tail[0:w, :], gate_b[:, :], None, ALU.add)
                    ins.then_inc(S("tail_evac"), 1)
                    yield

            def turn(ap, d):
                return ap[:, d, ::-1] if d else ap[:, d, :]

            def mix_x(u):
                hd, tt = u // 3, u % 3
                t0, tn = TILES[tt]
                if u:
                    dve.wait_ge(S("ml_used"), u)
                dve.wait_ge(S("ml_cbk"), hd + 1)
                for d in range(2):
                    mk = strip[0:tn, d, META + P - t0:META + P - t0 + T]
                    ins = V.scalar_tensor_tensor(ml_x[0:tn, d, :], cb(hd, d)[0:tn], cols[0:tn, tt, d, 0, hd:hd + 1],
                                                 mk, ALU.add, ALU.min)
                ins.then_inc(S("ml_x_done"), 1)

            def mix_p(u):
                hd, tt = u // 3, u % 3
                tn = TILES[tt][1]
                dve.wait_ge(S("ml_scores"), u + 1)
                dve.wait_ge(S("ml_w_done"), u + 1)
                if u >= 1:
                    dve.wait_ge(S("ml_pn"), u)
                for d in range(2):
                    ins = V.scalar_tensor_tensor(ml_p[0:tn, d, :], pm[2][0:tn, 0:T], ML_SCALE, ml_x[0:tn, d, :],
                                                 ALU.mult, ALU.mult, accum_out=den[0:tn, d:d + 1])
                ins.then_inc(S("ml_used"), 1)
                dve.wait_ge(S("ml_used"), u + 1)
                link(V.scalar_tensor_tensor(den[0:tn, 2:4], den[0:tn, 0:2], -1.0, den[0:tn, 0:2], ALU.mult, ALU.max))
                link(V.tensor_tensor(den[0:tn, 2:4], den[0:tn, 2:4], cols[0:tn, tt, :, 1, hd], ALU.max))
                link(V.reciprocal(den[0:tn, 4:6], den[0:tn, 2:4]))
                if u >= 1:
                    dve.wait_ge(S("ml_ptdone"), u)
                link(V.tensor_scalar(ml_sum[0:tn, :], ml_p[0:tn, 0, :], den[0:tn, 4:5], None, ALU.mult))
                V.scalar_tensor_tensor(ml_sum[0:tn, :], ml_p[0:tn, 1, :], den[0:tn, 5:6], ml_sum[0:tn, :],
                                       ALU.mult, ALU.add).then_inc(S("ml_pn"), 1)

            def normed_q(u):
                dve.wait_ge(S("qk_rt"), u + 1)
                link(V.reciprocal(rt2[:, 0, :], rt2[:, 0, :]))
                V.scalar_tensor_tensor(q_rev[:, u, 0:META], proj[:, u, 0:META], vec[:, V_QG:V_QG + 1], rt2[:, 0, 0:META],
                                       ALU.mult, ALU.mult)
                o, q_, r_ = (v.rearrange("p (a b) -> p a b", b=P) for v in (q_rev[:, u, META:T], proj[:, u, META:T], rt2[:, 0, META:T]))
                V.scalar_tensor_tensor(o[:, :, ::-1], q_, vec[:, V_QG:V_QG + 1], r_, ALU.mult, ALU.mult)

            def normed_k(u):
                link(V.reciprocal(rt2[:, 1, :], rt2[:, 1, :]))
                V.scalar_tensor_tensor(proj[:, 8 + u, :], proj[:, 8 + u, :], vec[:, V_KG:V_KG + 1], rt2[:, 1, :],
                                       ALU.mult, ALU.mult).then_inc(S("qk_ready"), 1)

            def meta_queries():
                dve.wait_ge(S("nm_scores"), 1)
                s3 = pm[3][0:META, 0:P].rearrange("p (h q) -> p h q", q=META)
                link(V.tensor_scalar(na_m[:, :, :], s3, NA_SCALE, None, ALU.mult))
                mx = col[0:META, 8:16]
                link(V.tensor_reduce(mx, na_m[:, :, :], AX.X, ALU.max))
                V.tensor_tensor(na_m[:, :, :], na_m[:, :, :], bcast(mx, META, 2), ALU.subtract).then_inc(S("nm_max"), 1)
                dve.wait_ge(S("nm_exp"), 1)
                link(V.tensor_reduce(mx, na_m[:, :, :], AX.X, ALU.add))
                link(V.reciprocal(mx, mx))
                V.memset(pt[:, :, :, 0:META], 0.0)
                V.tensor_tensor(na_m[:, :, :], na_m[:, :, :], bcast(mx, META, 2), ALU.mult).then_inc(S("nm_norm"), 1)

            def soft_a(n):
                dve.wait_ge(S("na_scores"), n + 1)
                dve.wait_ge(S("bias_ready"), n + 1)
                if n >= 2:
                    dve.wait_ge(S("na_exp"), n - 1)
                V.scalar_tensor_tensor(na_s[:, n % 2, :], pm[n % 2][:, 0:T], NA_SCALE, bias[:, n % 4, :],
                                       ALU.mult, ALU.add).then_inc(S("na_biased"), 1)
                dve.wait_ge(S("na_biased"), n + 1)
                V.tensor_reduce(col[:, n % 2:n % 2 + 1], na_s[:, n % 2, :], AX.X, ALU.max, negate=True).then_inc(S("na_max"), 1)

            def soft_b(n):
                dve.wait_ge(S("na_exp"), n + 1)
                c = col[:, 4 + n % 2:5 + n % 2]
                link(V.reciprocal(c, col[:, 2 + n % 2:3 + n % 2]))
                V.tensor_scalar(na_p[:, n % 2, :], na_p[:, n % 2, :], c, None, ALU.mult).then_inc(S("na_norm"), 1)

            def low(hd):
                dve.wait_ge(S("x_hi"), 24 + hd + 1)
                V.tensor_tensor(act_lo[:, 8 + hd, :], ntmp[:, hd % 4, :], act_hi[:, 8 + hd, :].bitcast(F32),
                                ALU.subtract).then_inc(S("act_ready"), 1)

            def even():
                one = bass.AP(ones, 0, [[P, ML_HEADS], [0, T]])
                for t in range(EVEN_TICKS):
                    if t == 2:
                        dve.wait_ge(S("ml_ln"), 1)
                        link(V.scalar_tensor_tensor(row_l[:, :, :], row_f[:, :, :], 0.0, row_l[:, :, :], ALU.min, ALU.subtract))
                        V.tensor_tensor_scan(turn(row_b, 0), one, turn(row_l, 0), 0.0, ALU.mult, ALU.add)
                        link(V.tensor_tensor_scan(turn(row_b, 1), one, turn(row_l, 1), 0.0, ALU.mult, ALU.add))
                        V.tensor_tensor(row_c[:, :, :], row_c[:, :, :], row_b[:, :, :], ALU.subtract).then_inc(S("ml_c"), 1)
                        dve.wait_ge(S("ml_c"), 1)
                    if t == 3:
                        V.tensor_tensor_scan(turn(row_m, 0), one, turn(row_c, 0), 0.0, ALU.mult, ALU.max)
                        link(V.tensor_tensor_scan(turn(row_m, 1), one, turn(row_c, 1), 0.0, ALU.mult, ALU.max))
                        link(V.scalar_tensor_tensor(row_l[:, :, :], row_b[:, :, :], -1.0, row_m[:, :, :], ALU.mult, ALU.subtract))
                        V.tensor_scalar(row_m[:, :, :], row_m[:, :, :], -1.0, None, ALU.mult).then_inc(S("ml_nm"), 1)
                    if t == MIX0:
                        dve.wait_ge(S("ml_colc"), 1)
                        dve.wait_ge(S("mask_done"), 2)
                    u = at_tick(t, MIX0 + 1, UNIT, 3 * ML_HEADS)
                    if u is not None:
                        mix_p(u)
                    u = at_tick(t, MIX0, UNIT, 3 * ML_HEADS)
                    if u is not None:
                        mix_x(u)
                    hd = at_tick(t, MIX0 + 12, PER_HEAD, ML_HEADS)
                    if hd is not None:
                        dve.wait_ge(S("po_rt"), hd + 1)
                        link(V.reciprocal(e_rr[:, :], e_rr[:, :]))
                        for k in (2 * hd, 2 * hd + 1):
                            link(V.scalar_tensor_tensor(y_ml[:, k, :], y_ml[:, k, :], vec[:, V_ML + k:V_ML + k + 1], e_rr[:, :],
                                                        ALU.mult, ALU.mult))
                            dve.wait_ge(S("po_gate"), hd + 1)
                            V.tensor_tensor(y_ml[:, k, :], y_ml[:, k, :], proj[:, 40 + k, :], ALU.mult).then_inc(S("ml_made"), 1)
                    k = at_tick(t, QK0 + 2, 2, NA_HEADS)
                    if k is not None:
                        normed_q(k)
                    k = at_tick(t, QK0 + 3, 2, NA_HEADS)
                    if k is not None:
                        normed_k(k)
                    if t == META0 + 1:
                        meta_queries()
                    n = at_tick(t, NA0 + 1, 1, NA_UNITS)
                    if n is not None:
                        soft_a(n)
                        soft_b(n)
                    for k in Y_SPLIT.get(t, ()):
                        dve.wait_ge(S("x_hi"), KT + k + 1)
                        V.tensor_tensor(act_lo[:, k, :], y_ml[:, k, :], act_hi[:, k, :].bitcast(F32),
                                        ALU.subtract).then_inc(S("act_ready"), 1)
                    hd = at_tick(t, NA0 + 5, 2, NA_HEADS)
                    if hd is not None:
                        low(hd)
                    yield

            def decays():
                onesT = bass.AP(ones, 0, [[P, P], [0, T]])
                for q in range(8):
                    j, k = q // 4, 2 * (q % 4)
                    yield
                    yield
                    dve.wait_ge(S("gu_ln"), q + 1)
                    b2 = bc[:, j, k:k + 2, :]
                    link(V.scalar_tensor_tensor(b2, b2, 0.0, ge[:, :, :], ALU.min, ALU.subtract))
                    for m in range(2):
                        v = turn(bc[:, :, k + m, :], j)
                        ins = V.tensor_tensor_scan(v, onesT, v, 0.0, ALU.mult, ALU.add)
                    ins.then_inc(S("b_done"), 1)
                    yield

            def gates_side():
                dve.wait_ge(S("act_ready"), NORM_READY[2] + KT)
                V.memset(proj[:, 0:8, 0:Q0], 0.0)
                V.memset(gup[:, :, :], 0.0).then_inc(S("gup_in"), 1)
                yield from norm_side(2)

            def gla():
                dve.wait_ge(S("b_done"), 8)
                dve.wait_ge(S("lmask_done"), 14)

                def sub(v):
                    if v >= 2:
                        dve.wait_ge(S("gl_g"), level_units[v - 2] + 1)
                    for d in range(2):
                        o, b, r = level_sub(v, d, "q")
                        ins = V.tensor_tensor(o, b, r, ALU.subtract)
                    ins.then_inc(S("gl_dsub"), 1)

                def mul(v):
                    dve.wait_ge(S("gl_exp"), v + 1)
                    e, q_ = level_mul(v, "q")
                    V.tensor_tensor(e, e, q_, ALU.mult).then_inc(S("gl_dmul"), 1)

                def take(u):
                    hd, l = units[u]
                    b, s = pm[u % 2], hd % 2
                    dve.wait_ge(S("gl_g"), u + 1)
                    if u >= 1:
                        dve.wait_ge(S("gl_cp"), u)
                    diag = strided(at_t[:, s, 0, META:META + P], [[T + P, 2], [1, P]])
                    if l is None:
                        if hd >= 2:
                            dve.wait_ge(S("gl_pv"), 4 * (hd - 1))
                        V.scalar_tensor_tensor(at_m[:, s, 0:META], b[0:META, 2 * P:2 * P + META], 2.0, ident[0:META, 0:META],
                                               ALU.mult, ALU.mult)
                        ins = V.scalar_tensor_tensor(diag, strided(b, [[P, 2], [1, P]]), 2.0, bcast(ident[:, :], 2),
                                                     ALU.mult, ALU.mult)
                        ins.then_inc(S("gl_cp"), 1)
                        return
                    kind, H = LEVELS[l]
                    if kind == "in":
                        mk = lmask[:, l, :].bitcast(U16)
                        if H <= 8:
                            V.copy_predicated(at_m[:, s, 0:META], mk[0:META, 0:META], b[0:META, 2 * P:2 * P + META])
                        ins = V.copy_predicated(diag, bcast(mk, 2), strided(b, [[P, 2], [1, P]]))
                    elif H == META:
                        V.tensor_copy(at_m[:, s, META:META + P], b[0:META, 0:P])
                        ins = V.tensor_copy(at_t[:, s, 0, 0:META], b[:, P:P + META])
                    else:
                        V.tensor_copy(at_m[:, s, META + P:T], b[0:META, 0:P])
                        V.tensor_copy(at_t[:, s, 0, META + P:T], b[:, P:2 * P])
                        ins = V.tensor_copy(at_t[:, s, 1, 0:META + P], b[:, 2 * P:3 * P + META])
                    ins.then_inc(S("gl_cp"), 1)

                for t in range(GL_TICKS):
                    for v in ((0, 1) if t == 0 else (t + 1,)):
                        if v < len(level_units):
                            sub(v)
                    if t < len(level_units):
                        mul(t)
                    if t >= 1 and t - 1 < len(UNITS_AT):
                        for u in UNITS_AT[t - 1]:
                            take(u)
                    if t in MAKE:
                        make(MAKE[t])
                    for k in HIGH.get(t, ()):
                        low_gla(k)
                    yield

            def make(k):
                hd = k // 4
                rr, o = bc[:, 0, 2 * hd, Q0:T], o_tile(k)[:, Q0:T]
                if k % 4 == 0:
                    dve.wait_ge(S("po_rt"), 4 + hd + 1)
                    dve.wait_ge(S("po_gate"), 4 + hd + 1)
                    link(V.reciprocal(rr, rr))
                link(V.scalar_tensor_tensor(o, o, vec[:, V_GLA + k:V_GLA + k + 1], rr, ALU.mult, ALU.mult))
                V.tensor_tensor(o, o, proj[:, 32 + k, Q0:T], ALU.mult).then_inc(S("n_ready"), 1)

            def low_gla(k):
                dve.wait_ge(S("x_hi"), 64 + k + 1)
                V.tensor_tensor(act_lo[:, k, Q0:T], o_tile(k)[:, Q0:T], act_hi[:, k, Q0:T].bitcast(F32),
                                ALU.subtract).then_inc(S("act_ready"), 1)

            dve.wait_ge(S("par_evac"), 1)
            for k in range(KT):
                norm_low(0, k)
                if k % 4 == 3 and k < 12:
                    lo(gemms[0], 0, k // 4)
            mixers = even()
            gemm(G["ml_in"], first=norm_side(0), last_beside=mixers)
            gemm(G["na_in"], beside=mixers)
            gemm(G["ml_out"], beside=mixers)
            finish(mixers)
            gemm(G["na_out"], last_beside=norm_early(1))

            def ffn_stage(layer, n):
                norm(n)
                gemm(G[f"up{layer}0"], first=norm_side(n))
                gemm(G[f"down{layer}0"])
                gemm(G[f"up{layer}1"])
                gemm(G[f"down{layer}1"])
                gemm(G[f"up{layer}2"])

            ffn_stage(0, 1)
            gemm(G["down02"], last_beside=norm_early(2))
            norm(2)
            decay = decays()
            gemm(G["q_in"], first=gates_side(), beside=decay)
            gemm(G["k_in"], beside=decay)
            finish(decay)
            mixer = gla()
            gemm(G["v_in"], beside=mixer)
            gemm(G["r_in"], beside=mixer)
            gemm(G["gl_out0"], beside=mixer)
            finish(mixer)
            gemm(G["gl_out1"], last_beside=norm_early(3))
            ffn_stage(1, 3)
            gemm(G["down12"])

        @block.tensor
        def _(pe):
            mm = nc.tensor.matmul
            tr = nc.tensor.transpose

            def gemm(g, first=None, beside=None, last_beside=None):
                mid = g.get("mid")
                xh, xl = (g_hi, g_lo) if mid else (act_hi, act_lo)
                t0 = g["t0"]

                def body(i, side=None):
                    n = i + g["it0"]
                    for s in range(8):
                        grp, c = s // g["gs"], s % g["gs"]
                        kc, k0 = g["ks"][c], sum(g["ks"][:c])
                        if c == 0:
                            pe.wait_ge(S("bank_free"), i * g["ng"] + (g["gr0"] + grp + 1))
                        if grp == 0:
                            if mid:
                                pe.wait_ge(S("mid_split"), g["c0"] + (k0 + kc + 1) // 2)
                            else:
                                pe.wait_ge(S("act_ready"), g["ready"] + k0 + kc)
                        pe.wait_ge(S("split_done"), n * 8 + (s + 1))
                        for m in range(2):
                            o = ps[:, 2 * (grp % 2) + m, 0:T - t0]
                            for k in range(kc):
                                kk = g["x0"] + k0 + k
                                w0 = k * 256 + m * P
                                wh, wl = w_hi[:, s % 4, w0:w0 + P], w_lo[:, s % 4, w0:w0 + P]
                                end = c == g["gs"] - 1 and k == kc - 1
                                mm(o, wh, xh[:, kk, t0:T], start=(c == 0 and k == 0), stop=False)
                                mm(o, wh, xl[:, kk, t0:T], start=False, stop=False)
                                ins = mm(o, wl, xh[:, kk, t0:T], start=False, stop=end)
                        ins.then_inc(S("used"), 1)
                        if side:
                            advance(side)

                start = 0
                if first:
                    body(0, first)
                    finish(first)
                    start = 1
                last = g["iters"] - 1
                if beside:
                    for i in range(start, last):
                        body(i, beside)
                else:
                    with pe.Fori(start, last) as i:
                        body(i)
                body(last, beside or last_beside)

            def norm_side(n):
                for t in range(4):
                    yield
                pe.wait_ge(S("sq_added"), 3 * n + 3)
                for k in range(4):
                    ins = mm(pm[0][:, 0:T], ones[:, :], sq[:, k, :], start=(k == 0), stop=(k == 3))
                ins.then_inc(S("ss_ready"), 1)
                yield
                if n in (0, 2):
                    o, w = (0, GATES) if n == 0 else (GATES, LRS)
                    pe.wait_ge(S("tail_scaled"), n // 2 + 1)
                    for k in range(KT):
                        ins = mm(pm[1][0:w, 0:T], tail_w[:, k, o:o + w], h[:, k, :], start=(k == 0), stop=(k == KT - 1))
                    ins.then_inc(S("tail_done"), 1)
                    yield
                if n == 0:
                    pe.wait_ge(S("conv_in"), 16 * 8)
                    for j in range(8):
                        b = pm[2] if j < 5 else pm[3]
                        ins = tr(b[:, 88 * (j % 5):88 * (j % 5 + 1)], stage[0:88, j, :], ident[0:88, 0:88])
                    ins.then_inc(S("par_done"), 1)
                    yield

            def vt(n, src, b):
                tr(pm[b][0:META, 2 * P:3 * P], src[:, 0:META], ident[:, :])
                tr(pm[b][:, 0:P], src[:, META:META + P], ident[:, :])
                tr(pm[b][:, P:2 * P], src[:, META + P:T], ident[:, :]).then_inc(S("vt_done"), 1)

            def weigh(o, v0, ptt, ptm):
                mm(o, v_tok[0:META, 0, v0:v0 + P], ptm, start=True, stop=False)
                mm(o, v_tok[:, 1, v0:v0 + P], ptt[:, 0, :], start=False, stop=False)
                return mm(o, v_tok[:, 2, v0:v0 + P], ptt[:, 1, :], start=False, stop=True)

            def even():
                gr = G["na_in"]["gr0"]
                for t in range(EVEN_TICKS):
                    if t == 0:
                        pe.wait_ge(S("tail_evac"), 1)
                        for j in range(4):
                            ins = mm(pm[j][0:ML_HEADS, 0:T], ident[0:GATES, 4 * j:4 * j + 4], tail[0:GATES, :], start=True, stop=True)
                        ins.then_inc(S("ml_sel"), 1)
                    if t == 4:
                        pe.wait_ge(S("ml_nm"), 1)
                        pe.wait_ge(S("ml_en"), 1)
                        for tt, (t0, tn) in enumerate(TILES):
                            for d in range(2):
                                for q, row in enumerate((row_m, row_f)):
                                    o = ((tt * 2 + d) * 2 + q) * 4
                                    ins = mm(pm[0][0:tn, o:o + 4], row[:, d, t0:t0 + tn], ident[0:4, 0:4], start=True, stop=True)
                        ins.then_inc(S("ml_cols"), 1)
                    hd = at_tick(t, CB0, 1, ML_HEADS)
                    if hd is not None:
                        if hd == 0:
                            pe.wait_ge(S("sel_done"), 1)
                            pe.wait_ge(S("ml_c"), 1)
                            pe.wait_ge(S("ml_colc"), 1)
                        else:
                            pe.wait_ge(S("ml_cbk"), hd)
                        for d in range(2):
                            ins = mm(pm[d][:, 0:T], selrow[:, hd, :], row_c[:, d, :], start=True, stop=True)
                        ins.then_inc(S("ml_cb"), 1)
                    u = at_tick(t, MIX0, UNIT, 3 * ML_HEADS)
                    if u is not None:
                        hd, (t0, tn) = u // 3, TILES[u % 3]
                        if u == 0:
                            pe.wait_ge(S("bank_free"), 2 + gr)
                            pe.wait_ge(S("vt_copied"), 8)
                        else:
                            pe.wait_ge(S("ml_used"), u)
                        mm(pm[2][0:tn, 0:T], proj[:, 24 + hd, t0:t0 + tn], proj[:, 28 + hd, :], start=True, stop=True).then_inc(S("ml_scores"), 1)
                    hd = at_tick(t, MIX0 + 8, PER_HEAD, ML_HEADS)
                    if hd is not None:
                        pe.wait_ge(S("ml_ptcopied"), 3 * hd + 3)
                        if hd == 0:
                            pe.wait_ge(S("ml_cbk"), ML_HEADS)
                        else:
                            pe.wait_ge(S("po_rt"), hd)
                        for e in range(2):
                            ins = weigh(pm[e][:, 0:T], 1024 + hd * 256 + e * P, ml_ptt, ml_ptm[:, :])
                        ins.then_inc(S("ml_pv"), 1)
                    u = at_tick(t, MIX0 + 2, UNIT, 3 * ML_HEADS)
                    if u is not None:
                        tn = TILES[u % 3][1]
                        pe.wait_ge(S("ml_pn"), u + 1)
                        if u >= 1:
                            pe.wait_ge(S("ml_ptcopied"), u)
                        b = pm[3]
                        tr(b[0:META, 2 * P:2 * P + tn], ml_sum[0:tn, 0:META], ident[0:tn, 0:tn])
                        tr(b[:, 0:tn], ml_sum[0:tn, META:META + P], ident[0:tn, 0:tn])
                        tr(b[:, P:P + tn], ml_sum[0:tn, META + P:T], ident[0:tn, 0:tn]).then_inc(S("ml_ptdone"), 1)
                    hd = at_tick(t, MIX0 + 9, PER_HEAD, ML_HEADS)
                    if hd is not None:
                        pe.wait_ge(S("po_sq"), hd + 1)
                        for j in range(2):
                            ins = mm(pm[0][:, 0:T], ones[:, :], e_sq[:, j, :], start=(j == 0), stop=(j == 1))
                        ins.then_inc(S("po_ss"), 1)
                    k = at_tick(t, QK0 + 1, 2, NA_HEADS)
                    if k is not None:
                        pe.wait_ge(S("qk_sq"), k + 1)
                        if k:
                            pe.wait_ge(S("qk_rt"), k)
                        else:
                            pe.wait_ge(S("ml_ptcopied"), 3 * ML_HEADS)
                        for j in range(2):
                            ins = mm(pm[2 + j][:, 0:T], ones[:, :], sq2[:, j, :], start=True, stop=True)
                        ins.then_inc(S("qk_ss"), 1)
                    for n, b in EVEN_VT.get(t, ()):
                        if n < 8:
                            pe.wait_ge(S("bank_free"), 2 + 8)
                        else:
                            pe.wait_ge(S("bank_free"), 2 + gr + 8 + (n - 8) // 2 + 1)
                        if n < 2:
                            pe.wait_ge(S("ml_ln"), 1)
                        elif n < 8:
                            pe.wait_ge(S("vt_copied"), n - 1)
                        elif n < 10:
                            pe.wait_ge(S("po_rt"), ML_HEADS)
                        elif n < 12:
                            pe.wait_ge(S("vt_copied"), n - 1)
                        else:
                            pe.wait_ge(S("na_stored"), (t - NA0 - 4) // 2 + 1)
                        vt(n, proj[:, E_ML[n] if n < 8 else E_NA[n - 8], :], b)
                    if t == META0:
                        pe.wait_ge(S("qk_ready"), NA_HEADS)
                        for hd in range(NA_HEADS):
                            ins = mm(pm[3][0:META, META * hd:META * (hd + 1)], q_rev[:, hd, 0:META], proj[:, 8 + hd, 0:META], start=True, stop=True)
                        ins.then_inc(S("nm_scores"), 1)
                    if t == META0 + 1:
                        pe.wait_ge(S("nm_norm"), 1)
                        for hd in range(NA_HEADS):
                            ins = tr(pm[3][0:META, P + META * hd:P + META * (hd + 1)], na_m[:, hd, :], ident[0:META, 0:META])
                        ins.then_inc(S("nm_ptdone"), 1)
                    n = at_tick(t, NA0, 1, NA_UNITS)
                    if n is not None:
                        hd, qt = n // 2, n % 2
                        t0 = TILES[1 + qt][0]
                        if n < 2:
                            pe.wait_ge(S("vt_copied"), 12)
                        else:
                            pe.wait_ge(S("na_biased"), n - 1)
                        mm(pm[n % 2][:, 0:T], q_rev[:, hd, t0:t0 + P], proj[:, 8 + hd, :], start=True, stop=True).then_inc(S("na_scores"), 1)
                    n = at_tick(t, NA0 + 2, 1, NA_UNITS)
                    if n is not None:
                        pe.wait_ge(S("na_norm"), n + 1)
                        if n >= 1:
                            pe.wait_ge(S("na_ptcopied"), n)
                        b = pm[2]
                        tr(b[0:META, 2 * P:3 * P], na_p[:, n % 2, 0:META], ident[:, :])
                        tr(b[:, 0:P], na_p[:, n % 2, META:META + P], ident[:, :])
                        tr(b[:, P:2 * P], na_p[:, n % 2, META + P:T], ident[:, :]).then_inc(S("na_ptdone"), 1)
                    hd = at_tick(t, NA0 + 4, 2, NA_HEADS)
                    if hd is not None:
                        pe.wait_ge(S("na_ptcopied"), 2 * hd + 2)
                        if hd == 0:
                            pe.wait_ge(S("nm_ptcopied"), 1)
                        else:
                            pe.wait_ge(S("na_stored"), hd)
                        pe.wait_ge(S("vt_copied"), sum(len(v) for q, v in EVEN_VT.items() if q < t))
                        weigh(pm[3][:, 0:T], hd * P, pt[:, hd % 2], pt_m[:, hd % 2, :]).then_inc(S("na_pv"), 1)
                    yield

            def decays():
                pe.wait_ge(S("tail_evac"), 2)
                pe.wait_ge(S("gup_in"), 33)
                for q in range(8):
                    j, k = q // 4, 2 * (q % 4)
                    if q >= 2:
                        pe.wait_ge(S("gu_x"), q - 1)
                    for m in range(2):
                        ins = mm(pm[2 * (q % 2) + m][:, 0:T], gup[:, j, (k + m) * P:(k + m + 1) * P], tail[:, :], start=True, stop=True)
                    ins.then_inc(S("gu_mm"), 1)
                    yield
                    yield
                    yield

            def gram(o, l0, ln, r0, rn, L, R):
                for j in range(2):
                    ins = mm(o, L[:, j, l0:l0 + ln], R[:, j, r0:r0 + rn], start=(j == 0), stop=(j == 1))
                return ins

            def gla():
                pe.wait_ge(S("bank_free"), 2 + G["v_in"]["gr0"])
                pe.wait_ge(S("gu_x"), 8)
                for t in range(GL_TICKS):
                    for u in (UNITS_AT[t] if t < len(UNITS_AT) else ()):
                        unit(u)
                    if t in GL_VT or t in WEIGH or t in SQUARE:
                        pe.wait_ge(S("vt_copied"), 16 + before(t, GL_VT))
                        pe.wait_ge(S("gl_stored"), before(t, WEIGH))
                        pe.wait_ge(S("po_rt"), ML_HEADS + before(t, SQUARE))
                    for n in GL_VT.get(t, ()):
                        pe.wait_ge(S("bank_free"), 2 + G["v_in"]["gr0"] + n // 2 + 1)
                        vt(16 + n, ntmp[:, n % 4, :], 2 + n % 2)
                    if t in WEIGH:
                        n = WEIGH[t]
                        hd = n // 4
                        pe.wait_ge(S("gl_cp"), UH * (hd + 1))
                        weigh(pm[2 + n % 2][:, Q0:T], n * P, at_t[:, hd % 2, :, Q0:T], at_m[:, hd % 2, Q0:T]).then_inc(S("gl_pv"), 1)
                    if t in SQUARE:
                        squares(SQUARE[t])
                    yield

            def squares(hd):
                pe.wait_ge(S("po_sq"), 4 + hd + 1)
                for j in range(4):
                    ins = mm(pm[2 + hd % 2][:, Q0:T], ones[:, :], bc[:, j // 2, 2 * hd + j % 2, Q0:T], start=(j == 0), stop=(j == 3))
                ins.then_inc(S("po_ss"), 1)

            def unit(u):
                hd, l = units[u]
                b = pm[u % 2]
                if u >= 2:
                    pe.wait_ge(S("gl_cp"), u - 1)
                if l is None:
                    L, R = proj[:, 8 + 2 * hd:10 + 2 * hd, :], proj[:, 2 * hd:2 * hd + 2, :]
                    kind, H = "in", 1
                else:
                    v = u - hd - 1
                    pe.wait_ge(S("gl_dmul"), v + 1)
                    pe.wait_ge(S("gl_pmul"), v + 1)
                    L, R = gl_e[:, v % 2, 1], gl_e[:, v % 2, 0]
                    kind, H = LEVELS[l]
                if kind == "in":
                    if H <= 8:
                        gram(b[0:META, 2 * P:2 * P + META], 0, META, 0, META, L, R)
                    gram(b[:, 0:P], META, P, META, P, L, R)
                    ins = gram(b[:, P:2 * P], META + P, P, META + P, P, L, R)
                elif H == META:
                    gram(b[0:META, 0:P], 0, META, META, P, L, R)
                    ins = gram(b[:, P:P + META], META, P, 0, META, L, R)
                else:
                    gram(b[0:META, 0:P], 0, META, META + P, P, L, R)
                    gram(b[:, P:2 * P], META, P, META + P, P, L, R)
                    ins = gram(b[:, 2 * P:3 * P + META], META + P, P, 0, META + P, L, R)
                ins.then_inc(S("gl_g"), 1)

            pe.wait_ge(S("const_done"), 3)
            for k in range(KT):
                pe.wait_ge(S(f"tok_in{k // 4}"), 32)
                if k >= 4:
                    pe.wait_ge(S("h_built"), k // 2 - 1)
                for tt, (t0, tn) in enumerate(TILES):
                    ins = tr(ps[:, k % 4, t0:t0 + tn], tok[0:tn, tt, k * P:(k + 1) * P], ident[0:tn, 0:tn])
                ins.then_inc(S("xT_done"), 1)
                if k == 3:
                    pe.wait_ge(S("param_in"), 16 * 7)
                    tr(pm[0][:, 0:V_N], stage[0:V_N, 8, :], ident[0:V_N, 0:V_N]).then_inc(S("par_done"), 1)
            pe.wait_ge(S("h_built"), KT // 2)
            mixers = even()
            gemm(G["ml_in"], first=norm_side(0), last_beside=mixers)
            gemm(G["na_in"], beside=mixers)
            gemm(G["ml_out"], beside=mixers)
            finish(mixers)
            gemm(G["na_out"])

            def ffn_stage(layer, n):
                gemm(G[f"up{layer}0"], first=norm_side(n))
                gemm(G[f"down{layer}0"])
                gemm(G[f"up{layer}1"])
                gemm(G[f"down{layer}1"])
                gemm(G[f"up{layer}2"])

            ffn_stage(0, 1)
            gemm(G["down02"])
            decay = decays()
            gemm(G["q_in"], first=norm_side(2), beside=decay)
            gemm(G["k_in"], beside=decay)
            finish(decay)
            mixer = gla()
            gemm(G["v_in"], beside=mixer)
            gemm(G["r_in"], beside=mixer)
            gemm(G["gl_out0"], beside=mixer)
            finish(mixer)
            gemm(G["gl_out1"])
            ffn_stage(1, 3)

            def ending():
                for t in range(8 * 4 + 6):
                    for b in range(2):
                        q = at_tick(t, 8 + 1 + 2 * b, 8, 4)
                        if q is not None:
                            n, t0 = 2 * q + b, TILES[1 + b][0]
                            pe.wait_ge(S("bank_free"), 2 + G["down12"]["gr0"] + 2 * (q + 1))
                            if n >= 4:
                                pe.wait_ge(S("out_evac"), n - 3)
                            for j in range(4):
                                ins = tr(pm[n % 4][:, j * P:(j + 1) * P], h[:, 4 * q + j, t0:t0 + P], ident[:, :])
                            ins.then_inc(S("out_done"), 1)
                    yield

            end = ending()
            gemm(G["down12"], beside=end)
            finish(end)


_INS = ["x", "meta_tokens", "norm_mix", "norm_ffn", "ab_w_in", "ab_gate_bias", "ab_q_gain", "ab_k_gain",
        "ab_rel_bias", "ab_ml_gain", "ab_w_out", "c_w_in", "c_gate_up", "c_gate_bias", "c_head_gain",
        "c_w_out", "ffn_w_up", "ffn_conv_w", "ffn_conv_b", "ffn_w_down"]


def kernel(**inputs):
    import numpy as _np
    import concourse.bacc as _bacc
    from concourse import mybir as _mybir
    from concourse.bass_utils import run_bass_kernel_spmd as _run

    nc = _bacc.Bacc("TRN2", target_bir_lowering=False, num_devices=1)
    arrays, args = {}, []
    for name in _INS:
        v = _np.ascontiguousarray(inputs[name])
        arrays[f"in_{name}"] = v
        args.append(nc.dram_tensor(f"in_{name}", v.shape, _mybir.dt.from_np(v.dtype), kind="ExternalInput").ap())
    args.append(nc.dram_tensor("out_y", (1, SEQ, D), _mybir.dt.float32, kind="ExternalOutput").ap())
    build(nc, *args)
    r = _run(nc, [arrays], core_ids=[0])
    return r.results[0]["out_y"]
```
